# Optimizing a Trainium2 kernel written in Bass

```python
import jax, jax.numpy as jnp
from jax import lax
import numpy as np

D_MODEL = 1024
BATCH = 1
SEQ = 512
DEPTH = 2

HEAD_DIM = 64
PLE_DIM = 256
GRID_W = 64
ROPE_THETA = 10000.0
RMS_EPS = 1e-6
D_FF = 2816
A_HEADS = 12
A_KV_HEADS = 4
A_GROUP = A_HEADS // A_KV_HEADS
A_RADIUS = 128
B_PAIRS = ((128, 1), (512, 4), (2048, 16))
B_SLOTS = 4
B_HEADS = B_SLOTS * len(B_PAIRS)
C_HEADS = D_MODEL // HEAD_DIM
NA_KH = 8
NA_KW = 16

A_Q = A_HEADS * HEAD_DIM
A_KV = A_KV_HEADS * HEAD_DIM
B_W = B_HEADS * HEAD_DIM
AB_IN = A_Q + 2 * A_KV + 3 * B_W
AB_OUT = A_Q + B_SLOTS * HEAD_DIM
C_IN = 3 * C_HEADS * HEAD_DIM
C_OUT = C_HEADS * HEAD_DIM
N_EVEN = (DEPTH + 1) // 2
N_ODD = DEPTH // 2
NEG_INF = -1e30


def rmsnorm(x, g):
    xf = x.astype(jnp.float32)
    y = xf * lax.rsqrt(jnp.mean(xf * xf, axis=-1, keepdims=True) + RMS_EPS)
    return (y * g.astype(jnp.float32)).astype(x.dtype)

def swiglu(x, w_gate, w_up, w_down):
    return (jax.nn.silu(x @ w_gate) * (x @ w_up)) @ w_down

def rope(x, pos):
    half = x.shape[-1] // 2
    inv = ROPE_THETA ** (-jnp.arange(half, dtype=jnp.float32) / half)
    ang = pos.astype(jnp.float32)[:, None] * inv[None, :]
    cos = jnp.cos(ang)[None, :, None, :]
    sin = jnp.sin(ang)[None, :, None, :]
    xf = x.astype(jnp.float32)
    x1, x2 = xf[..., :half], xf[..., half:]
    return jnp.concatenate([x1 * cos - x2 * sin, x2 * cos + x1 * sin], axis=-1).astype(x.dtype)

def banded_attention(q, k, v, radius, sink=None):
    n, L, hk, g, dh = q.shape
    bs = radius
    nb = -(-L // bs)
    lp = nb * bs
    q = jnp.pad(q, ((0, 0), (0, lp - L), (0, 0), (0, 0), (0, 0)))
    kv_pad = ((0, 0), (bs, lp - L + bs), (0, 0), (0, 0))
    k = jnp.pad(k, kv_pad).reshape(n, nb + 2, bs, hk, dh)
    v = jnp.pad(v, kv_pad).reshape(n, nb + 2, bs, hk, dh)
    kw = jnp.concatenate([k[:, :-2], k[:, 1:-1], k[:, 2:]], axis=2)
    vw = jnp.concatenate([v[:, :-2], v[:, 1:-1], v[:, 2:]], axis=2)
    qb = q.reshape(n, nb, bs, hk, g, dh)
    qpos = jnp.arange(lp).reshape(nb, bs)
    kpos = (jnp.arange(nb)[:, None] - 1) * bs + jnp.arange(3 * bs)[None, :]
    mask = (jnp.abs(qpos[:, :, None] - kpos[:, None, :]) <= radius) & ((kpos >= 0) & (kpos < L))[:, None, :]
    s = jnp.einsum('nbqhgd,nbkhd->nbhgqk', qb, kw).astype(jnp.float32) * (dh ** -0.5)
    s = jnp.where(mask[None, :, None, None], s, NEG_INF)
    m = jnp.max(s, axis=-1)
    if sink is not None:
        m = jnp.maximum(m, sink[:, :, None])
    e = jnp.exp(s - m[..., None])
    den = jnp.sum(e, axis=-1)
    if sink is not None:
        den = den + jnp.exp(sink[:, :, None] - m)
    pr = (e / den[..., None]).astype(v.dtype)
    o = jnp.einsum('nbhgqk,nbkhd->nbqhgd', pr, vw).reshape(n, lp, hk, g, dh)[:, :L]
    lse = (m + jnp.log(den)).transpose(0, 1, 4, 2, 3).reshape(n, lp, hk, g)[:, :L]
    return o, lse

def dilated_attention(q, k, v):
    bsz, s, _, dh = q.shape
    outs, lses = [], []
    for gi, (window, dil) in enumerate(B_PAIRS):
        lo = gi * B_SLOTS
        sub = s // dil

        def to_res(t):
            t = t[:, :, lo:lo + B_SLOTS]
            return t.reshape(bsz, sub, dil, B_SLOTS, dh).transpose(0, 2, 1, 3, 4).reshape(bsz * dil, sub, B_SLOTS, dh)

        o, lse = banded_attention(to_res(q)[:, :, :, None], to_res(k), to_res(v), window // (2 * dil))
        outs.append(o[:, :, :, 0].reshape(bsz, dil, sub, B_SLOTS, dh).transpose(0, 2, 1, 3, 4).reshape(bsz, s, B_SLOTS, dh))
        lses.append(lse[..., 0].reshape(bsz, dil, sub, B_SLOTS).transpose(0, 2, 1, 3).reshape(bsz, s, B_SLOTS))
    wts = jax.nn.softmax(jnp.stack(lses, axis=0), axis=0)
    out = jnp.einsum('gbsh,gbshd->bshd', wts, jnp.stack(outs, axis=0).astype(jnp.float32))
    return out.astype(q.dtype)

def neighbourhood_attention(q, k, v, rpb):
    bsz, s, nh, dh = q.shape
    rows = s // GRID_W
    kh = min(NA_KH, rows)
    kw = NA_KW
    qg = q.reshape(bsz, rows, GRID_W, nh, dh)
    kg = k.reshape(bsz, rows, GRID_W, nh, dh)
    vg = v.reshape(bsz, rows, GRID_W, nh, dh)
    cols = jnp.arange(GRID_W)
    col_start = jnp.clip(cols - kw // 2, 0, GRID_W - kw)
    col_idx = col_start[:, None] + jnp.arange(kw)[None, :]
    dc = col_idx - cols[:, None] + (NA_KW - 1)
    scale = dh ** -0.5

    def row_fn(i):
        rs = jnp.clip(i - kh // 2, 0, rows - kh)
        k_win = lax.dynamic_slice_in_dim(kg, rs, kh, axis=1)[:, :, col_idx]
        v_win = lax.dynamic_slice_in_dim(vg, rs, kh, axis=1)[:, :, col_idx]
        q_row = lax.dynamic_index_in_dim(qg, i, axis=1, keepdims=False)
        sc = jnp.einsum('bjhd,bajkhd->bhjak', q_row, k_win).astype(jnp.float32) * scale
        dr = rs + jnp.arange(kh) - i + (NA_KH - 1)
        bias = rpb[:, dr][:, :, dc].transpose(0, 2, 1, 3).astype(jnp.float32)
        sc = (sc + bias[None]).reshape(bsz, nh, GRID_W, kh * kw)
        pr = jax.nn.softmax(sc, axis=-1).reshape(bsz, nh, GRID_W, kh, kw).astype(v.dtype)
        return jnp.einsum('bhjak,bajkhd->bjhd', pr, v_win)

    o = lax.map(row_fn, jnp.arange(rows))
    return o.transpose(1, 0, 2, 3, 4).reshape(bsz, s, nh, dh)

def ab_mixer(xn, w_in, sink, w_out, pos):
    bsz, s, _ = xn.shape
    splits = [A_Q, A_Q + A_KV, A_Q + 2 * A_KV, A_Q + 2 * A_KV + B_W, A_Q + 2 * A_KV + 2 * B_W]
    qa, ka, va, qb, kb, vb = jnp.split(xn @ w_in, splits, axis=-1)
    qa = rope(qa.reshape(bsz, s, A_HEADS, HEAD_DIM), pos).reshape(bsz, s, A_KV_HEADS, A_GROUP, HEAD_DIM)
    ka = rope(ka.reshape(bsz, s, A_KV_HEADS, HEAD_DIM), pos)
    va = va.reshape(bsz, s, A_KV_HEADS, HEAD_DIM)
    oa, _ = banded_attention(qa, ka, va, A_RADIUS, sink.astype(jnp.float32).reshape(A_KV_HEADS, A_GROUP))
    shp = (bsz, s, B_HEADS, HEAD_DIM)
    ob = dilated_attention(rope(qb.reshape(shp), pos), rope(kb.reshape(shp), pos), vb.reshape(shp))
    mixed = jnp.concatenate([oa.reshape(bsz, s, A_Q).astype(xn.dtype),
                             ob.reshape(bsz, s, B_SLOTS * HEAD_DIM).astype(xn.dtype)], axis=-1)
    return mixed @ w_out

def c_mixer(xn, w_in, rpb, w_out):
    bsz, s, _ = xn.shape
    q, k, v = jnp.split(xn @ w_in, 3, axis=-1)
    shp = (bsz, s, C_HEADS, HEAD_DIM)
    o = neighbourhood_attention(q.reshape(shp), k.reshape(shp), v.reshape(shp), rpb)
    return o.reshape(bsz, s, C_OUT) @ w_out

def first_inputs(seed: int = 0) -> dict:
    key = jax.random.key(seed)
    ks = jax.random.split(key, 21)
    d = D_MODEL

    def nrm(k, shape, scale):
        return scale * jax.random.normal(k, shape, jnp.float32)

    def gain(k, shape):
        return 1.0 + 0.05 * jax.random.normal(k, shape, jnp.float32)

    return {
        'x': nrm(ks[0], (BATCH, SEQ, d), 1.0),
        'p': nrm(ks[1], (DEPTH, BATCH, SEQ, PLE_DIM), 1.0),
        'norm_ffn1': gain(ks[2], (DEPTH, d)),
        'ffn1_w_gate': nrm(ks[3], (DEPTH, d, D_FF), d ** -0.5),
        'ffn1_w_up': nrm(ks[4], (DEPTH, d, D_FF), d ** -0.5),
        'ffn1_w_down': nrm(ks[5], (DEPTH, D_FF, d), D_FF ** -0.5),
        'norm_mix': gain(ks[6], (DEPTH, d)),
        'w_in_ab': nrm(ks[7], (N_EVEN, d, AB_IN), d ** -0.5),
        'sink_a': nrm(ks[8], (N_EVEN, A_HEADS), 0.5),
        'w_out_ab': nrm(ks[9], (N_EVEN, AB_OUT, d), AB_OUT ** -0.5),
        'w_in_c': nrm(ks[10], (N_ODD, d, C_IN), d ** -0.5),
        'rpb_c': nrm(ks[11], (N_ODD, C_HEADS, 2 * NA_KH - 1, 2 * NA_KW - 1), 0.5),
        'w_out_c': nrm(ks[12], (N_ODD, C_OUT, d), C_OUT ** -0.5),
        'norm_ffn2': gain(ks[13], (DEPTH, d)),
        'ffn2_w_gate': nrm(ks[14], (DEPTH, d, D_FF), d ** -0.5),
        'ffn2_w_up': nrm(ks[15], (DEPTH, d, D_FF), d ** -0.5),
        'ffn2_w_down': nrm(ks[16], (DEPTH, D_FF, d), D_FF ** -0.5),
        'norm_ple': gain(ks[17], (DEPTH, d)),
        'w_ple_gate': nrm(ks[18], (DEPTH, d, d), d ** -0.5),
        'w_ple_proj': nrm(ks[19], (DEPTH, PLE_DIM, d), PLE_DIM ** -0.5),
        'norm_final': gain(ks[20], (d,)),
    }

def first_block(x, p, norm_ffn1, ffn1_w_gate, ffn1_w_up, ffn1_w_down, norm_mix, w_in_ab, sink_a,
              w_out_ab, w_in_c, rpb_c, w_out_c, norm_ffn2, ffn2_w_gate, ffn2_w_up, ffn2_w_down,
              norm_ple, w_ple_gate, w_ple_proj, norm_final):
    s = x.shape[1]
    pos = jnp.arange(s, dtype=jnp.int32)
    h = x
    for i in range(DEPTH):
        h = h + 0.5 * swiglu(rmsnorm(h, norm_ffn1[i]), ffn1_w_gate[i], ffn1_w_up[i], ffn1_w_down[i])
        hn = rmsnorm(h, norm_mix[i])
        j = i // 2
        if i % 2 == 0:
            h = h + ab_mixer(hn, w_in_ab[j], sink_a[j], w_out_ab[j], pos)
        else:
            h = h + c_mixer(hn, w_in_c[j], rpb_c[j], w_out_c[j])
        h = h + 0.5 * swiglu(rmsnorm(h, norm_ffn2[i]), ffn2_w_gate[i], ffn2_w_up[i], ffn2_w_down[i])
        gate = jax.nn.sigmoid(rmsnorm(h, norm_ple[i]) @ w_ple_gate[i])
        h = h + gate * (p[i] @ w_ple_proj[i])
    return rmsnorm(h, norm_final)


DEPTH_2 = 1

EPS = 1e-6
D_MIX = D_MODEL
HG_HEADS = 4
HG_DK = 128
HG_DV = 128
HG_WIDTH = HG_HEADS * HG_DV
HG_CHUNK = 64
NSA_HEADS = 8
NSA_KV_GROUPS = 2
NSA_HD = 64
NSA_WIDTH = NSA_HEADS * NSA_HD
NSA_KV = NSA_KV_GROUPS * NSA_HD
CMP_BLOCK = 32
CMP_STRIDE = 16
CMP_HIDDEN = 256
SEL_BLOCK = 64
N_SEL = 16
WINDOW = 512
Q_BLOCK = 128
N_EXPERTS = 64
TOP_K = 8
N_GROUPS = 8
TOPK_GROUPS = 4
EXPERT_HIDDEN = 256
SHARED_HIDDEN = 256
ROUTED_SCALE = 2.5
EXPERT_BLOCK = 128
IN_SPLITS = (HG_WIDTH,) * 4 + (NSA_WIDTH,) + (NSA_KV,) * 6 + (3 * NSA_HEADS,)
IN_COLS = 4 * HG_WIDTH + NSA_WIDTH + 6 * NSA_KV + 3 * NSA_HEADS


def rmsnorm_2(x, g):
    xf = x.astype(jnp.float32)
    y = xf * lax.rsqrt(jnp.mean(xf * xf, axis=-1, keepdims=True) + EPS)
    return (y * g.astype(jnp.float32)).astype(x.dtype)

def rope_2(t, pos):
    half = t.shape[-1] // 2
    inv = ROPE_THETA ** (-jnp.arange(half, dtype=jnp.float32) / half)
    ang = pos.astype(jnp.float32)[:, None] * inv[None, :]
    cos, sin = jnp.cos(ang), jnp.sin(ang)
    t1 = t[..., :half].astype(jnp.float32)
    t2 = t[..., half:].astype(jnp.float32)
    return jnp.concatenate([t1 * cos - t2 * sin, t2 * cos + t1 * sin], axis=-1).astype(t.dtype)

def swiglu_2(t, w_gu, w_dn):
    g, u = jnp.split(t @ w_gu, 2, axis=-1)
    return (jax.nn.silu(g) * u) @ w_dn

def hgrn2_mixer(q, f_logit, i, gate, lb, norm_g):
    B, S, _ = q.shape
    f32 = jnp.float32
    f = lb + (1.0 - lb) * jax.nn.sigmoid(f_logit.astype(f32))
    log_f = jnp.log(f)
    k = 1.0 - f
    n_ch = S // HG_CHUNK

    def to_chunks(t, d):
        return t.reshape(B, n_ch, HG_CHUNK, HG_HEADS, d).transpose(1, 0, 3, 2, 4)

    qc = to_chunks(q.astype(f32) * HG_DK ** -0.5, HG_DK)
    kc = to_chunks(k, HG_DK)
    vc = to_chunks(i.astype(f32), HG_DV)
    bc = jnp.cumsum(to_chunks(log_f, HG_DK), axis=3)
    causal = jnp.tril(jnp.ones((HG_CHUNK, HG_CHUNK), bool))

    def step(state, inp):
        q_, k_, v_, b_ = inp
        diff = jnp.where(causal[:, :, None], b_[:, :, :, None, :] - b_[:, :, None, :, :], -jnp.inf)
        a = jnp.einsum('bhtd,bhtsd,bhsd->bhts', q_, jnp.exp(diff), k_)
        o = a @ v_ + jnp.einsum('bhtd,bhde->bhte', q_ * jnp.exp(b_), state)
        b_last = b_[:, :, -1]
        state = jnp.exp(b_last)[..., None] * state + jnp.einsum(
            'bhsd,bhse->bhde', k_ * jnp.exp(b_last[:, :, None, :] - b_), v_)
        return state, o

    s0 = jnp.zeros((B, HG_HEADS, HG_DK, HG_DV), f32)
    _, o = lax.scan(step, s0, (qc, kc, vc, bc))
    o = o.transpose(1, 0, 3, 2, 4).reshape(B, S, HG_HEADS, HG_DV)
    o = o * lax.rsqrt(jnp.mean(o * o, axis=-1, keepdims=True) + EPS) * norm_g.astype(f32).reshape(HG_HEADS, HG_DV)
    o = o.reshape(B, S, HG_WIDTH) * jax.nn.silu(gate.astype(f32))
    return o.astype(q.dtype)

def nsa_mixer(q, kc, vc, ks, vs, kw, vw, gate_logit,
              pos_k, w1_k, b1_k, w2_k, pos_v, w1_v, b1_v, w2_v):
    B, S, _ = q.shape
    G, HG, HD = NSA_KV_GROUPS, NSA_HEADS // NSA_KV_GROUPS, NSA_HD
    f32 = jnp.float32
    pos = jnp.arange(S)
    scale = HD ** -0.5
    qh = q.reshape(B, S, G, HG, HD).transpose(0, 2, 3, 1, 4)
    q_rot = rope_2(qh, pos)

    def kv_heads(t):
        return t.reshape(B, S, G, HD).transpose(0, 2, 1, 3)

    n_cmp = (S - CMP_BLOCK) // CMP_STRIDE + 1
    tok_idx = jnp.arange(n_cmp)[:, None] * CMP_STRIDE + jnp.arange(CMP_BLOCK)[None, :]

    def compress(t, pe, w1, b1, w2):
        blocks = kv_heads(t)[:, :, tok_idx] + pe
        hdn = jax.nn.gelu(blocks.reshape(B, G, n_cmp, CMP_BLOCK * HD) @ w1 + b1)
        return hdn @ w2

    k_cmp = compress(kc, pos_k, w1_k, b1_k, w2_k)
    v_cmp = compress(vc, pos_v, w1_v, b1_v, w2_v)
    s_cmp = jnp.einsum('bghsd,bgcd->bghsc', qh, k_cmp).astype(f32) * scale
    c_start = jnp.arange(n_cmp) * CMP_STRIDE
    cmp_mask = (c_start + CMP_BLOCK - 1)[None, :] <= pos[:, None]
    p_cmp = jax.nn.softmax(jnp.where(cmp_mask, s_cmp, -1e30), axis=-1) * cmp_mask
    o_cmp = jnp.einsum('bghsc,bgcd->bghsd', p_cmp, v_cmp.astype(f32))

    n_sb = S // SEL_BLOCK
    n_sel = min(N_SEL, n_sb)
    s_start = jnp.arange(n_sb) * SEL_BLOCK
    overlap = jnp.clip(jnp.minimum(c_start[:, None] + CMP_BLOCK, s_start[None, :] + SEL_BLOCK)
                       - jnp.maximum(c_start[:, None], s_start[None, :]), 0, None).astype(f32) / CMP_BLOCK
    p_slc = jnp.einsum('bghsc,cj->bgsj', p_cmp, overlap)
    cur = pos // SEL_BLOCK
    blk = jnp.arange(n_sb)
    available = blk[None, :] <= cur[:, None]
    forced = (blk[None, :] == 0) | (blk[None, :] == cur[:, None]) | (blk[None, :] == cur[:, None] - 1)
    sel_score = jnp.where(forced, 1e30, jnp.where(available, p_slc, -1e30))
    top_val, top_idx = lax.top_k(sel_score, n_sel)
    top_valid = top_val > -1e29

    n_qb = S // Q_BLOCK
    k_blocks = rope_2(kv_heads(ks), pos).reshape(B, G, n_sb, SEL_BLOCK * HD)
    v_blocks = kv_heads(vs).reshape(B, G, n_sb, SEL_BLOCK * HD)
    bi = jnp.arange(B)[:, None, None]
    gi = jnp.arange(G)[None, :, None]

    def by_qblock(t, axis):
        shape = t.shape[:axis] + (n_qb, Q_BLOCK) + t.shape[axis + 1:]
        return jnp.moveaxis(t.reshape(shape), axis, 0)

    def slc_block(args):
        qb, idx, valid, qpos = args
        flat = idx.reshape(B, G, Q_BLOCK * n_sel)
        kg = k_blocks[bi, gi, flat].reshape(B, G, Q_BLOCK, n_sel, SEL_BLOCK, HD)
        vg = v_blocks[bi, gi, flat].reshape(B, G, Q_BLOCK, n_sel, SEL_BLOCK, HD)
        s = jnp.einsum('bghqd,bgqnld->bghqnl', qb, kg).astype(f32) * scale
        kpos = idx[..., None] * SEL_BLOCK + jnp.arange(SEL_BLOCK)
        ok = valid[..., None] & (kpos <= qpos[:, None, None])
        s = jnp.where(ok[:, :, None], s, -1e30).reshape(B, G, HG, Q_BLOCK, n_sel * SEL_BLOCK)
        p = jax.nn.softmax(s, axis=-1).reshape(B, G, HG, Q_BLOCK, n_sel, SEL_BLOCK)
        return jnp.einsum('bghqnl,bgqnld->bghqd', p, vg.astype(f32))

    o_slc = lax.map(slc_block, (by_qblock(q_rot, 3), by_qblock(top_idx, 2),
                                by_qblock(top_valid, 2), pos.reshape(n_qb, Q_BLOCK)))
    o_slc = jnp.moveaxis(o_slc, 0, 3).reshape(B, G, HG, S, HD)

    n_back = WINDOW // Q_BLOCK

    def banded(t):
        tp = jnp.pad(t, ((0, 0), (0, 0), (WINDOW, 0), (0, 0))).reshape(B, G, n_qb + n_back, Q_BLOCK, HD)
        return jnp.concatenate([tp[:, :, o:o + n_qb] for o in range(n_back + 1)], axis=3)

    kwb = banded(rope_2(kv_heads(kw), pos))
    vwb = banded(kv_heads(vw))
    qw = q_rot.reshape(B, G, HG, n_qb, Q_BLOCK, HD)
    s_w = jnp.einsum('bghnqd,bgnkd->bghnqk', qw, kwb).astype(f32) * scale
    qpos = pos.reshape(n_qb, Q_BLOCK)
    kpos = (jnp.arange(n_qb)[:, None] - n_back) * Q_BLOCK + jnp.arange((n_back + 1) * Q_BLOCK)[None, :]
    d = qpos[:, :, None] - kpos[:, None, :]
    ok_w = (d >= 0) & (d < WINDOW) & (kpos[:, None, :] >= 0)
    p_w = jax.nn.softmax(jnp.where(ok_w, s_w, -1e30), axis=-1)
    o_win = jnp.einsum('bghnqk,bgnkd->bghnqd', p_w, vwb.astype(f32)).reshape(B, G, HG, S, HD)

    gates = jax.nn.sigmoid(gate_logit.astype(f32)).reshape(B, S, G, HG, 3).transpose(0, 2, 3, 1, 4)
    o = gates[..., 0:1] * o_cmp + gates[..., 1:2] * o_slc + gates[..., 2:3] * o_win
    return o.transpose(0, 3, 1, 2, 4).reshape(B, S, NSA_WIDTH).astype(q.dtype)

def routed_experts(t, top_i, top_w, w_gu, w_dn):
    T, D = t.shape
    A = T * TOP_K
    e_flat = top_i.reshape(A).astype(jnp.int32)
    w_flat = top_w.reshape(A).astype(jnp.float32)
    order = jnp.argsort(e_flat)
    e_sorted = e_flat[order]
    tok_sorted = (order // TOP_K).astype(jnp.int32)
    counts = jnp.bincount(e_flat, length=N_EXPERTS)
    start = jnp.cumsum(counts) - counts
    padded = (counts + EXPERT_BLOCK - 1) // EXPERT_BLOCK * EXPERT_BLOCK
    pad_end = jnp.cumsum(padded)
    pad_start = pad_end - padded
    dest = pad_start[e_sorted] + jnp.arange(A) - start[e_sorted]
    n_blk = -(-A // EXPERT_BLOCK) + N_EXPERTS
    P = n_blk * EXPERT_BLOCK
    rows = jnp.full((P,), T, jnp.int32).at[dest].set(tok_sorted)
    wts = jnp.zeros((P,), jnp.float32).at[dest].set(w_flat[order])
    blk_expert = jnp.minimum(jnp.searchsorted(pad_end, jnp.arange(n_blk) * EXPERT_BLOCK, side='right'),
                             N_EXPERTS - 1)
    t_pad = jnp.concatenate([t, jnp.zeros((1, D), t.dtype)], axis=0)

    def one_block(args):
        rb, e = args
        return swiglu_2(t_pad[rb], w_gu[e], w_dn[e]).astype(jnp.float32)

    ys = lax.map(one_block, (rows.reshape(n_blk, EXPERT_BLOCK), blk_expert)).reshape(P, D)
    out = jnp.zeros((T + 1, D), jnp.float32).at[rows].add(ys * wts[:, None])
    return out[:T]

def moe_ffn(h, router_w, router_bias, w_gu, w_dn, w_sh_gu, w_sh_dn):
    B, S, D = h.shape
    t = h.reshape(B * S, D)
    scores = jax.nn.sigmoid((t @ router_w).astype(jnp.float32))
    choice = scores + router_bias.astype(jnp.float32)
    grp = choice.reshape(B * S, N_GROUPS, N_EXPERTS // N_GROUPS)
    grp_score = lax.top_k(grp, 2)[0].sum(-1)
    top_g = lax.top_k(grp_score, TOPK_GROUPS)[1]
    gmask = jnp.any(top_g[..., None] == jnp.arange(N_GROUPS), axis=-2)
    emask = jnp.repeat(gmask, N_EXPERTS // N_GROUPS, axis=-1)
    top_i = lax.top_k(jnp.where(emask, choice, -jnp.inf), TOP_K)[1]
    top_w = jnp.take_along_axis(scores, top_i, axis=-1)
    top_w = top_w / jnp.sum(top_w, axis=-1, keepdims=True) * ROUTED_SCALE
    routed = routed_experts(t, top_i, top_w, w_gu, w_dn)
    shared = swiglu_2(t, w_sh_gu, w_sh_dn).astype(jnp.float32)
    return (routed + shared).reshape(B, S, D).astype(h.dtype)

def second_inputs(seed: int = 0) -> dict:
    key = jax.random.key(seed)
    ks = jax.random.split(key, 26)
    L = DEPTH_2

    def nrm(k, shape, s):
        return jax.random.normal(k, shape, jnp.float32) * s

    return {
        "x": nrm(ks[0], (BATCH, SEQ, D_MODEL), 1.0),
        "c": nrm(ks[1], (BATCH, D_MODEL), 1.0),
        "w_ada": nrm(ks[2], (L, D_MODEL, 6 * D_MODEL), 0.5 * D_MODEL ** -0.5),
        "b_ada": nrm(ks[3], (L, 6 * D_MODEL), 0.02),
        "norm1_g": 1.0 + nrm(ks[4], (L, D_MODEL), 0.02),
        "w_in": nrm(ks[5], (L, D_MODEL, IN_COLS), D_MODEL ** -0.5),
        "hg_lb_logits": nrm(ks[6], (L + 1, HG_WIDTH), 0.5),
        "hg_norm_g": 1.0 + nrm(ks[7], (L, HG_WIDTH), 0.02),
        "cmp_pos_k": nrm(ks[8], (L, CMP_BLOCK, NSA_HD), 0.1),
        "cmp_w1_k": nrm(ks[9], (L, CMP_BLOCK * NSA_HD, CMP_HIDDEN), (CMP_BLOCK * NSA_HD) ** -0.5),
        "cmp_b1_k": nrm(ks[10], (L, CMP_HIDDEN), 0.02),
        "cmp_w2_k": nrm(ks[11], (L, CMP_HIDDEN, NSA_HD), CMP_HIDDEN ** -0.5),
        "cmp_pos_v": nrm(ks[12], (L, CMP_BLOCK, NSA_HD), 0.1),
        "cmp_w1_v": nrm(ks[13], (L, CMP_BLOCK * NSA_HD, CMP_HIDDEN), (CMP_BLOCK * NSA_HD) ** -0.5),
        "cmp_b1_v": nrm(ks[14], (L, CMP_HIDDEN), 0.02),
        "cmp_w2_v": nrm(ks[15], (L, CMP_HIDDEN, NSA_HD), CMP_HIDDEN ** -0.5),
        "w_out": nrm(ks[16], (L, D_MIX, D_MODEL), D_MIX ** -0.5),
        "norm2_g": 1.0 + nrm(ks[17], (L, D_MODEL), 0.02),
        "router_w": nrm(ks[18], (L, D_MODEL, N_EXPERTS), D_MODEL ** -0.5),
        "router_bias": nrm(ks[19], (L, N_EXPERTS), 0.01),
        "w_exp_gu": nrm(ks[20], (L, N_EXPERTS, D_MODEL, 2 * EXPERT_HIDDEN), D_MODEL ** -0.5),
        "w_exp_dn": nrm(ks[21], (L, N_EXPERTS, EXPERT_HIDDEN, D_MODEL), EXPERT_HIDDEN ** -0.5),
        "w_sh_gu": nrm(ks[22], (L, D_MODEL, 2 * SHARED_HIDDEN), D_MODEL ** -0.5),
        "w_sh_dn": nrm(ks[23], (L, SHARED_HIDDEN, D_MODEL), SHARED_HIDDEN ** -0.5),
        "final_g": 1.0 + nrm(ks[24], (D_MODEL,), 0.02),
    }

def second_block(x, c, w_ada, b_ada, norm1_g, w_in, hg_lb_logits, hg_norm_g,
              cmp_pos_k, cmp_w1_k, cmp_b1_k, cmp_w2_k, cmp_pos_v, cmp_w1_v, cmp_b1_v, cmp_w2_v,
              w_out, norm2_g, router_w, router_bias, w_exp_gu, w_exp_dn, w_sh_gu, w_sh_dn, final_g):
    offsets = np.cumsum(IN_SPLITS)[:-1].tolist()
    lb_all = jnp.cumsum(jax.nn.softmax(hg_lb_logits.astype(jnp.float32), axis=0), axis=0)
    c_act = jax.nn.silu(c)
    for l in range(DEPTH_2):
        mod = (c_act @ w_ada[l] + b_ada[l])[:, None, :]
        sh1, sc1, g1, sh2, sc2, g2 = jnp.split(mod, 6, axis=-1)
        h = rmsnorm_2(x, norm1_g[l]) * (1.0 + sc1) + sh1
        hq, hf, hi, hgt, nq, kc, vc, ksl, vsl, kwn, vwn, ngate = jnp.split(h @ w_in[l], offsets, axis=-1)
        o_hg = hgrn2_mixer(hq, hf, hi, hgt, lb_all[l], hg_norm_g[l])
        o_nsa = nsa_mixer(nq, kc, vc, ksl, vsl, kwn, vwn, ngate,
                          cmp_pos_k[l], cmp_w1_k[l], cmp_b1_k[l], cmp_w2_k[l],
                          cmp_pos_v[l], cmp_w1_v[l], cmp_b1_v[l], cmp_w2_v[l])
        x = x + g1 * (jnp.concatenate([o_hg, o_nsa], axis=-1) @ w_out[l])
        h = rmsnorm_2(x, norm2_g[l]) * (1.0 + sc2) + sh2
        x = x + g2 * moe_ffn(h, router_w[l], router_bias[l], w_exp_gu[l], w_exp_dn[l], w_sh_gu[l], w_sh_dn[l])
    return rmsnorm_2(x, final_g)


def setup_inputs(seed=0):
    out = dict(first_inputs(seed))
    for name, value in second_inputs(seed + 1).items():
        if name != "x":
            out[name + "_2"] = value
    return out


def reference(
    x, p, norm_ffn1, ffn1_w_gate, ffn1_w_up, ffn1_w_down, norm_mix, w_in_ab, sink_a, w_out_ab,
    w_in_c, rpb_c, w_out_c, norm_ffn2, ffn2_w_gate, ffn2_w_up, ffn2_w_down, norm_ple,
    w_ple_gate, w_ple_proj, norm_final, c_2, w_ada_2, b_ada_2, norm1_g_2, w_in_2,
    hg_lb_logits_2, hg_norm_g_2, cmp_pos_k_2, cmp_w1_k_2, cmp_b1_k_2, cmp_w2_k_2, cmp_pos_v_2,
    cmp_w1_v_2, cmp_b1_v_2, cmp_w2_v_2, w_out_2, norm2_g_2, router_w_2, router_bias_2,
    w_exp_gu_2, w_exp_dn_2, w_sh_gu_2, w_sh_dn_2, final_g_2,
):
    x = first_block(
        x, p, norm_ffn1, ffn1_w_gate, ffn1_w_up, ffn1_w_down, norm_mix, w_in_ab, sink_a,
        w_out_ab, w_in_c, rpb_c, w_out_c, norm_ffn2, ffn2_w_gate, ffn2_w_up, ffn2_w_down,
        norm_ple, w_ple_gate, w_ple_proj, norm_final,
    )
    return second_block(
        x, c_2, w_ada_2, b_ada_2, norm1_g_2, w_in_2, hg_lb_logits_2, hg_norm_g_2, cmp_pos_k_2,
        cmp_w1_k_2, cmp_b1_k_2, cmp_w2_k_2, cmp_pos_v_2, cmp_w1_v_2, cmp_b1_v_2, cmp_w2_v_2,
        w_out_2, norm2_g_2, router_w_2, router_bias_2, w_exp_gu_2, w_exp_dn_2, w_sh_gu_2,
        w_sh_dn_2, final_g_2,
    )


_drawn_inputs = setup_inputs


def setup_inputs(seed=0):
    import zlib

    import numpy as np

    out = dict(_drawn_inputs(seed))
    spreads = {}
    factors = {'sink_a': 56.32,
     'norm1_g_2': 2.969,
     'hg_norm_g_2': 16.467,
     'cmp_pos_k_2': 8.0,
     'cmp_b1_k_2': 60.97,
     'cmp_pos_v_2': 14.085,
     'cmp_b1_v_2': 64.0,
     'final_g_2': 7.93,
     'norm2_g_2': 4.7,
     'router_bias_2': 3.366}
    for name, (base, spread) in spreads.items():
        noise = np.random.default_rng([zlib.crc32(name.encode()), seed]).standard_normal(out[name].shape)
        drawn = base * np.exp(spread * noise) if base else spread * noise
        out[name] = __import__('jax').numpy.asarray(drawn.astype(out[name].dtype))
    for name, factor in factors.items():
        out[name] = (out[name] * factor).astype(out[name].dtype)
    return out
```

```python
from contextlib import ExitStack, contextmanager

import numpy as np

import concourse.bass as bass
from concourse import mybir

ALU = mybir.AluOpType
ACT = mybir.ActivationFunctionType
AX = mybir.AxisListType
F32 = mybir.dt.float32

P = 128
T = 512
TT = T // P
D = 1024
KD = D // P
FF = 2816
NF = FF // P
HD = 64
NEG = -1e30
EPS = 1e-6
UNIT = KD * 256
SLOT = max(UNIT, NF * P)
N_EXP = 64
EXP_H = 256
SCMAX = 384 + 512 + 512
ROUTED_SCALE = 2.5
HG_SCALE = 128 ** -0.5
N_CMP = (T - 32) // 16 + 1
GELU_C = 2.0 * (2.0 / np.pi) ** 0.5

A_PAIRS = [(0, 3), (1, 4), (2, 5), (6, 9), (7, 10), (8, 11)]
N_PAIRS = [(0, 4), (1, 5), (2, 6), (3, 7)]

NORMS = ["ffn1_0", "mix_0", "ffn2_0", "ple_0", "ffn1_1", "mix_1", "ffn2_1", "ple_1", "first", "norm1", "norm2", "final"]
COLS = {}
_at = 0
for _name, _n in ([(f"g_{n}", KD) for n in NORMS] + [
        ("b_ada", 48), ("c", KD), ("lb", 8), ("hg_g", 4), ("b1k", 2), ("b1v", 2), ("pe_k", 32), ("pe_v", 32),
        ("sink", 12), ("router_bias", N_EXP), ("w2k", 128), ("w2v", 128), ("router_w", KD * N_EXP)]):
    COLS[_name] = (_at, _n)
    _at += _n
NCOL = _at

PHASES = []
for _l in range(2):
    PHASES += [(f"gu_{_l}_0", NF), (f"down_{_l}_0", KD)]
    PHASES += [("in_ab", 10), ("v_ab", 4), ("out_ab", 4)] if _l == 0 else [("in_c", 8), ("v_c", 4), ("out_c", 4)]
    PHASES += [(f"gu_{_l}_1", NF), (f"down_{_l}_1", KD), (f"pg_{_l}", 4), (f"pp_{_l}", 4)]
PHASES += [("ada", 24), ("in_2", 10), ("tok_2", 4), ("cmp", 4), ("out_2", 4), ("shared", 4), ("experts", 3 * N_EXP)]
BASE = {}
_at = 0
for _name, _n in PHASES:
    assert _n % 2 == 0
    BASE[_name] = (_at, _n)
    _at += _n


def unit_floats(phase):
    if phase.startswith("down"):
        return NF * P
    return 2 * 256 if phase.startswith("pp") else UNIT


class Chain:

    def __init__(self, eng, sem):
        self.eng, self.sem, self.n, self.turn = eng, sem, 0, None

    def __call__(self, ins):
        ins.then_inc(self.sem, 1)
        self.n += 1
        self.eng.wait_ge(self.sem, self.n if self.turn is None else self.turn + self.n)

    @contextmanager
    def loop(self, turns, per):
        if turns == 1:
            yield 0
            return
        start = self.n
        with self.eng.Fori(0, turns) as i:
            self.turn = i * per
            yield i
            assert self.n == start + per, (self.n - start, per)
            self.turn = None
        self.n += per * (turns - 1)


def block_kernel(nc, dr, out, stop_at=None):
    with ExitStack() as ctx:
        def sb(name, n):
            return ctx.enter_context(nc.sbuf_tensor(name, [P, n], F32))

        def sem(name):
            return ctx.enter_context(nc.semaphore(name))

        def tiles(ap, n):
            return ap.rearrange("p (a n) -> p a n", n=n)

        h_buf = sb("h_buf", KD * T)
        xn_buf = sb("xn_buf", KD * T)
        ring_buf = sb("ring_buf", 2 * SLOT)
        big = sb("big", 16384)
        mixed_buf = sb("mixed_buf", KD * T)
        s_buf = sb("s_buf", 2 * SCMAX)
        pt_buf = sb("pt_buf", 2 * SCMAX)
        mask = sb("mask", 3072)
        rot = sb("rot", 2 * T)
        eye = sb("eye", P)
        ones = sb("ones", P)
        eps = sb("eps", 1)
        sq_buf = sb("sq_buf", 2 * T)
        sil_buf = sb("sil_buf", 2 * T)
        std = sb("std", T)
        rstd = sb("rstd", T)
        tmp_buf = sb("tmp_buf", 2 * T)
        diag_buf = sb("diag_buf", 6 * P)
        small = sb("small", 512)
        cols = sb("cols", NCOL)
        mod = sb("mod", 64)
        ps_t = ctx.enter_context(nc.psum_tensor("ps", [P, 8 * T], F32))

        h, xn, mixed = tiles(h_buf[:, :], T), tiles(xn_buf[:, :], T), tiles(mixed_buf[:, :], T)
        ring = [ring_buf[:, s * SLOT:(s + 1) * SLOT] for s in range(2)]
        sq, sil, tmp = tiles(sq_buf[:, :], T), tiles(sil_buf[:, :], T), tiles(tmp_buf[:, :], T)
        diag = tiles(diag_buf[:, :], P)
        ps = tiles(ps_t[:, :], T)
        hid = tiles(big[:, 0:NF * T], T)
        cos, sin = rot[:, 0:T], rot[:, T:2 * T]

        def col(name):
            a, n = COLS[name]
            return cols[:, a:a + n]

        consts_in = sem("consts_in")
        set_up = sem("set_up")
        loaded = [sem(f"loaded{s}") for s in range(2)]
        units_done = sem("units_done")
        evac_done = sem("evac_done")
        h_ready = sem("h_ready")
        sq_ready = sem("sq_ready")
        sq_used = sem("sq_used")
        std_ready = sem("std_ready")
        xn_ready = sem("xn_ready")
        sil_ready = sem("sil_ready")
        dve_own = sem("dve_own")
        act_own = sem("act_own")
        pool_own = sem("pool_own")
        out_done = sem("out_done")

        block = ctx.enter_context(nc.Block())

        NORM_N = {n: k for k, n in enumerate(NORMS)}
        H_STAGES = ["ffn1_0", "mix_0", "ffn2_0", "ple_0", "ffn1_1", "mix_1", "ffn2_1", "ple_1", "first", "mix_2", "moe"]
        H_AT = {n: KD * (k + 1) for k, n in enumerate(H_STAGES)}
        NORM_H = {"ffn1_0": 0, "mix_0": 8, "ffn2_0": 16, "ple_0": 24, "ffn1_1": 32, "mix_1": 40, "ffn2_1": 48,
                  "ple_1": 56, "first": 64, "norm1": 72, "norm2": 80, "final": 88}
        SIL_AT = {}
        at = 0
        for name, n in PHASES:
            if name.startswith("gu"):
                SIL_AT[name] = at
                at += n
        SIL_MOE = at

        def plan_a():
            q, kk = tiles(big[:, 0:12 * T], T), tiles(big[:, 12 * T:20 * T], T)
            v = tiles(big[:, 20 * T:20 * T + 4 * D], D)
            units = []
            for p in range(6):
                for hf in range(2):
                    r = slice(64 * hf, 64 * hf + 64)
                    for t in range(TT):
                        lo, hi = max(t - 1, 0), min(t + 2, TT)
                        n = (hi - lo) * P
                        a = (lo - t + 1) * P
                        kv = 2 * (p // 3) + hf
                        units.append(dict(
                            segs=[(q[r, p, t * P:t * P + P], kk[r, p // 3, lo * P:hi * P], mask[:, a:a + n], 0, n)],
                            groups=[(0, n)], sink=A_PAIRS[p][hf],
                            chunks=[(0, c * P, P, v[:, lo + c, kv * HD:kv * HD + HD]) for c in range(hi - lo)],
                            pair=p, out=p, half=hf, t=t, last=hf == 1 and t == TT - 1, first=hf == 0 and t == 0))
            return units

        def plan_b():
            q, kk = tiles(big[:, 0:12 * T], T), tiles(big[:, 12 * T:20 * T], T)
            v = tiles(big[:, 20 * T:20 * T + 4 * D], D)
            units = []
            for p in range(2):
                for hf in range(2):
                    r = slice(64 * hf, 64 * hf + 64)
                    for t in range(TT):
                        segs, chunks, at = [], [], 0
                        for g in range(3):
                            lo, hi = (max(t - 1, 0), min(t + 2, TT)) if g == 0 else (0, TT)
                            n = (hi - lo) * P
                            m0 = 384 + (lo - t + 1) * P if g == 0 else 768 + 896 * (g - 1) + 384 - t * P
                            segs.append((q[r, 6 + 2 * g + p, t * P:t * P + P], kk[r, 2 + 2 * g + p, lo * P:hi * P],
                                         mask[:, m0:m0 + n], at, n))
                            c0 = 256 + (4 * g + 2 * p + hf) * HD
                            chunks += [(0, at + c * P, P, v[:, lo + c, c0:c0 + HD]) for c in range(hi - lo)]
                            at += n
                        units.append(dict(segs=segs, groups=[(0, at)], sink=None, chunks=chunks, pair=p, out=6 + p,
                                          half=hf, t=t, last=hf == 1 and t == TT - 1, first=hf == 0 and t == 0))
            return units

        def plan_c():
            q, kk = tiles(big[:, 0:8 * T], T), tiles(big[:, 8 * T:16 * T], T)
            v = tiles(big[:, 16 * T:16 * T + 4 * D], D)
            units = []
            for p in range(8):
                for hf in range(2):
                    r = slice(64 * hf, 64 * hf + 64)
                    for t in range(TT):
                        a = 64 + 1024 * hf + (7 - 2 * t) * 64
                        units.append(dict(
                            segs=[(q[r, p, t * P:t * P + P], kk[r, p, :], mask[:, a:a + T], 0, T)],
                            groups=[(0, T)], sink=None,
                            chunks=[(0, c * P, P, v[:, c, (2 * p + hf) * HD:(2 * p + hf) * HD + HD]) for c in range(TT)],
                            pair=p, out=p, half=hf, t=t, last=hf == 1 and t == TT - 1, first=hf == 0 and t == 0))
            return units

        R_HQ, R_HF, R_HG = 0, 4 * T, 8 * T
        R_NQ, R_NR, R_KCV, R_KSW = 12 * T, 16 * T, 20 * T, 22 * T
        R_VI = 24 * T
        R_VSW = R_VI + TT * T
        R_GATE = R_VSW + TT * 256
        R_KCMP = R_GATE + TT * 24
        R_VCMP = R_KCMP + 32
        gates = tiles(big[:, R_GATE:R_GATE + TT * 24], 24)
        kcmp = big[:, R_KCMP:R_KCMP + 32]
        vcmp = tiles(big[:, R_VCMP:R_VCMP + 2 * HD], HD)

        def plan_n():
            q, qr = tiles(big[:, R_NQ:R_NR], T), tiles(big[:, R_NR:R_KCV], T)
            kk = tiles(big[:, R_KSW:R_VI], T)
            v = tiles(big[:, R_VSW:R_GATE], 256)
            units = []
            for p in range(4):
                for hf in range(2):
                    r = slice(64 * hf, 64 * hf + 64)
                    for t in range(TT):
                        n = (t + 1) * P
                        segs = [(qr[r, p, t * P:t * P + P], kk[r, 0, 0:n], mask[:, 384 - t * P:512], 0, n),
                                (qr[r, p, t * P:t * P + P], kk[r, 1, 0:n], mask[:, 384 - t * P:512], n, n),
                                (q[r, p, t * P:t * P + P], kcmp[r, :], mask[:, 512 + 32 * t:544 + 32 * t], 2 * n, 32)]
                        chunks = [(g, g * n + c * P, P, v[:, c, g * P + hf * HD:g * P + hf * HD + HD])
                                  for g in range(2) for c in range(t + 1)]
                        chunks.append((2, 2 * n, 32, vcmp[0:32, hf, :]))
                        units.append(dict(segs=segs, groups=[(0, n), (n, n), (2 * n, 32)], sink=None, chunks=chunks,
                                          gate=3 * N_PAIRS[p][hf], pair=p, out=4 + p, half=hf, t=t,
                                          last=hf == 1 and t == TT - 1, first=hf == 0 and t == 0))
            return units

        ATT = {}
        for name, units, sc_banks, pt_banks in (("a", plan_a(), (0, 1), (2, 3)), ("b", plan_b(), (0,), (3,)),
                                                ("c", plan_c(), (0, 1), (2, 3)), ("n", plan_n(), (0,), (3,))):
            ATT[name] = dict(
                units=units, sc=sc_banks, pt=pt_banks,
                mask_in=sem(f"{name}_mask_in"),
                qkv=sem(f"{name}_qkv"),
                sc_ready=sem(f"{name}_sc_ready"),
                sc_read=sem(f"{name}_sc_read"),
                negm=sem(f"{name}_negm"),
                exps=sem(f"{name}_exps"),
                fac=sem(f"{name}_fac"),
                diag=sem(f"{name}_diag"),
                pt_ready=sem(f"{name}_pt_ready"),
                pts=sem(f"{name}_pts"),
                pv=sem(f"{name}_pv"),
                out=sem(f"{name}_out"),
            )
        c_bias_in = [sem(f"c_bias_in{s}") for s in range(2)]
        c_bias = [sem(f"c_bias{s}") for s in range(2)]
        mx = small[:, 0:8]
        negm = small[:, 8:16]
        den = small[:, 16:24]
        es = small[:, 24:26]
        fac = small[:, 32:40]
        rden = small[:, 40:48]

        p_in = sem("p_in")
        hg = {n: sem(f"hg_{n}") for n in ("mask_in", "sig", "ln_in", "ln", "cum", "diff", "e", "ql", "kl", "qk", "mul", "acc",
                                          "ex_in", "ex", "kx", "x_ps", "x_sb", "o_ps", "o_sq", "o_sum", "o_std", "o_out", "lbe")}
        cm = {n: sem(f"cm_{n}") for n in ("blk", "h1", "g1", "th", "hid", "kv", "kv_sb")}
        rt = {n: sem(f"rt_{n}") for n in ("lg", "sig", "w", "wt_ps", "wt_sb", "wt_out", "ada_c", "gate")}
        moe = {n: sem(f"moe_{n}") for n in ("gu", "sil", "hid", "dn", "acc")}
        wrow_in = [sem(f"wrow_in{s}") for s in range(2)]

        def u(phase):
            return BASE[phase][0]

        X_PAIRS = [(a, b) for a in range(TT) for b in range(a + 1, TT)]

        STAGES = ["ffn1_0", "mix_0", "ffn2_0", "ple_0", "ffn1_1", "mix_1", "ffn2_1", "ple_1", "mix_2", "moe"]
        if stop_at is not None:
            STAGES = STAGES[:STAGES.index(stop_at) + 1]

        @block.sync
        def _(sp):
            sp.dma_start(h_buf[:, :], dr["xT"]).then_inc(consts_in, 16)

            def load(phase, turn, s):
                n = unit_floats(phase)
                sp.dma_start(ring[s][:, 0:n], dr[phase][bass.ds(2 * turn + s, 1), :, :].rearrange("a p n -> p (a n)")
                             ).then_inc(loaded[s], 16)

            def stream(phase):
                base, n = BASE[phase]
                for s in range(2):
                    if base:
                        sp.wait_ge(units_done, base + s - 1)
                    load(phase, 0, s)
                if n > 2:
                    with sp.Fori(1, n // 2) as i:
                        for s in range(2):
                            sp.wait_ge(units_done, i * 2 + (base + s - 1))
                            load(phase, i, s)

            def att_mask(name, ap, n, after=None):
                if after is not None:
                    sp.wait_ge(*after)
                sp.dma_start(mask[:, 0:n], dr[ap]).then_inc(ATT[name]["mask_in"], 16)

            for st in STAGES:
                if st.startswith("ffn"):
                    l, k = st[-1], int(st[3]) - 1
                    stream(f"gu_{l}_{k}")
                    stream(f"down_{l}_{k}")
                elif st.startswith("ple"):
                    l = st[-1]
                    sp.wait_ge(h_ready, NORM_H[f"ple_{l}"])
                    sp.dma_start(big[:, 8 * T:10 * T], dr["pT"][int(l), :, :]).then_inc(p_in, 16)
                    stream(f"pg_{l}")
                    stream(f"pp_{l}")
                elif st == "mix_0":
                    att_mask("a", "mask_ab", 2560)
                    stream("in_ab")
                    stream("v_ab")
                    stream("out_ab")
                elif st == "mix_1":
                    att_mask("c", "mask_c", 64, (h_ready, H_AT["mix_0"]))
                    stream("in_c")
                    stream("v_c")
                    for hd in range(16):
                        if hd >= 2:
                            sp.wait_ge(ATT["c"]["sc_read"], TT * (hd - 1))
                        b = 64 + 1024 * (hd % 2)
                        for r in range(2):
                            sp.dma_start(mask[64 * r:64 * r + 64, b + 64 * r:b + 64 * r + 960],
                                         dr["rpb"][hd, :, :]).then_inc(c_bias_in[hd % 2], 16)
                    stream("out_c")
                elif st == "mix_2":
                    stream("ada")
                    stream("in_2")
                    stream("tok_2")
                    sp.wait_ge(h_ready, H_AT["mix_1"])
                    sp.dma_start(mask[:, 0:1024], dr["mask_h"]).then_inc(hg["mask_in"], 16)
                    stream("cmp")
                    att_mask("n", "mask_n", 641, (hg["o_out"], 4))
                    stream("out_2")
                elif st == "moe":
                    stream("shared")
                    sp.wait_ge(rt["wt_sb"], 1)
                    sp.dma_start(dr["wt"], s_buf[0:N_EXP, 0:T]).then_inc(rt["wt_out"], 16)
                    sp.wait_ge(rt["wt_out"], 16)
                    base = u("experts")

                    def expert(e, turn, s):
                        if turn is None:
                            turn = 0
                        else:
                            sp.wait_ge(moe["hid"], 2 * turn + s - 1)
                        sp.dma_start(tmp[:, s, :], dr["wt"][bass.ds(2 * turn + s, 1), :].to_broadcast([P, T])
                                     ).then_inc(wrow_in[s], 16)
                        for j in range(3):
                            sl = (3 * s + j) % 2
                            sp.wait_ge(units_done, turn * 6 + (base + 3 * s + j - 1))
                            sp.dma_start(ring[sl][:, 0:UNIT],
                                         dr["experts"][bass.ds(turn * 6 + (3 * s + j), 1), :, :].rearrange(
                                             "a p n -> p (a n)")).then_inc(loaded[sl], 16)
                    for s in range(2):
                        expert(s, None, s)
                    with sp.Fori(1, N_EXP // 2) as i:
                        for s in range(2):
                            expert(None, i, s)
            if stop_at is None:
                sp.wait_ge(xn_ready, KD * len(NORMS))
                sp.dma_start(out, xn_buf[:, :]).then_inc(out_done, 16)
            else:
                sp.wait_ge(h_ready, H_AT[stop_at])
                sp.dma_start(out, h_buf[:, :]).then_inc(out_done, 16)
            sp.wait_ge(out_done, 16)

        @block.tensor
        def _(pe):
            pe.wait_ge(set_up, 1)
            pe.wait_ge(consts_in, 16 * 4)

            def unit_waits(turn, U, s):
                pe.wait_ge(loaded[s], turn * 16 + 16 * (U // 2 + 1))
                pe.wait_ge(evac_done, turn * 2 + (U + 1))

            @contextmanager
            def turns(n):
                if n == 1:
                    yield 0
                else:
                    with pe.Fori(0, n) as i:
                        yield i

            def norm_sum(name):
                n = NORM_N[name] * KD
                for k in range(KD):
                    pe.wait_ge(sq_ready, n + k + 1)
                    nc.tensor.matmul(ps[:, 7, :], ones[:, :], sq[:, k % 2, :], start=(k == 0), stop=(k == KD - 1)
                                     ).then_inc(sq_used, 1)

            def dense(phase, rhs, n=T, kt=KD):
                U, units = BASE[phase]
                with turns(units // 2) as i:
                    for s in range(2):
                        unit_waits(i, U + s, s)
                        w = tiles(ring[s][:, 0:kt * 256], 256)
                        for j in range(2):
                            for k in range(kt):
                                last = nc.tensor.matmul(ps[:, 2 * s + j, 0:n], w[:, k, j * P:j * P + P], rhs(k),
                                                        start=(k == 0), stop=(k == kt - 1))
                        last.then_inc(units_done, 1)

            def token_major(phase, first=0, units=None, width=256):
                U = u(phase) + first
                with turns((units or BASE[phase][1]) // 2) as i:
                    for s in range(2):
                        unit_waits(i, U + s, s)
                        w = tiles(ring[s][:, 0:UNIT], 256)
                        for t in range(TT):
                            for k in range(KD):
                                last = nc.tensor.matmul(ps[:, 2 * s + t // 2, 256 * (t % 2):256 * (t % 2) + 256],
                                                        xn[:, k, t * P:t * P + P], w[:, k, :],
                                                        start=(k == 0), stop=(k == KD - 1))
                        last.then_inc(units_done, 1)

            def xn_rhs(k):
                return xn[:, k, :]

            def ffn(st):
                l, k = st[-1], int(st[3]) - 1
                norm_sum(st)
                pe.wait_ge(xn_ready, KD * (NORM_N[st] + 1))
                dense(f"gu_{l}_{k}", xn_rhs)
                U, n = BASE[f"down_{l}_{k}"]
                pe.wait_ge(evac_done, U + 2)
                with turns(n // 2) as i:
                    for s in range(2):
                        unit_waits(i, U + s, s)
                        w = tiles(ring[s][:, 0:NF * P], P)
                        for f in range(NF):
                            last = nc.tensor.matmul(ps[:, 2 * s, :], w[:, f, :], hid[:, f, :],
                                                    start=(f == 0), stop=(f == NF - 1))
                        last.then_inc(units_done, 1)

            def attention(name):
                a = ATT[name]
                units, ns, np_ = a["units"], len(a["sc"]), len(a["pt"])
                pe.wait_ge(a["qkv"], 1)
                for i in range(len(units) + 2):
                    if i < len(units):
                        if i >= ns:
                            pe.wait_ge(a["sc_read"], i - ns + 1)
                        for g, (q, kk, _, _, n) in enumerate(units[i]["segs"]):
                            last = nc.tensor.matmul(ps[:, a["sc"][i % ns] + g, 0:n], q, kk, start=True, stop=True)
                        last.then_inc(a["sc_ready"], 1)
                    if 1 <= i <= len(units):
                        j = i - 1
                        un = units[j]
                        pe.wait_ge(a["diag"], j + 1)
                        if j >= np_:
                            pe.wait_ge(a["pts"], j - np_ + 1)
                        for c, (g, c0, n, _) in enumerate(un["chunks"]):
                            b = a["pt"][j % np_] + c // 4
                            last = nc.tensor.matmul(ps[0:n, b, (c % 4) * P:(c % 4) * P + P],
                                                    s_buf[:, (j % 2) * SCMAX + c0:(j % 2) * SCMAX + c0 + n],
                                                    diag[:, 3 * (j % 2) + g, :], start=True, stop=True)
                        last.then_inc(a["pt_ready"], 1)
                    if i >= 2:
                        j = i - 2
                        un = units[j]
                        pe.wait_ge(a["pts"], j + 1)
                        if un["first"] and un["pair"] >= 2:
                            pe.wait_ge(a["out"], un["pair"] - 1)
                        o = ps[64 * un["half"]:64 * un["half"] + 64, 6 + un["pair"] % 2, un["t"] * P:un["t"] * P + P]
                        for c, (_, _, n, v) in enumerate(un["chunks"]):
                            b0 = (j % 2) * SCMAX + c * P
                            last = nc.tensor.matmul(o, v, pt_buf[0:n, b0:b0 + P],
                                                    start=(c == 0), stop=(c == len(un["chunks"]) - 1))
                        last.then_inc(a["pv"], 1)

            def project_out(phase, ready):
                pe.wait_ge(*ready)
                dense(phase, lambda k: mixed[:, k, :])

            def hgrn():
                q, kk = tiles(big[:, R_HQ:R_HF], T), tiles(big[:, R_HF:R_HG], T)
                v = tiles(big[:, R_VI:R_VSW], T)
                for hd in range(4):
                    for lv in range(8):
                        i = 8 * hd + lv
                        if lv < 7:
                            pe.wait_ge(hg["ql"], 7 * hd + lv + 1)
                            pe.wait_ge(hg["kl"], 7 * hd + lv + 1)
                        if i >= 2:
                            pe.wait_ge(hg["mul"], i - 1)
                        for t in range(TT):
                            if lv == 7:
                                kl, ql = kk[:, hd, t * P:t * P + P], q[:, hd, t * P:t * P + P]
                            else:
                                kl = s_buf[:, (i % 2) * T + t * P:(i % 2) * T + t * P + P]
                                ql = s_buf[:, (2 + i % 2) * T + t * P:(2 + i % 2) * T + t * P + P]
                            last = nc.tensor.matmul(ps[:, i % 2, t * P:t * P + P], kl, ql, start=True, stop=True)
                        last.then_inc(hg["qk"], 1)
                    pe.wait_ge(hg["kx"], hd + 1)
                    for n, (a, b) in enumerate(X_PAIRS):
                        kx = pt_buf[:, (b - a) * T + a * P:(b - a) * T + a * P + P]
                        last = nc.tensor.matmul(ps[:, 2 + n // 4, (n % 4) * P:(n % 4) * P + P], kx,
                                                pt_buf[:, b * P:b * P + P], start=True, stop=True)
                    last.then_inc(hg["x_ps"], 1)
                    pe.wait_ge(hg["x_sb"], hd + 1)
                    pe.wait_ge(hg["acc"], 8 * (hd + 1))
                    if hd >= 1:
                        pe.wait_ge(hg["o_out"], hd)
                    for b in range(TT):
                        for a in range(b + 1):
                            if a == b:
                                at = xn_buf[:, b * P:b * P + P]
                            else:
                                n = X_PAIRS.index((a, b))
                                at = xn_buf[:, T + n * P:T + n * P + P]
                            last = nc.tensor.matmul(ps[:, 4, b * P:b * P + P], v[:, a, hd * P:hd * P + P], at,
                                                    start=(a == 0), stop=(a == b))
                    last.then_inc(hg["o_ps"], 1)
                    pe.wait_ge(hg["o_sq"], hd + 1)
                    nc.tensor.matmul(ps[:, 5, :], ones[:, :], sq[:, 0, :], start=True, stop=True
                                     ).then_inc(hg["o_sum"], 1)

            def compress():
                U = u("cmp")
                for kv in range(2):
                    pe.wait_ge(cm["blk"], kv + 1)
                    blk = s_buf[:, kv * 1024:kv * 1024 + 992].rearrange("p (l n) -> p l n", l=16)
                    for s in range(2):
                        pe.wait_ge(loaded[s], 16 * (U // 2 + kv + 1))
                        pe.wait_ge(evac_done, U + 2 * kv + s + 1)
                        w = tiles(ring[s][:, 0:UNIT], 256)
                        for l in range(8):
                            for j in range(2):
                                last = nc.tensor.matmul(ps[:, 2 * kv + j, 0:62], w[:, l, j * P:j * P + P],
                                                        blk[:, 8 * s + l, :], start=(s == 0 and l == 0),
                                                        stop=(s == 1 and l == 7))
                        last.then_inc(units_done, 1)
                for kv in range(2):
                    pe.wait_ge(cm["hid"], kv + 1)
                    w2 = tiles(col("w2k" if kv == 0 else "w2v"), HD)
                    hb = s_buf[:, 2048 + kv * 128:2048 + kv * 128 + 124].rearrange("p (j n) -> p j n", j=2)
                    for g in range(2):
                        for j in range(2):
                            if kv == 0:
                                o, a, b = ps[64 * g:64 * g + 64, 4, 0:N_CMP], w2[:, j, :], hb[:, j, g * 31:g * 31 + 31]
                            else:
                                o, a, b = ps[0:N_CMP, 5, g * HD:g * HD + HD], hb[:, j, g * 31:g * 31 + 31], w2[:, j, :]
                            last = nc.tensor.matmul(o, a, b, start=(j == 0), stop=(j == 1))
                    last.then_inc(cm["kv"], 1)

            def router():
                for t in range(TT):
                    for k in range(KD):
                        last = nc.tensor.matmul(ps[:, 4, t * N_EXP:(t + 1) * N_EXP], xn[:, k, t * P:t * P + P],
                                                tiles(col("router_w"), N_EXP)[:, k, :], start=(k == 0), stop=(k == KD - 1))
                last.then_inc(rt["lg"], 1)

            def router_t():
                pe.wait_ge(rt["w"], 1)
                wr = tiles(s_buf[:, 1024:1024 + TT * N_EXP], N_EXP)
                for t in range(TT):
                    last = nc.tensor.transpose(ps[0:N_EXP, 5, t * P:t * P + P], wr[:, t, :], eye[:, :])
                last.then_inc(rt["wt_ps"], 1)

            def expert_gu(turn, U, slots, n):
                for j in range(2):
                    s = slots[j]
                    pe.wait_ge(loaded[s], turn * 48 + 16 * ((U + j) // 2 + 1))
                    if j == 0 and n is not None:
                        pe.wait_ge(moe["hid"], n)
                    w = tiles(ring[s][:, 0:UNIT], 256)
                    for m in range(2):
                        for k in range(KD):
                            last = nc.tensor.matmul(ps[:, 2 * j + m, :], w[:, k, m * P:m * P + P], xn[:, k, :],
                                                    start=(k == 0), stop=(k == KD - 1))
                    last.then_inc(units_done, 1)

            def expert_dn(w, m, n, hbuf):
                if n is not None:
                    pe.wait_ge(moe["acc"], n)
                for k in range(2):
                    last = nc.tensor.matmul(ps[:, 4 + m % 4, :], w[:, k, :], hbuf[:, k, :], start=(k == 0), stop=(k == 1))
                last.then_inc(moe["dn"], 1)
                return last

            for st in STAGES:
                if st.startswith("ffn"):
                    ffn(st)
                elif st.startswith("ple"):
                    l = st[-1]
                    norm_sum(st)
                    pe.wait_ge(xn_ready, KD * (NORM_N[st] + 1))
                    dense(f"pg_{l}", xn_rhs)
                    pe.wait_ge(p_in, 16 * (int(l) + 1))
                    dense(f"pp_{l}", lambda k: big[:, (8 + k) * T:(9 + k) * T], kt=2)
                elif st == "mix_0":
                    norm_sum(st)
                    pe.wait_ge(xn_ready, KD * (NORM_N[st] + 1))
                    dense("in_ab", xn_rhs)
                    token_major("v_ab")
                    attention("a")
                    attention("b")
                    project_out("out_ab", (ATT["b"]["out"], 2))
                elif st == "mix_1":
                    norm_sum(st)
                    pe.wait_ge(xn_ready, KD * (NORM_N[st] + 1))
                    dense("in_c", xn_rhs)
                    token_major("v_c")
                    attention("c")
                    project_out("out_c", (ATT["c"]["out"], 8))
                elif st == "mix_2":
                    pe.wait_ge(rt["ada_c"], 1)
                    dense("ada", lambda k: mod[:, 56 + k:57 + k], n=1)
                    norm_sum("first")
                    norm_sum("norm1")
                    pe.wait_ge(xn_ready, KD * (NORM_N["norm1"] + 1))
                    dense("in_2", xn_rhs)
                    token_major("tok_2")
                    compress()
                    hgrn()
                    attention("n")
                    project_out("out_2", (ATT["n"]["out"], 4))
                elif st == "moe":
                    norm_sum("norm2")
                    pe.wait_ge(xn_ready, KD * (NORM_N["norm2"] + 1))
                    router()
                    U = u("shared")
                    pe.wait_ge(evac_done, U + 2)
                    expert_gu(0, U, (0, 1), None)
                    router_t()
                    hb = tiles(big[:, 0:2 * T], T)
                    pe.wait_ge(moe["hid"], 1)
                    pe.wait_ge(rt["wt_sb"], 1)
                    for j in range(2):
                        pe.wait_ge(loaded[j], 16 * ((U + 2 + j) // 2 + 1))
                        for m in range(4):
                            w = ring[j][:, 0:1024].rearrange("p (k n) -> p k n", k=2)[:, :, m * P:m * P + P]
                            last = expert_dn(w, 4 * j + m, 4 * j + m - 3 if 4 * j + m >= 4 else None, hb)
                        pe.wait_ge(moe["dn"], 4 * j + 4)
                        pe.sem_inc(units_done, 1)
                    U = u("experts")
                    with pe.Fori(0, N_EXP // 2) as i:
                        for s in range(2):
                            U0 = U + 3 * s
                            expert_gu(i, U0, [(3 * s) % 2, (3 * s + 1) % 2], i * 2 + (1 + s))
                            sl = (3 * s + 2) % 2
                            pe.wait_ge(moe["hid"], i * 2 + (2 + s))
                            pe.wait_ge(loaded[sl], i * 48 + 16 * ((U0 + 2) // 2 + 1))
                            hb = tiles(big[:, (1 + s) * 2 * T:(2 + s) * 2 * T], T)
                            for m in range(KD):
                                w = ring[sl][:, 0:UNIT].rearrange("p (k n) -> p k n", k=2)[:, :, m * P:m * P + P]
                                last = expert_dn(w, m, i * 16 + (8 * s + m + 8 - 3), hb)
                            pe.wait_ge(moe["dn"], i * 16 + (8 * s + 16))
                            pe.sem_inc(units_done, 1)
                    norm_sum("final")


        @block.scalar
        def _(act):
            link = Chain(act, act_own)
            act.dma_start(cols[:, :], dr["cols"]).then_inc(consts_in, 16)
            act.dma_start(rot[:, :], dr["rot"]).then_inc(consts_in, 16)
            act.dma_start(eye[:, :], dr["eye"]).then_inc(consts_in, 16)
            act.wait_ge(consts_in, 64)
            act.wait_ge(set_up, 1)

            def norm(name):
                n = NORM_N[name] * KD
                if NORM_H[name]:
                    act.wait_ge(h_ready, NORM_H[name])
                for k in range(KD):
                    if n + k >= 2:
                        act.wait_ge(sq_used, n + k - 1)
                    nc.scalar.activation(sq[:, k % 2, :], h[:, k, :], ACT.Square).then_inc(sq_ready, 1)
                act.wait_ge(sq_used, n + KD)
                nc.scalar.activation(std[:, :], ps[:, 7, :], ACT.Sqrt, bias=eps[:, 0:1], scale=1.0 / D
                                     ).then_inc(std_ready, 1)

            def ffn(st):
                norm(st)
                phase = f"gu_{st[-1]}_{int(st[3]) - 1}"
                U, n = BASE[phase]
                with link.loop(n // 2, 0) as i:
                    for s in range(2):
                        act.wait_ge(units_done, i * 2 + (U + s + 1))
                        act.wait_ge(evac_done, i * 2 + (U + s + 1))
                        nc.scalar.activation(sil[:, s, :], ps[:, 2 * s, :], ACT.Silu).then_inc(sil_ready, 1)

            def attention(name):
                a = ATT[name]
                units, np_ = a["units"], len(a["pt"])
                for i in range(len(units) + 1):
                    if i < len(units):
                        un, b = units[i], i % 2
                        act.wait_ge(a["negm"], i + 1)
                        if i >= 2:
                            act.wait_ge(a["fac"], i - 1)
                        if un["sink"] is not None:
                            nc.scalar.activation(es[:, b:b + 1], negm[:, 4 * b:4 * b + 1], ACT.Exp,
                                                 bias=col("sink")[:, un["sink"]:un["sink"] + 1])
                        for g, (c0, n) in enumerate(un["groups"]):
                            p = s_buf[:, b * SCMAX + c0:b * SCMAX + c0 + n]
                            last = nc.scalar.activation(p, p, ACT.Exp, bias=negm[:, 4 * b + g:4 * b + g + 1],
                                                        accum_out=den[:, 4 * b + g:4 * b + g + 1])
                        last.then_inc(a["exps"], 1)
                    if i >= 1:
                        j = i - 1
                        un, b = units[j], j % 2
                        act.wait_ge(a["pt_ready"], j + 1)
                        if j >= 2:
                            act.wait_ge(a["pv"], j - 1)
                        full = sum(c[2] == P for c in un["chunks"])
                        bank = a["pt"][j % np_]
                        src = ps_t[:, bank * T:bank * T + full * P]
                        last = nc.scalar.activation(pt_buf[:, b * SCMAX:b * SCMAX + full * P], src, ACT.Copy)
                        if full < len(un["chunks"]):
                            n = un["chunks"][-1][2]
                            last = nc.scalar.activation(
                                pt_buf[0:n, b * SCMAX + full * P:b * SCMAX + full * P + P],
                                ps_t[0:n, bank * T + full * P:bank * T + full * P + P], ACT.Copy)
                        last.then_inc(a["pts"], 1)

            def hgrn():
                z = big[:, R_HF:R_HG]
                act.wait_ge(evac_done, u("in_2") + 2 + 6)
                nc.scalar.activation(z, z, ACT.Sigmoid).then_inc(hg["sig"], 1)
                nc.scalar.activation(big[:, R_HG:R_NQ], big[:, R_HG:R_NQ], ACT.Silu).then_inc(hg["sig"], 1)
                gt = big[:, R_GATE:R_GATE + TT * 24]
                act.wait_ge(evac_done, u("tok_2") + 2 + 4)
                link(nc.scalar.activation(gt, gt, ACT.Sigmoid))
                act.wait_ge(hg["ln_in"], 1)
                nc.scalar.activation(xn_buf[:, 4 * T:8 * T], z, ACT.Ln).then_inc(hg["ln"], 1)
                for hd in range(4):
                    for lv in range(7):
                        i = 7 * hd + lv
                        e = tmp[:, i % 2, :]
                        act.wait_ge(hg["diff"], i + 1)
                        link(nc.scalar.activation(e, e, ACT.Abs))
                        nc.scalar.activation(e, e, ACT.Exp, scale=-1.0).then_inc(hg["e"], 1)
                    b = xn_buf[:, (4 + hd) * T:(5 + hd) * T]
                    act.wait_ge(hg["ex_in"], hd + 1)
                    nc.scalar.activation(sil[:, 0, :], b, ACT.Exp)
                    for t in range(TT):
                        last = nc.scalar.activation(sil[:, 1, t * P:t * P + P], b[:, t * P:t * P + P], ACT.Exp, scale=-1.0,
                                                    bias=b[:, t * P + P - 1:t * P + P])
                    last.then_inc(hg["ex"], 1)
                    act.wait_ge(hg["o_ps"], hd + 1)
                    nc.scalar.activation(sq[:, 0, :], ps[:, 4, :], ACT.Square).then_inc(hg["o_sq"], 1)
                    act.wait_ge(hg["o_sum"], hd + 1)
                    nc.scalar.activation(std[:, :], ps[:, 5, :], ACT.Sqrt, bias=eps[:, 0:1], scale=1.0 / P
                                         ).then_inc(hg["o_std"], 1)

            for st in STAGES:
                if st.startswith("ffn"):
                    ffn(st)
                elif st.startswith("ple"):
                    norm(st)
                    U, n = BASE[f"pg_{st[-1]}"]
                    g = tiles(big[:, 0:8 * T], T)
                    for m in range(n):
                        act.wait_ge(units_done, U + m + 1)
                        for j in range(2):
                            last = nc.scalar.activation(g[:, 2 * m + j, :], ps[:, 2 * (m % 2) + j, :], ACT.Sigmoid)
                        last.then_inc(evac_done, 1)
                elif st == "mix_0":
                    norm(st)
                    attention("a")
                    attention("b")
                elif st == "mix_1":
                    norm(st)
                    attention("c")
                elif st == "mix_2":
                    nc.scalar.activation(mod[:, 56:64], col("c"), ACT.Silu).then_inc(rt["ada_c"], 1)
                    norm("first")
                    norm("norm1")
                    for kv in range(2):
                        act.wait_ge(cm["th"], kv + 1)
                        t3 = s_buf[:, 2304 + kv * 128:2304 + kv * 128 + 124]
                        nc.scalar.activation(t3, t3, ACT.Sigmoid, scale=GELU_C).then_inc(cm["g1"], 1)
                    act.wait_ge(hg["lbe"], 1)
                    nc.scalar.activation(small[:, 64:72], small[:, 64:72], ACT.Exp).then_inc(hg["lbe"], 1)
                    hgrn()
                    attention("n")
                elif st == "moe":
                    norm("norm2")
                    act.wait_ge(rt["lg"], 1)
                    nc.scalar.activation(s_buf[:, 0:256], ps[:, 4, 0:256], ACT.Sigmoid).then_inc(rt["sig"], 1)
                    U = u("shared")
                    act.wait_ge(units_done, U + 2)
                    for j in range(2):
                        last = nc.scalar.activation(sil[:, j, :], ps[:, j, :], ACT.Silu)
                    last.then_inc(moe["sil"], 1)
                    U = u("experts")
                    with act.Fori(0, N_EXP // 2) as i:
                        for s in range(2):
                            act.wait_ge(units_done, i * 6 + (U + 3 * s + 1))
                            act.wait_ge(moe["hid"], i * 2 + (1 + s))
                            for j in range(2):
                                last = nc.scalar.activation(sil[:, j, :], ps[:, j, :], ACT.Silu)
                            last.then_inc(moe["sil"], 1)
                    norm("final")

        @block.gpsimd
        def _(pool):
            link = Chain(pool, pool_own)
            link(nc.gpsimd.memset(ones[:, :], 1.0))
            nc.gpsimd.memset(eps[:, :], EPS).then_inc(set_up, 1)
            pool.wait_ge(consts_in, 64)

            def attention(name):
                a = ATT[name]
                for i, un in enumerate(a["units"]):
                    if name == "c":
                        hd = 2 * un["pair"] + un["half"]
                        if i == 0:
                            bias_mask(0)
                        if un["t"] == 1 and hd + 1 < 16:
                            bias_mask(hd + 1)
                    pool.wait_ge(a["fac"], i + 1)
                    if i >= 2:
                        pool.wait_ge(a["pt_ready"], i - 1)
                    for g in range(len(un["groups"])):
                        last = nc.gpsimd.tensor_scalar(diag[:, 3 * (i % 2) + g, :], eye[:, :],
                                                       fac[:, 4 * (i % 2) + g:4 * (i % 2) + g + 1], None, ALU.mult)
                    last.then_inc(a["diag"], 1)

            def bias_mask(hd):
                if hd == 0:
                    pool.wait_ge(ATT["c"]["mask_in"], 16)
                pool.wait_ge(c_bias_in[hd % 2], 32 * (hd // 2 + 1))
                a = 64 + 1024 * (hd % 2)
                b = mask[:, a:a + 1024].rearrange("p (a n) -> p a n", n=64)
                last = nc.gpsimd.tensor_tensor(b, b, mask[:, None, 0:64].to_broadcast([P, 16, 64]), ALU.add)
                last.then_inc(c_bias[hd % 2], 1)

            def hgrn():
                q, kk = tiles(big[:, R_HQ:R_HF], T), tiles(big[:, R_HF:R_HG], T)
                acc = tiles(xn_buf[:, 0:T], P)
                for hd in range(4):
                    for lv in range(8):
                        i = 8 * hd + lv
                        if lv < 7:
                            pool.wait_ge(hg["e"], 7 * hd + lv + 1)
                            if i >= 2:
                                pool.wait_ge(hg["qk"], i - 1)
                            nc.gpsimd.tensor_tensor(s_buf[:, (i % 2) * T:(i % 2) * T + T], kk[:, hd, :],
                                                    tmp[:, (7 * hd + lv) % 2, :], ALU.mult).then_inc(hg["kl"], 1)
                        if lv >= 1:
                            add(hd, lv - 1, acc)
                    add(hd, 7, acc)

            def add(hd, lv, acc):
                i = 8 * hd + lv
                pool.wait_ge(hg["mul"], i + 1)
                src = tiles(pt_buf[:, 4 * T:5 * T], P) if i % 2 else tiles(s_buf[:, 4 * T:5 * T], P)
                if lv == 0:
                    if hd >= 1:
                        pool.wait_ge(hg["o_ps"], hd)
                    ins = nc.gpsimd.tensor_copy(acc, src)
                else:
                    pool.wait_ge(hg["acc"], i)
                    ins = nc.gpsimd.tensor_tensor(acc, acc, src, ALU.add)
                ins.then_inc(hg["acc"], 1)

            for st in STAGES:
                if st == "mix_0":
                    attention("a")
                    attention("b")
                elif st == "mix_1":
                    attention("c")
                elif st == "mix_2":
                    hgrn()
                    attention("n")

        @block.vector
        def _(dve):
            link = Chain(dve, dve_own)
            dve.wait_ge(consts_in, 64)
            dve.wait_ge(set_up, 1)
            dve.sem_inc(evac_done, 2)

            def norm(name, gain=None, shift=None, dst=xn):
                n = NORM_N[name] + 1
                gain = col(f"g_{name}") if gain is None else gain
                dve.wait_ge(std_ready, n)
                link(nc.vector.reciprocal(rstd[:, :], std[:, :]))
                for k in range(KD):
                    ins = nc.vector.scalar_tensor_tensor(out=dst[:, k, :], in0=h[:, k, :], scalar=gain[:, k:k + 1],
                                                         in1=rstd[:, :], op0=ALU.mult, op1=ALU.mult)
                    if shift is None:
                        ins.then_inc(xn_ready, 1)
                    else:
                        link(ins)
                        nc.vector.tensor_scalar(xn[:, k, :], xn[:, k, :], shift[:, k:k + 1], None, ALU.add
                                                ).then_inc(xn_ready, 1)

            def residual(phase, name, factor, per):
                U, n = BASE[phase]
                with link.loop(n // 2, 0) as i:
                    for s in range(2):
                        dve.wait_ge(units_done, i * 2 + (U + s + 1))
                        for j in range(per):
                            m = i * (2 * per) + (per * s + j)
                            hm = h_buf[:, bass.ds(m * T, T)]
                            f = factor if isinstance(factor, float) else factor[:, bass.ds(m, 1)]
                            last = nc.vector.scalar_tensor_tensor(out=hm, in0=ps[:, 2 * s + j, :], scalar=f, in1=hm,
                                                                  op0=ALU.mult, op1=ALU.add)
                            last.then_inc(h_ready, 1)
                        dve.wait_ge(h_ready, i * (2 * per) + (H_AT[name] - KD + per * (s + 1)))
                        dve.sem_inc(evac_done, 1)

            def ffn(st):
                norm(st)
                phase = f"gu_{st[-1]}_{int(st[3]) - 1}"
                U, n = BASE[phase]
                with link.loop(n // 2, 0) as i:
                    for s in range(2):
                        dve.wait_ge(sil_ready, i * 2 + (SIL_AT[phase] + s + 1))
                        nc.vector.tensor_tensor(big[:, bass.ds(i * (2 * T) + s * T, T)], sil[:, s, :],
                                                ps[:, 2 * s + 1, :], ALU.mult).then_inc(evac_done, 1)
                residual(f"down_{st[-1]}_{int(st[3]) - 1}", st, 0.5, 1)

            def rope_tile(src, dst, scale):
                link(nc.vector.scalar_tensor_tensor(out=dst, in0=src, scalar=scale, in1=cos, op0=ALU.mult, op1=ALU.mult))
                for g in range(4):
                    o, a = 32 * (g ^ 1), 32 * g
                    ins = nc.vector.scalar_tensor_tensor(out=tmp[o:o + 32, 0, :], in0=src[a:a + 32, :], scalar=scale,
                                                         in1=sin[a:a + 32, :], op0=ALU.mult, op1=ALU.mult)
                link(ins)
                return nc.vector.tensor_tensor(dst, dst, tmp[:, 0, :], ALU.add)

            def rope_units(phase, first, n, dst, scale):
                U = u(phase) + first
                with link.loop(n // 2, 12) as i:
                    for s in range(2):
                        dve.wait_ge(units_done, i * 2 + (U + s + 1))
                        for j in range(2):
                            d = big[:, bass.ds(i * (4 * T) + (dst + (2 * s + j) * T), T)]
                            link(rope_tile(ps[:, 2 * s + j, :], d, scale))
                        dve.sem_inc(evac_done, 1)

            def copy_units(phase, first, n, dst, scale=1.0):
                U = u(phase) + first
                for m in range(n):
                    dve.wait_ge(units_done, U + m + 1)
                    b = 2 * (m + first) % 4
                    nc.vector.tensor_scalar(big[:, dst + 2 * m * T:dst + 2 * (m + 1) * T],
                                            ps_t[:, b * T:(b + 2) * T], scale, None, ALU.mult).then_inc(evac_done, 1)

            def token_units(phase, first, n, dst, pitch, width=256):
                U = u(phase) + first
                d = tiles(big[:, dst:dst + TT * pitch], pitch)
                for m in range(n):
                    dve.wait_ge(units_done, U + m + 1)
                    b = 2 * (m + first) % 4
                    nc.vector.tensor_copy(d[:, :, m * 256:m * 256 + width],
                                          tiles(ps_t[:, b * T:(b + 2) * T], 256)[:, :, 0:width]).then_inc(evac_done, 1)

            def attention(name):
                a = ATT[name]
                units, ns = a["units"], len(a["sc"])
                dve.wait_ge(a["mask_in"], 16)
                done = 0
                for i in range(len(units) + 3):
                    if i < len(units):
                        un, b = units[i], i % 2
                        dve.wait_ge(a["sc_ready"], i + 1)
                        if i >= 2:
                            dve.wait_ge(a["pt_ready"], i - 1)
                        if name == "c" and un["t"] == 0:
                            hd = 2 * un["pair"] + un["half"]
                            dve.wait_ge(c_bias[hd % 2], hd // 2 + 1)
                        for g, (_, _, add, c0, n) in enumerate(un["segs"]):
                            last = nc.vector.tensor_tensor_reduce(
                                out=s_buf[:, b * SCMAX + c0:b * SCMAX + c0 + n], in0=ps[:, a["sc"][i % ns] + g, 0:n],
                                in1=add, scale=1.0, scalar=-3e38, op0=ALU.add, op1=ALU.max,
                                accum_out=mx[:, 4 * b + g:4 * b + g + 1])
                        last.then_inc(a["sc_read"], 1)
                        dve.wait_ge(a["sc_read"], i + 1)
                        ng = len(un["segs"])
                        m = mx[:, 4 * b:4 * b + ng]
                        if un["sink"] is not None:
                            ins = nc.vector.tensor_scalar(negm[:, 4 * b:4 * b + 1], m,
                                                          col("sink")[:, un["sink"]:un["sink"] + 1], -1.0, ALU.max, ALU.mult)
                        elif len(un["groups"]) < ng:
                            ins = nc.vector.tensor_reduce(negm[:, 4 * b:4 * b + 1], m, AX.X, ALU.max, negate=True)
                        else:
                            ins = nc.vector.tensor_scalar(negm[:, 4 * b:4 * b + ng], m, -1.0, None, ALU.mult)
                        ins.then_inc(a["negm"], 1)
                    if 1 <= i <= len(units):
                        j = i - 1
                        un, b = units[j], j % 2
                        ng = len(un["groups"])
                        dve.wait_ge(a["exps"], j + 1)
                        if j >= 2:
                            dve.wait_ge(a["diag"], j - 1)
                        dn = den[:, 4 * b:4 * b + ng]
                        if un["sink"] is not None:
                            link(nc.vector.tensor_tensor(rden[:, 4 * b:4 * b + 1], dn, es[:, b:b + 1], ALU.add))
                            dn = rden[:, 4 * b:4 * b + 1]
                        if "gate" in un:
                            link(nc.vector.reciprocal(rden[:, 4 * b:4 * b + ng], dn))
                            gt = gates[:, un["t"], un["gate"]:un["gate"] + 3]
                            nc.vector.tensor_tensor(fac[:, 4 * b:4 * b + 2], rden[:, 4 * b:4 * b + 2], gt[:, 1:3], ALU.mult)
                            ins = nc.vector.tensor_tensor(fac[:, 4 * b + 2:4 * b + 3], rden[:, 4 * b + 2:4 * b + 3], gt[:, 0:1],
                                                          ALU.mult)
                        else:
                            ins = nc.vector.reciprocal(fac[:, 4 * b:4 * b + ng], dn)
                        ins.then_inc(a["fac"], 1)
                    if i >= 3 and units[i - 3]["last"]:
                        un = units[i - 3]
                        dve.wait_ge(a["pv"], i - 2)
                        nc.vector.tensor_copy(mixed[:, un["out"], :], ps[:, 6 + un["pair"] % 2, :]).then_inc(a["out"], 1)

            def compress():
                for kv in range(2):
                    pe_c = col("pe_k" if kv == 0 else "pe_v")
                    blk = s_buf[:, kv * 1024:kv * 1024 + 992].rearrange("p (l g c) -> p g c l", l=16, g=2)
                    src = big[:, R_KCV + kv * T:R_KCV + (kv + 1) * T]
                    for g in range(2):
                        for par in range(2):
                            for half in range(2):
                                r = slice(64 * g, 64 * g + 64)
                                tk = src[r, 16 * half:16 * half + 16 * N_CMP].rearrange("p (c m q) -> p c m q", m=8, q=2)
                                pos = pe_c[r, 16 * half:16 * half + 16].rearrange("p (m q) -> p m q", q=2)
                                ins = nc.vector.tensor_tensor(
                                    blk[64 * par:64 * par + 64, g, :, 8 * half:8 * half + 8], tk[:, :, :, par],
                                    pos[:, None, :, par].to_broadcast([64, N_CMP, 8]), ALU.add)
                    ins.then_inc(cm["blk"], 1)
                U = u("cmp")
                for kv in range(2):
                    dve.wait_ge(units_done, U + 2 * kv + 2)
                    x1 = s_buf[:, 2048 + kv * 128:2048 + kv * 128 + 124].rearrange("p (j n) -> p j n", j=2)
                    t3 = s_buf[:, 2304 + kv * 128:2304 + kv * 128 + 124].rearrange("p (j n) -> p j n", j=2)
                    b1 = col("b1k" if kv == 0 else "b1v")
                    for j in range(2):
                        ins = nc.vector.tensor_scalar(x1[:, j, :], ps[:, 2 * kv + j, 0:62], b1[:, j:j + 1], None, ALU.add)
                    link(ins)
                    dve.sem_inc(evac_done, 2)
                    link(nc.vector.tensor_tensor(t3, x1, x1, ALU.mult))
                    link(nc.vector.tensor_scalar(t3, t3, 0.044715, 1.0, ALU.mult, ALU.add))
                    nc.vector.tensor_tensor(t3, t3, x1, ALU.mult).then_inc(cm["th"], 1)
                for kv in range(2):
                    x1 = s_buf[:, 2048 + kv * 128:2048 + kv * 128 + 124]
                    t3 = s_buf[:, 2304 + kv * 128:2304 + kv * 128 + 124]
                    dve.wait_ge(cm["g1"], kv + 1)
                    nc.vector.tensor_tensor(x1, x1, t3, ALU.mult).then_inc(cm["hid"], 1)
                nc.vector.memset(kcmp, 0.0)
                link(nc.vector.memset(big[0:32, R_VCMP:R_VCMP + 2 * HD], 0.0))
                dve.wait_ge(cm["kv"], 2)
                nc.vector.tensor_copy(kcmp[:, 0:N_CMP], ps[:, 4, 0:N_CMP])
                link(nc.vector.tensor_copy(big[0:N_CMP, R_VCMP:R_VCMP + 2 * HD], ps[0:N_CMP, 5, 0:2 * HD]))

            def hgrn():
                q, f = tiles(big[:, R_HQ:R_HF], T), tiles(big[:, R_HF:R_HG], T)
                lbs = small[:, 64:72]
                lg = col("lb")
                m = small[:, 72:76]
                link(nc.vector.tensor_tensor(m, lg[:, 0:4], lg[:, 4:8], ALU.max))
                nc.vector.tensor_tensor(lbs[:, 0:4], lg[:, 0:4], m, ALU.subtract)
                nc.vector.tensor_tensor(lbs[:, 4:8], lg[:, 4:8], m, ALU.subtract).then_inc(hg["lbe"], 1)
                dve.wait_ge(hg["lbe"], 2)
                link(nc.vector.tensor_tensor(m, lbs[:, 0:4], lbs[:, 4:8], ALU.add))
                link(nc.vector.reciprocal(small[:, 76:80], m))
                lb, lb1 = small[:, 80:84], small[:, 84:88]
                nc.vector.tensor_tensor(lb, lbs[:, 0:4], small[:, 76:80], ALU.mult)
                link(nc.vector.tensor_tensor(lb1, lbs[:, 4:8], small[:, 76:80], ALU.mult))
                dve.wait_ge(hg["sig"], 2)
                for hd in range(4):
                    ins = nc.vector.tensor_scalar(f[:, hd, :], f[:, hd, :], lb1[:, hd:hd + 1], lb[:, hd:hd + 1],
                                                  ALU.mult, ALU.add)
                link(ins)
                nc.vector.tensor_scalar(big[:, R_HF:R_HG], big[:, R_HF:R_HG], 2.0 ** -64, None, ALU.max
                                        ).then_inc(hg["ln_in"], 1)
                dve.wait_ge(hg["ln"], 1)
                link(nc.vector.tensor_scalar(big[:, R_HF:R_HG], big[:, R_HF:R_HG], -1.0, 1.0, ALU.mult, ALU.add))
                for n in range(4 * TT):
                    lf = xn_buf[:, 4 * T + n * P:4 * T + n * P + P]
                    ins = nc.vector.tensor_tensor_scan(mixed_buf[:, n * P:n * P + P],
                                                       ones[:, :], lf, 0.0, ALU.mult, ALU.add)
                link(ins)
                link(nc.vector.tensor_copy(xn_buf[:, 4 * T:8 * T], mixed_buf[:, 0:4 * T]))
                dve.sem_inc(hg["cum"], 1)
                dve.wait_ge(hg["mask_in"], 16)
                for hd in range(4):
                    b = xn_buf[:, (4 + hd) * T:(5 + hd) * T]

                    def diff(lv):
                        i = 7 * hd + lv
                        half = 64 >> lv
                        if i >= 2:
                            dve.wait_ge(hg["kl"], i - 1)
                            dve.wait_ge(hg["ql"], i - 1)
                        bv = b.rearrange("p (n c) -> p n c", c=2 * half)
                        nc.vector.tensor_tensor(tmp[:, i % 2, :].rearrange("p (n c) -> p n c", c=2 * half), bv,
                                                bv[:, :, half - 1:half].to_broadcast([P, T // (2 * half), 2 * half]),
                                                ALU.subtract).then_inc(hg["diff"], 1)

                    def masked(lv):
                        i = 8 * hd + lv
                        dve.wait_ge(hg["qk"], i + 1)
                        if i >= 2:
                            dve.wait_ge(hg["acc"], i - 1)
                        dst = tiles(pt_buf[:, 4 * T:5 * T], P) if i % 2 else tiles(s_buf[:, 4 * T:5 * T], P)
                        nc.vector.tensor_tensor(dst, tiles(ps[:, i % 2, :], P),
                                                mask[:, None, lv * P:lv * P + P].to_broadcast([P, TT, P]), ALU.mult
                                                ).then_inc(hg["mul"], 1)

                    diff(0)
                    for lv in range(8):
                        i = 8 * hd + lv
                        if lv + 1 < 7:
                            diff(lv + 1)
                        if lv < 7:
                            dve.wait_ge(hg["e"], 7 * hd + lv + 1)
                            if i >= 2:
                                dve.wait_ge(hg["qk"], i - 1)
                            nc.vector.tensor_tensor(s_buf[:, (2 + i % 2) * T:(3 + i % 2) * T], q[:, hd, :],
                                                    tmp[:, (7 * hd + lv) % 2, :], ALU.mult).then_inc(hg["ql"], 1)
                        if lv >= 1:
                            masked(lv - 1)
                    dve.sem_inc(hg["ex_in"], 1)
                    masked(7)
                    dve.wait_ge(hg["ex"], hd + 1)
                    if hd >= 1:
                        dve.wait_ge(hg["x_ps"], hd)
                    eb, ek = sil[:, 0, :], sil[:, 1, :]
                    nc.vector.tensor_tensor(pt_buf[:, 0:T], q[:, hd, :], eb, ALU.mult)
                    link(nc.vector.tensor_tensor(pt_buf[:, T:2 * T], f[:, hd, :], ek, ALU.mult))
                    for t in range(2):
                        ins = nc.vector.tensor_scalar(pt_buf[:, 2 * T + t * P:2 * T + t * P + P],
                                                      pt_buf[:, T + t * P:T + t * P + P],
                                                      eb[:, (t + 2) * P - 1:(t + 2) * P], None, ALU.mult)
                    link(ins)
                    nc.vector.tensor_scalar(pt_buf[:, 3 * T:3 * T + P], pt_buf[:, 2 * T:2 * T + P],
                                            eb[:, 3 * P - 1:3 * P], None, ALU.mult).then_inc(hg["kx"], 1)
                    dve.wait_ge(hg["x_ps"], hd + 1)
                    if hd >= 1:
                        dve.wait_ge(hg["o_ps"], hd)
                    nc.vector.tensor_copy(xn_buf[:, T:T + 6 * P], ps_t[:, 2 * T:2 * T + 6 * P]).then_inc(hg["x_sb"], 1)
                    dve.wait_ge(hg["o_std"], hd + 1)
                    link(nc.vector.reciprocal(rstd[:, :], std[:, :]))
                    link(nc.vector.scalar_tensor_tensor(out=mixed[:, hd, :], in0=ps[:, 4, :], scalar=col("hg_g")[:, hd:hd + 1],
                                                        in1=rstd[:, :], op0=ALU.mult, op1=ALU.mult))
                    nc.vector.tensor_tensor(mixed[:, hd, :], mixed[:, hd, :], tiles(big[:, R_HG:R_NQ], T)[:, hd, :],
                                            ALU.mult).then_inc(hg["o_out"], 1)

            def router():
                IMM = -3e30
                sc = tiles(s_buf[:, 0:256], N_EXP)
                ch = tiles(s_buf[:, 256:512], N_EXP)
                m8 = tiles(s_buf[:, 512:768], 8)
                rep = tiles(s_buf[:, 768:1024], N_EXP)
                wr = tiles(s_buf[:, 1024:1280], N_EXP)
                dve.wait_ge(rt["sig"], 1)
                link(nc.vector.tensor_tensor(ch, sc, col("router_bias")[:, None, :].to_broadcast([P, TT, N_EXP]), ALU.add))
                for n in range(32):
                    ins = nc.vector.max(m8[:, n, :], s_buf[:, 256 + 8 * n:264 + 8 * n])
                gs = tiles(small[:, 128:176], 12)
                g8, gr = tiles(small[:, 176:208], 8), tiles(small[:, 208:256], 12)
                link(nc.vector.memset(small[:, 128:176], 3e30))
                ins = nc.vector.tensor_tensor(gs[:, :, 0:8], s_buf[:, 512:768].rearrange("p (t g e) -> p t g e", g=8, e=8)[:, :, :, 0],
                                              s_buf[:, 512:768].rearrange("p (t g e) -> p t g e", g=8, e=8)[:, :, :, 1], ALU.add)
                link(ins)
                for t in range(TT):
                    ins = nc.vector.max(g8[:, t, :], gs[:, t, :])
                link(ins)
                for t in range(TT):
                    ins = nc.vector.match_replace(gr[:, t, :], g8[:, t, :], gs[:, t, :], IMM)
                link(ins)
                pen = tiles(small[:, 256:288], 8)
                link(nc.vector.tensor_scalar(pen, gr[:, :, 0:8], IMM, NEG, ALU.not_equal, ALU.mult))
                c4 = s_buf[:, 256:512].rearrange("p (t g e) -> p t g e", g=8, e=8)
                for t in range(TT):
                    ins = nc.vector.tensor_tensor(c4[:, t], c4[:, t], pen[:, t, :, None].to_broadcast([P, 8, 8]), ALU.add)
                link(ins)
                v8 = tiles(small[:, 288:320], 8)
                for t in range(TT):
                    ins = nc.vector.max(v8[:, t, :], ch[:, t, :])
                link(ins)
                for t in range(TT):
                    ins = nc.vector.match_replace(rep[:, t, :], v8[:, t, :], ch[:, t, :], IMM)
                link(ins)
                sm, rs = small[:, 320:324], small[:, 324:328]
                for t in range(TT):
                    ins = nc.vector.scalar_tensor_tensor(out=wr[:, t, :], in0=rep[:, t, :], scalar=IMM, in1=sc[:, t, :],
                                                         op0=ALU.is_equal, op1=ALU.mult)
                link(ins)
                link(nc.vector.tensor_reduce(sm, wr, AX.X, ALU.add))
                link(nc.vector.reciprocal(rs, sm))
                for t in range(TT):
                    ins = nc.vector.tensor_scalar(wr[:, t, :], wr[:, t, :], rs[:, t:t + 1], ROUTED_SCALE, ALU.mult, ALU.mult)
                ins.then_inc(rt["w"], 1)

            def expert_add(m, n, first):
                dve.wait_ge(moe["dn"], n)
                y = mixed[:, m, :]
                if first:
                    nc.vector.tensor_copy(y, ps[:, 4 + m % 4, :]).then_inc(moe["acc"], 1)
                else:
                    nc.vector.tensor_tensor(y, y, ps[:, 4 + m % 4, :], ALU.add).then_inc(moe["acc"], 1)

            for st in STAGES:
                if st.startswith("ffn"):
                    ffn(st)
                elif st.startswith("ple"):
                    l = st[-1]
                    norm(st)
                    g = tiles(big[:, 0:8 * T], T)
                    U, n = BASE[f"pp_{l}"]
                    dve.wait_ge(evac_done, U + 2)
                    for m in range(n):
                        dve.wait_ge(units_done, U + m + 1)
                        for j in range(2):
                            k = 2 * m + j
                            link(nc.vector.tensor_tensor(g[:, k, :], g[:, k, :], ps[:, 2 * (m % 2) + j, :], ALU.mult))
                            nc.vector.tensor_tensor(h[:, k, :], h[:, k, :], g[:, k, :], ALU.add).then_inc(h_ready, 1)
                        dve.sem_inc(evac_done, 1)
                elif st == "mix_0":
                    norm(st)
                    rope_units("in_ab", 0, 6, 0, HD ** -0.5)
                    rope_units("in_ab", 6, 4, 12 * T, 1.0)
                    token_units("v_ab", 0, 4, 20 * T, D)
                    dve.wait_ge(evac_done, u("v_ab") + 6)
                    dve.sem_inc(ATT["a"]["qkv"], 1)
                    dve.sem_inc(ATT["b"]["qkv"], 1)
                    dve.sem_inc(ATT["b"]["mask_in"], 16)
                    attention("a")
                    attention("b")
                    residual("out_ab", st, 1.0, 2)
                elif st == "mix_1":
                    norm(st)
                    copy_units("in_c", 0, 4, 0, HD ** -0.5)
                    copy_units("in_c", 4, 4, 8 * T)
                    token_units("v_c", 0, 4, 16 * T, D)
                    dve.wait_ge(evac_done, u("v_c") + 6)
                    dve.sem_inc(ATT["c"]["qkv"], 1)
                    attention("c")
                    residual("out_c", st, 1.0, 2)
                elif st == "mix_2":
                    U, n = BASE["ada"]
                    with link.loop(n // 2, 0) as i:
                        for s in range(2):
                            dve.wait_ge(units_done, i * 2 + (U + s + 1))
                            for j in range(2):
                                m = i * 4 + (2 * s + j)
                                a = COLS["b_ada"][0]
                                ins = nc.vector.tensor_tensor(mod[:, bass.ds(m, 1)], ps[:, 2 * s + j, 0:1],
                                                              cols[:, bass.ds(m + a, 1)], ALU.add)
                            ins.then_inc(evac_done, 1)
                    dve.wait_ge(evac_done, U + n + 2)
                    nc.vector.scalar_tensor_tensor(out=col("g_norm1"), in0=mod[:, 8:16], scalar=1.0, in1=col("g_norm1"),
                                                   op0=ALU.add, op1=ALU.mult)
                    link(nc.vector.scalar_tensor_tensor(out=col("g_norm2"), in0=mod[:, 32:40], scalar=1.0, in1=col("g_norm2"),
                                                        op0=ALU.add, op1=ALU.mult))
                    norm("first", dst=h)
                    dve.wait_ge(xn_ready, KD * (NORM_N["first"] + 1))
                    dve.sem_inc(h_ready, KD)
                    norm("norm1", shift=mod[:, 0:8])
                    copy_units("in_2", 0, 2, R_HQ, HG_SCALE)
                    copy_units("in_2", 2, 4, R_HF)
                    U = u("in_2") + 6
                    for m in range(2):
                        dve.wait_ge(units_done, U + m + 1)
                        for j in range(2):
                            k = 2 * m + j
                            src = ps[:, 2 * (m % 2) + j, :]
                            nc.vector.tensor_scalar(big[:, R_NQ + k * T:R_NQ + (k + 1) * T], src, HD ** -0.5, None, ALU.mult)
                            link(rope_tile(src, big[:, R_NR + k * T:R_NR + (k + 1) * T], HD ** -0.5))
                        dve.sem_inc(evac_done, 1)
                    copy_units("in_2", 8, 1, R_KCV)
                    U = u("in_2") + 9
                    dve.wait_ge(units_done, U + 1)
                    for j in range(2):
                        link(rope_tile(ps[:, 2 + j, :], big[:, R_KSW + j * T:R_KSW + (j + 1) * T], 1.0))
                    dve.sem_inc(evac_done, 1)
                    token_units("tok_2", 0, 2, R_VI, T)
                    token_units("tok_2", 2, 1, R_VSW, 256)
                    token_units("tok_2", 3, 1, R_GATE, 24, width=24)
                    dve.wait_ge(evac_done, u("tok_2") + 6)
                    compress()
                    hgrn()
                    g3 = gates[:, 0, :].rearrange("p (n c) -> p n c", c=3)
                    dve.wait_ge(ATT["n"]["mask_in"], 16)
                    link(nc.vector.tensor_scalar(g3[:, :, 0], g3[:, :, 0], mask[:, 640:641], None, ALU.mult))
                    dve.sem_inc(ATT["n"]["qkv"], 1)
                    attention("n")
                    residual("out_2", st, mod[:, 16:24], 2)
                elif st == "moe":
                    norm("norm2", shift=mod[:, 24:32])
                    router()
                    dve.wait_ge(moe["sil"], 1)
                    hb = tiles(big[:, 0:2 * T], T)
                    for j in range(2):
                        ins = nc.vector.tensor_tensor(hb[:, j, :], sil[:, j, :], ps[:, 2 + j, :], ALU.mult)
                    ins.then_inc(moe["hid"], 1)
                    dve.wait_ge(rt["wt_ps"], 1)
                    nc.vector.tensor_copy(s_buf[0:N_EXP, 0:T], ps[0:N_EXP, 5, :]).then_inc(rt["wt_sb"], 1)
                    for m in range(KD):
                        expert_add(m, m + 1, True)
                    U = u("experts")
                    with dve.Fori(0, N_EXP // 2) as i:
                        for s in range(2):
                            hb = tiles(big[:, (1 + s) * 2 * T:(2 + s) * 2 * T], T)
                            wr = tmp[:, s, :]
                            dve.wait_ge(moe["sil"], i * 2 + (s + 2))
                            dve.wait_ge(wrow_in[s], i * 16 + 16)
                            for j in range(2):
                                ins = nc.vector.tensor_tensor(sil[:, j, :], sil[:, j, :], wr, ALU.mult)
                            ins.then_inc(moe["gu"], 1)
                            dve.wait_ge(moe["gu"], i * 2 + (s + 1))
                            dve.wait_ge(units_done, i * 6 + (U + 3 * s + 2))
                            for j in range(2):
                                ins = nc.vector.tensor_tensor(hb[:, j, :], sil[:, j, :], ps[:, 2 + j, :], ALU.mult)
                            ins.then_inc(moe["hid"], 1)
                            for m in range(KD):
                                expert_add(m, i * 16 + (8 * s + 8 + m + 1), False)
                    dve.wait_ge(moe["acc"], KD * (N_EXP + 1))
                    for m in range(KD):
                        nc.vector.scalar_tensor_tensor(out=h[:, m, :], in0=mixed[:, m, :], scalar=mod[:, 40 + m:41 + m],
                                                       in1=h[:, m, :], op0=ALU.mult, op1=ALU.add).then_inc(h_ready, 1)
                    norm("final")


def _units(w, width=256):
    k, n = w.shape
    return np.ascontiguousarray(w.reshape(k // P, P, n // width, width).transpose(2, 1, 0, 3)).reshape(
        n // width, P, (k // P) * width)


def _column(v):
    return v.reshape(-1, P).T


def _heads(w, order):
    return np.concatenate([w[:, a * HD:(a + 1) * HD] for a in order], axis=1)


def _constants():
    q, kk = np.arange(P)[:, None], np.arange(896)[None, :]
    off = kk - 384 - q
    near = kk[:, :384] - P - q
    where = lambda ok: np.where(ok, np.float32(0), np.float32(NEG)).astype(np.float32)
    mask_ab = np.concatenate([
        where(np.abs(near) <= 128), where(np.abs(near) <= 64),
        where((np.abs(off) <= 256) & (off % 4 == 0)), where((np.abs(off) <= 1024) & (off % 16 == 0))], axis=1)
    qj, kj = np.arange(64)[:, None], np.arange(64)[None, :]
    start = np.clip(qj - 8, 0, 48)
    mask_c = np.tile(where((kj >= start) & (kj < start + 16)), (2, 1))
    causal = where(off[:, :512] <= 0)
    pos = np.arange(T).reshape(TT, P).T[:, :, None]
    c = np.arange(32)[None, None, :]
    cmp_ok = (c * 16 + 31 <= pos) & (c < N_CMP)
    mask_n = np.concatenate([causal, where(cmp_ok).reshape(P, TT * 32)], axis=1)
    mask_n = np.concatenate([mask_n, (np.arange(P) >= 31).astype(np.float32)[:, None]], axis=1)
    s, t = np.arange(P)[:, None], np.arange(P)[None, :]
    levels = []
    for lv in range(7):
        half = 64 >> lv
        levels.append((s // (2 * half) == t // (2 * half)) & (s % (2 * half) < half) & (t % (2 * half) >= half))
    levels.append(s == t)
    mask_h = np.concatenate(levels, axis=1).astype(np.float32)
    inv = (np.float32(10000.0) ** (-np.arange(32, dtype=np.float32) / np.float32(32))).astype(np.float32)
    ang = np.arange(T, dtype=np.float32)[None, :] * inv[:, None]
    co, si = np.cos(ang).astype(np.float32), np.sin(ang).astype(np.float32)
    rot = np.concatenate([np.tile(co, (4, 1)), np.concatenate([si, -si, si, -si], axis=0)], axis=1)
    return dict(mask_ab=mask_ab, mask_c=mask_c, mask_n=mask_n, mask_h=mask_h, rot=rot,
                eye=np.eye(P, dtype=np.float32))


def _lay_out(i):
    f = lambda n: np.asarray(i[n])
    c = _constants()
    a = {k: c[k] for k in ("mask_ab", "mask_c", "mask_n", "mask_h", "rot", "eye")}
    tok = lambda x: np.ascontiguousarray(x.T.reshape(-1, P, T).transpose(1, 0, 2)).reshape(P, -1)
    a["xT"] = tok(f("x")[0])
    a["pT"] = np.stack([tok(f("p")[l, 0]) for l in range(2)])
    for l in range(2):
        for k, n in enumerate(("ffn1", "ffn2")):
            g, up = f(f"{n}_w_gate")[l], f(f"{n}_w_up")[l]
            both = np.concatenate([g.reshape(D, NF, 1, P), up.reshape(D, NF, 1, P)], axis=2).reshape(D, 2 * FF)
            a[f"gu_{l}_{k}"] = _units(both)
            a[f"down_{l}_{k}"] = _units(f(f"{n}_w_down")[l], P)
        a[f"pg_{l}"] = _units(f("w_ple_gate")[l])
        a[f"pp_{l}"] = _units(f("w_ple_proj")[l])
    w = f("w_in_ab")[0]
    order_a = [x for p in A_PAIRS for x in p]
    qa, ka, va, qb, kb, vb = np.split(w, [768, 1024, 1280, 2048, 2816], axis=1)
    a["in_ab"] = _units(np.concatenate([_heads(qa, order_a), qb, ka, kb], axis=1))
    a["v_ab"] = _units(np.concatenate([va, vb], axis=1))
    w = f("w_out_ab")[0]
    a["out_ab"] = _units(np.concatenate([w[x * HD:(x + 1) * HD] for x in order_a] + [w[768:]], axis=0))
    w = f("w_in_c")[0]
    a["in_c"], a["v_c"] = _units(w[:, :2048]), _units(w[:, 2048:])
    a["out_c"] = _units(f("w_out_c")[0])
    rpb = np.pad(f("rpb_c")[0], ((0, 0), (0, 0), (48, 48)))
    a["rpb"] = np.ascontiguousarray(np.stack([rpb[:, :, 63 - j:127 - j] for j in range(64)], axis=1)).reshape(16, 64, 960)
    a["ada"] = _units(f("w_ada_2")[0])
    order_n = [x for p in N_PAIRS for x in p]
    hq, hf, hi, hgt, nq, kc, vc, ks, vs, kw, vw, ng = np.split(
        f("w_in_2")[0], np.cumsum([512] * 5 + [128] * 6).tolist(), axis=1)
    a["in_2"] = _units(np.concatenate([hq, hf, hgt, _heads(nq, order_n), kc, vc, ks, kw], axis=1))
    a["tok_2"] = _units(np.concatenate([hi, vs, vw, np.pad(ng, ((0, 0), (0, 232)))], axis=1))
    a["cmp"] = np.stack([x for n in ("k", "v") for x in
                         f(f"cmp_w1_{n}_2")[0].reshape(2, 8, P, 256).transpose(0, 2, 1, 3).reshape(2, P, UNIT)])
    w = f("w_out_2")[0]
    a["out_2"] = _units(np.concatenate([w[:512]] + [w[512 + x * HD:512 + (x + 1) * HD] for x in order_n], axis=0))
    down = f("w_sh_dn_2")[0].reshape(2, P, 2, 512).transpose(2, 1, 0, 3).reshape(2, P, 1024)
    a["shared"] = np.concatenate([_units(f("w_sh_gu_2")[0]), np.pad(down, ((0, 0), (0, 0), (0, UNIT - 1024)))], axis=0)
    gu, dn = f("w_exp_gu_2")[0], f("w_exp_dn_2")[0]
    e = np.empty((N_EXP, 3, P, UNIT), np.float32)
    e[:, 0:2] = gu.reshape(N_EXP, KD, P, 2, 256).transpose(0, 3, 2, 1, 4).reshape(N_EXP, 2, P, UNIT)
    e[:, 2] = dn.reshape(N_EXP, 2, P, D).transpose(0, 2, 1, 3).reshape(N_EXP, P, UNIT)
    a["experts"] = e.reshape(3 * N_EXP, P, UNIT)
    gains = {"ffn1": "norm_ffn1", "mix": "norm_mix", "ffn2": "norm_ffn2", "ple": "norm_ple"}
    parts = []
    for n in NORMS:
        if n[-2] == "_":
            parts.append(_column(f(gains[n[:-2]])[int(n[-1])]))
        else:
            parts.append(_column({"first": f("norm_final"), "norm1": f("norm1_g_2")[0], "norm2": f("norm2_g_2")[0], "final": f("final_g_2")}[n]))
    parts += [_column(f("b_ada_2")[0]), _column(f("c_2")[0]), _column(f("hg_lb_logits_2")[0]), _column(f("hg_lb_logits_2")[1]),
              _column(f("hg_norm_g_2")[0]), _column(f("cmp_b1_k_2")[0]), _column(f("cmp_b1_v_2")[0]),
              np.tile(f("cmp_pos_k_2")[0].T, (2, 1)), np.tile(f("cmp_pos_v_2")[0].T, (2, 1)),
              np.broadcast_to(f("sink_a")[0], (P, 12)), np.broadcast_to(f("router_bias_2")[0], (P, N_EXP))]
    cols3 = lambda w: w.reshape(-1, P, w.shape[1]).transpose(1, 0, 2).reshape(P, -1)
    parts += [cols3(f("cmp_w2_k_2")[0]), cols3(f("cmp_w2_v_2")[0]), cols3(f("router_w_2")[0])]
    a["cols"] = np.concatenate(parts, axis=1)
    assert a["cols"].shape == (P, NCOL)
    return {k: np.ascontiguousarray(v, dtype=v.dtype) for k, v in a.items()}


def _program(nc, arrays, stop_at=None):
    dr = {n: nc.dram_tensor(f"in_{n}", a.shape, F32, kind="ExternalInput").ap() for n, a in arrays.items()}
    dr["wt"] = nc.dram_tensor("expert_weights", [N_EXP, T], F32, kind="Internal").ap()
    out = nc.dram_tensor("out_0", [P, KD * T], F32, kind="ExternalOutput").ap()
    block_kernel(nc, dr, out, stop_at)


def kernel(**inputs):
    import concourse.bacc as bacc
    from concourse.bass_utils import run_bass_kernel_spmd
    arrays = _lay_out(inputs)
    nc = bacc.Bacc("TRN2", target_bir_lowering=False, num_devices=1)
    _program(nc, arrays)
    r = run_bass_kernel_spmd(nc, [{f"in_{n}": a for n, a in arrays.items()}], core_ids=[0])
    y = r.results[0]["out_0"].reshape(P, KD, T)
    return np.ascontiguousarray(y.transpose(2, 1, 0)).reshape(1, T, D)
```

```python
from contextlib import ExitStack, contextmanager

import numpy as np

import concourse.bass as bass
from concourse import mybir

ALU = mybir.AluOpType
ACT = mybir.ActivationFunctionType
AX = mybir.AxisListType
F32 = mybir.dt.float32
F32R = mybir.dt.float32r
I32 = mybir.dt.int32

P = 128
T = 512
TT = T // P
D = 1024
KD = D // P
FF = 2816
NF = FF // P
HD = 64
NEG = -1e30
EPS = 1e-6
UNIT = KD * 256
SLOT = max(UNIT, NF * P)
N_EXP = 64
EXP_H = 256
TOP_K = 8
MAX_BLOCKS = T * TOP_K // P + N_EXP
NS = 3
SCMAX = 384 + 512 + 512
ROUTED_SCALE = 2.5
HG_SCALE = 128 ** -0.5
N_CMP = (T - 32) // 16 + 1
GELU_C = 2.0 * (2.0 / np.pi) ** 0.5

A_PAIRS = [(0, 3), (1, 4), (2, 5), (6, 9), (7, 10), (8, 11)]
N_PAIRS = [(0, 4), (1, 5), (2, 6), (3, 7)]

NORMS = ["ffn1_0", "mix_0", "ffn2_0", "ple_0", "ffn1_1", "mix_1", "ffn2_1", "ple_1", "first", "norm1", "norm2", "final"]
COLS = {}
_at = 0
for _name, _n in ([(f"g_{n}", KD) for n in NORMS] + [
        ("b_ada", 48), ("c", KD), ("lb", 8), ("hg_g", 4), ("b1k", 2), ("b1v", 2), ("pe_k", 32), ("pe_v", 32),
        ("sink", 12), ("router_bias", N_EXP), ("w2k", 128), ("w2v", 128), ("router_w", KD * N_EXP)]):
    COLS[_name] = (_at, _n)
    _at += _n
NCOL = _at

PHASES = []
for _l in range(2):
    PHASES += [(f"gu_{_l}_0", NF), (f"down_{_l}_0", KD)]
    PHASES += [("in_ab", 10), ("v_ab", 4), ("out_ab", 4)] if _l == 0 else [("in_c", 8), ("v_c", 4), ("out_c", 4)]
    PHASES += [(f"gu_{_l}_1", NF), (f"down_{_l}_1", KD), (f"pg_{_l}", 4), (f"pp_{_l}", 4)]
PHASES += [("ada", 24), ("in_2", 10), ("tok_2", 4), ("cmp", 4), ("out_2", 4), ("shared", 4)]
BASE = {}
_at = 0
for _name, _n in PHASES:
    assert _n % 2 == 0
    BASE[_name] = (_at, _n)
    _at += _n


def unit_floats(phase):
    if phase.startswith("down"):
        return NF * P
    return 2 * 256 if phase.startswith("pp") else UNIT


class Chain:

    def __init__(self, eng, sem):
        self.eng, self.sem, self.n, self.turn = eng, sem, 0, None

    def __call__(self, ins):
        ins.then_inc(self.sem, 1)
        self.n += 1
        self.eng.wait_ge(self.sem, self.n if self.turn is None else self.turn + self.n)

    @contextmanager
    def loop(self, turns, per):
        if turns == 1:
            yield 0
            return
        start = self.n
        with self.eng.Fori(0, turns) as i:
            self.turn = i * per
            yield i
            assert self.n == start + per, (self.n - start, per)
            self.turn = None
        self.n += per * (turns - 1)


def block_kernel(nc, dr, out, stop_at=None):
    with ExitStack() as ctx:
        def sb(name, n):
            return ctx.enter_context(nc.sbuf_tensor(name, [P, n], F32))

        def sem(name):
            return ctx.enter_context(nc.semaphore(name))

        def tiles(ap, n):
            return ap.rearrange("p (a n) -> p a n", n=n)

        h_buf = sb("h_buf", KD * T)
        xn_buf = sb("xn_buf", KD * T)
        ring_buf = sb("ring_buf", 2 * SLOT)
        big = sb("big", 16384)
        with ExitStack() as overlay:
            o_hi, o_lo, send = (overlay.enter_context(nc.sbuf_tensor(n, [P, w], F32R))
                                for n, w in (("o_hi", 2 * D), ("o_lo", 2 * D), ("send", 2 * T)))
        s_buf = sb("s_buf", NS * SCMAX)
        pt_buf = sb("pt_buf", 2 * SCMAX)
        mixed_buf = sb("mixed_buf", KD * T)
        mask = sb("mask", 3072)
        rot = sb("rot", 2 * T)
        eye = sb("eye", P)
        ones = sb("ones", P)
        eps = sb("eps", 1)
        sq_buf = sb("sq_buf", 2 * T)
        sil_buf = sb("sil_buf", 2 * T)
        std = sb("std", T)
        rstd = sb("rstd", T)
        tmp_buf = sb("tmp_buf", 2 * T)
        diag_buf = sb("diag_buf", 6 * P)
        small = sb("small", 512)
        cols = sb("cols", NCOL)
        mod = sb("mod", 64)
        ps_t = ctx.enter_context(nc.psum_tensor("ps", [P, 8 * T], F32))

        h, xn, mixed = tiles(h_buf[:, :], T), tiles(xn_buf[:, :], T), tiles(mixed_buf[:, :], T)
        ring = [ring_buf[:, s * SLOT:(s + 1) * SLOT] for s in range(2)]
        sq, sil, tmp = tiles(sq_buf[:, :], T), tiles(sil_buf[:, :], T), tiles(tmp_buf[:, :], T)
        diag = tiles(diag_buf[:, :], P)
        ps = tiles(ps_t[:, :], T)
        hid = tiles(big[:, 0:NF * T], T)
        cos, sin = rot[:, 0:T], rot[:, T:2 * T]

        def col(name):
            a, n = COLS[name]
            return cols[:, a:a + n]

        consts_in = sem("consts_in")
        set_up = sem("set_up")
        loaded = [sem(f"loaded{s}") for s in range(2)]
        units_done = sem("units_done")
        evac_done = sem("evac_done")
        h_ready = sem("h_ready")
        sq_ready = sem("sq_ready")
        sq_used = sem("sq_used")
        std_ready = sem("std_ready")
        xn_ready = sem("xn_ready")
        sil_ready = sem("sil_ready")
        dve_own = sem("dve_own")
        act_own = sem("act_own")
        pool_own = sem("pool_own")
        out_done = sem("out_done")

        block = ctx.enter_context(nc.Block())

        NORM_N = {n: k for k, n in enumerate(NORMS)}
        H_STAGES = ["ffn1_0", "mix_0", "ffn2_0", "ple_0", "ffn1_1", "mix_1", "ffn2_1", "ple_1", "first", "mix_2", "moe"]
        H_AT = {n: KD * (k + 1) for k, n in enumerate(H_STAGES)}
        NORM_H = {"ffn1_0": 0, "mix_0": 8, "ffn2_0": 16, "ple_0": 24, "ffn1_1": 32, "mix_1": 40, "ffn2_1": 48,
                  "ple_1": 56, "first": 64, "norm1": 72, "norm2": 80, "final": 88}
        SIL_AT = {}
        at = 0
        for name, n in PHASES:
            if name.startswith("gu"):
                SIL_AT[name] = at
                at += n
        SIL_MOE = at

        def plan_a():
            q, kk = tiles(big[:, 0:12 * T], T), tiles(big[:, 12 * T:20 * T], T)
            v = tiles(big[:, 20 * T:20 * T + 4 * D], D)
            units = []
            for p in range(6):
                for hf in range(2):
                    r = slice(64 * hf, 64 * hf + 64)
                    for t in range(TT):
                        lo, hi = max(t - 1, 0), min(t + 2, TT)
                        n = (hi - lo) * P
                        a = (lo - t + 1) * P
                        kv = 2 * (p // 3) + hf
                        units.append(dict(
                            segs=[(q[r, p, t * P:t * P + P], kk[r, p // 3, lo * P:hi * P], mask[:, a:a + n], 0, n)],
                            groups=[(0, n)], sink=A_PAIRS[p][hf],
                            chunks=[(0, c * P, P, v[:, lo + c, kv * HD:kv * HD + HD]) for c in range(hi - lo)],
                            pair=p, out=p, half=hf, t=t, last=hf == 1 and t == TT - 1, first=hf == 0 and t == 0))
            return units

        def plan_b():
            q, kk = tiles(big[:, 0:12 * T], T), tiles(big[:, 12 * T:20 * T], T)
            v = tiles(big[:, 20 * T:20 * T + 4 * D], D)
            units = []
            for p in range(2):
                for hf in range(2):
                    r = slice(64 * hf, 64 * hf + 64)
                    for t in range(TT):
                        segs, chunks, at = [], [], 0
                        for g in range(3):
                            lo, hi = (max(t - 1, 0), min(t + 2, TT)) if g == 0 else (0, TT)
                            n = (hi - lo) * P
                            m0 = 384 + (lo - t + 1) * P if g == 0 else 768 + 896 * (g - 1) + 384 - t * P
                            segs.append((q[r, 6 + 2 * g + p, t * P:t * P + P], kk[r, 2 + 2 * g + p, lo * P:hi * P],
                                         mask[:, m0:m0 + n], at, n))
                            c0 = 256 + (4 * g + 2 * p + hf) * HD
                            chunks += [(0, at + c * P, P, v[:, lo + c, c0:c0 + HD]) for c in range(hi - lo)]
                            at += n
                        units.append(dict(segs=segs, groups=[(0, at)], sink=None, chunks=chunks, pair=p, out=6 + p,
                                          half=hf, t=t, last=hf == 1 and t == TT - 1, first=hf == 0 and t == 0))
            return units

        def plan_c():
            q, kk = tiles(big[:, 0:8 * T], T), tiles(big[:, 8 * T:16 * T], T)
            v = tiles(big[:, 16 * T:16 * T + 4 * D], D)
            units = []
            for p in range(8):
                for hf in range(2):
                    r = slice(64 * hf, 64 * hf + 64)
                    for t in range(TT):
                        a = 64 + 1024 * hf + (7 - 2 * t) * 64
                        units.append(dict(
                            segs=[(q[r, p, t * P:t * P + P], kk[r, p, :], mask[:, a:a + T], 0, T)],
                            groups=[(0, T)], sink=None,
                            chunks=[(0, c * P, P, v[:, c, (2 * p + hf) * HD:(2 * p + hf) * HD + HD]) for c in range(TT)],
                            pair=p, out=p, half=hf, t=t, last=hf == 1 and t == TT - 1, first=hf == 0 and t == 0))
            return units

        R_HQ, R_HF, R_HG = 0, 4 * T, 8 * T
        R_NQ, R_NR, R_KCV, R_KSW = 12 * T, 16 * T, 20 * T, 22 * T
        R_VI = 24 * T
        R_VSW = R_VI + TT * T
        R_GATE = R_VSW + TT * 256
        R_KCMP = R_GATE + TT * 24
        R_VCMP = R_KCMP + 32
        gates = tiles(big[:, R_GATE:R_GATE + TT * 24], 24)
        kcmp = big[:, R_KCMP:R_KCMP + 32]
        vcmp = tiles(big[:, R_VCMP:R_VCMP + 2 * HD], HD)

        def plan_n():
            q, qr = tiles(big[:, R_NQ:R_NR], T), tiles(big[:, R_NR:R_KCV], T)
            kk = tiles(big[:, R_KSW:R_VI], T)
            v = tiles(big[:, R_VSW:R_GATE], 256)
            units = []
            for p in range(4):
                for hf in range(2):
                    r = slice(64 * hf, 64 * hf + 64)
                    for t in range(TT):
                        n = (t + 1) * P
                        segs = [(qr[r, p, t * P:t * P + P], kk[r, 0, 0:n], mask[:, 384 - t * P:512], 0, n),
                                (qr[r, p, t * P:t * P + P], kk[r, 1, 0:n], mask[:, 384 - t * P:512], n, n),
                                (q[r, p, t * P:t * P + P], kcmp[r, :], mask[:, 512 + 32 * t:544 + 32 * t], 2 * n, 32)]
                        chunks = [(g, g * n + c * P, P, v[:, c, g * P + hf * HD:g * P + hf * HD + HD])
                                  for g in range(2) for c in range(t + 1)]
                        chunks.append((2, 2 * n, 32, vcmp[0:32, hf, :]))
                        units.append(dict(segs=segs, groups=[(0, n), (n, n), (2 * n, 32)], sink=None, chunks=chunks,
                                          gate=3 * N_PAIRS[p][hf], pair=p, out=4 + p, half=hf, t=t,
                                          last=hf == 1 and t == TT - 1, first=hf == 0 and t == 0))
            return units

        ATT = {}
        for name, units, sc_banks, pt_banks in (("a", plan_a(), (0, 1, 2), (3, 4)), ("b", plan_b(), (0,), (3,)),
                                                ("c", plan_c(), (0, 1, 2), (3, 4)), ("n", plan_n(), (0,), (3,))):
            ATT[name] = dict(
                units=units, sc=sc_banks, pt=pt_banks,
                mask_in=sem(f"{name}_mask_in"),
                qkv=sem(f"{name}_qkv"),
                sc_ready=sem(f"{name}_sc_ready"),
                sc_read=sem(f"{name}_sc_read"),
                negm=sem(f"{name}_negm"),
                exps=sem(f"{name}_exps"),
                fac=sem(f"{name}_fac"),
                diag=sem(f"{name}_diag"),
                pt_ready=sem(f"{name}_pt_ready"),
                pts=sem(f"{name}_pts"),
                pv=sem(f"{name}_pv"),
                out=sem(f"{name}_out"),
            )
        c_bias_in = [sem(f"c_bias_in{s}") for s in range(2)]
        c_bias = [sem(f"c_bias{s}") for s in range(2)]
        mx = small[:, 0:8]
        negm = small[:, 8:16]
        den = small[:, 16:24]
        es = small[:, 24:26]
        fac = small[:, 32:40]
        rden = small[:, 40:48]

        p_in = sem("p_in")
        hg = {n: sem(f"hg_{n}") for n in ("mask_in", "sig", "ln_in", "ln", "cum", "diff", "e", "ql", "kl", "qk", "mul", "acc",
                                          "ex_in", "ex", "kx", "x_ps", "x_sb", "o_ps", "o_sq", "o_sum", "o_std", "o_out", "lbe")}
        cm = {n: sem(f"cm_{n}") for n in ("blk", "h1", "g1", "th", "hid", "kv", "kv_sb")}
        rt = {n: sem(f"rt_{n}") for n in ("lg", "sig", "w", "wt_ps", "wt_sb", "wt_out", "ada_c", "gate")}
        moe = {n: sem(f"moe_{n}") for n in ("sil", "hid", "dn", "acc")}
        tab = {n: sem(f"tab_{n}") for n in (
            "const_in",
            "tok_ps", "tok_sb", "tok_out",
            "sel", "rank",
            "zero", "clear", "pairs", "filled", "in", "blocks", "blocks_out", "ready")}
        gathered = [sem(f"gathered{s}") for s in range(2)]
        gu_in = [sem(f"gu_in{s}") for s in range(2)]
        dn_in = [sem(f"dn_in{s}") for s in range(2)]
        bk = {n: sem(f"bk_{n}") for n in (
            "staged",
            "asked",
            "tx", "xt",
            "gu",
            "sil", "hid",
            "ht", "hts",
            "dn",
            "oh", "ol",
            "sum",
            "added")}
        w_gu = [big[:, s * 4096:(s + 1) * 4096].rearrange("p (k n) -> p k n", n=2 * EXP_H) for s in range(2)]
        w_dn = [big[:, 8192 + s * 2048:8192 + (s + 1) * 2048].rearrange("p (k n) -> p k n", n=D) for s in range(2)]
        xg = [big[:, 12288 + s * D:12288 + (s + 1) * D] for s in range(2)]
        xgt = [tiles(big[:, 14336 + s * D:14336 + (s + 1) * D], P) for s in range(2)]
        tok = big[:, 12288:16384].rearrange("p (t n) -> p t n", n=D)
        hid_b = [ring_buf[:, s * EXP_H:(s + 1) * EXP_H] for s in range(2)]
        hid_t = [tiles(ring_buf[:, 512 + s * EXP_H:512 + (s + 1) * EXP_H], P) for s in range(2)]
        sil_b = [ring_buf[:, 1024 + s * EXP_H:1024 + (s + 1) * EXP_H] for s in range(2)]
        place, pay = s_buf[:, 3456:3488].bitcast(I32), s_buf[:, 3392:3456]
        before, iota_t = mask[:, 0:P], mask[:, P:P + T]
        iota_e2 = mask[:, 640:704]
        slot_no, tok_no = mask[:, 704:705], mask[:, 705:709]
        tab_sb = mask[:, 1024:1024 + 2 * MAX_BLOCKS + 8].rearrange("p (b c) -> p b c", c=2)
        tab_f = mask[:, 1280:1280 + MAX_BLOCKS + 4]
        idx = mask[:, 1400:1402].bitcast(I32)
        n_turns = mask[:, 1404:1405].bitcast(I32)
        block_e = mask[:, 1405:1406].bitcast(I32)

        def u(phase):
            return BASE[phase][0]

        X_PAIRS = [(a, b) for a in range(TT) for b in range(a + 1, TT)]

        STAGES = ["ffn1_0", "mix_0", "ffn2_0", "ple_0", "ffn1_1", "mix_1", "ffn2_1", "ple_1", "mix_2", "moe"]
        if stop_at is not None:
            STAGES = STAGES[:STAGES.index(stop_at) + 1]

        @block.sync
        def _(sp):
            sp.dma_start(h_buf[:, :], dr["xT"]).then_inc(consts_in, 16)

            def load(phase, turn, s):
                n = unit_floats(phase)
                sp.dma_start(ring[s][:, 0:n], dr[phase][bass.ds(2 * turn + s, 1), :, :].rearrange("a p n -> p (a n)")
                             ).then_inc(loaded[s], 16)

            def stream(phase):
                base, n = BASE[phase]
                for s in range(2):
                    if base:
                        sp.wait_ge(units_done, base + s - 1)
                    load(phase, 0, s)
                if n > 2:
                    with sp.Fori(1, n // 2) as i:
                        for s in range(2):
                            sp.wait_ge(units_done, i * 2 + (base + s - 1))
                            load(phase, i, s)

            def att_mask(name, ap, n, after=None):
                if after is not None:
                    sp.wait_ge(*after)
                sp.dma_start(mask[:, 0:n], dr[ap]).then_inc(ATT[name]["mask_in"], 16)

            for st in STAGES:
                if st.startswith("ffn"):
                    l, k = st[-1], int(st[3]) - 1
                    stream(f"gu_{l}_{k}")
                    stream(f"down_{l}_{k}")
                elif st.startswith("ple"):
                    l = st[-1]
                    sp.wait_ge(h_ready, NORM_H[f"ple_{l}"])
                    sp.dma_start(big[:, 8 * T:10 * T], dr["pT"][int(l), :, :]).then_inc(p_in, 16)
                    stream(f"pg_{l}")
                    stream(f"pp_{l}")
                elif st == "mix_0":
                    att_mask("a", "mask_ab", 2560)
                    stream("in_ab")
                    stream("v_ab")
                    stream("out_ab")
                elif st == "mix_1":
                    att_mask("c", "mask_c", 64, (h_ready, H_AT["mix_0"]))
                    stream("in_c")
                    stream("v_c")
                    for hd in range(16):
                        if hd >= 2:
                            sp.wait_ge(ATT["c"]["sc_read"], TT * (hd - 1))
                        b = 64 + 1024 * (hd % 2)
                        for r in range(2):
                            sp.dma_start(mask[64 * r:64 * r + 64, b + 64 * r:b + 64 * r + 960],
                                         dr["rpb"][hd, :, :]).then_inc(c_bias_in[hd % 2], 16)
                    stream("out_c")
                elif st == "mix_2":
                    stream("ada")
                    stream("in_2")
                    stream("tok_2")
                    sp.wait_ge(h_ready, H_AT["mix_1"])
                    sp.dma_start(mask[:, 0:1024], dr["mask_h"]).then_inc(hg["mask_in"], 16)
                    stream("cmp")
                    att_mask("n", "mask_n", 641, (hg["o_out"], 4))
                    stream("out_2")
                elif st == "moe":
                    stream("shared")
                    sp.wait_ge(h_ready, H_AT["mix_2"])
                    sp.dma_start(mask[:, 0:709], dr["mask_m"]).then_inc(tab["const_in"], 16)
                    sp.wait_ge(tab["tok_sb"], TT)
                    sp.dma_start(dr["tok"].rearrange("(t p) n -> p t n", p=P), tok).then_inc(tab["tok_out"], 16)
                    sp.wait_ge(tab["zero"], 1)
                    sp.dma_start(dr["table"].rearrange("(p b) c -> p (b c)", p=P), s_buf[:, 3584:3584 + 2 * MAX_BLOCKS + 8]
                                 ).then_inc(tab["clear"], 16)
                    sp.wait_ge(tab["filled"], 16 * TT * TOP_K)
                    sp.dma_start(mask[:, 1024:1024 + 2 * MAX_BLOCKS + 8], dr["table"].rearrange("(p b) c -> p (b c)", p=P)
                                 ).then_inc(tab["in"], 16)
                    sp.wait_ge(tab["blocks"], 1)
                    sp.dma_start(dr["block_e"].rearrange("a p -> p a"), block_e).then_inc(tab["blocks_out"], 16)
                    sp.wait_ge(tab["blocks_out"], 16)
                    turns = sp.value_load(n_turns[0:1, 0:1], min_val=1, max_val=MAX_BLOCKS // 2)

                    def load_gu(e, s):
                        sp.dma_start(big[:, s * 4096:(s + 1) * 4096],
                                     dr["exp_gu"][bass.ds(e, 1), :, :].rearrange("a p n -> p (a n)")).then_inc(gu_in[s], 16)

                    def expert_of(b):
                        return sp.value_load(dr["block_e"][0:1, b], min_val=0, max_val=N_EXP - 1)

                    sp.wait_ge(tab["tok_out"], 16)
                    load_gu(expert_of(slice(0, 1)), 0)
                    with sp.Fori(0, turns) as i:
                        for s in range(2):
                            now, then = expert_of(bass.ds(i * 2 + s, 1)), expert_of(bass.ds(i * 2 + (s + 1), 1))
                            sp.wait_ge(bk["gu"], i * 2 + (s + 1))
                            load_gu(then, 1 - s)
                            sp.wait_ge(bk["dn"], i * 2 + (s + 1))
                            sp.dma_start(big[:, 8192 + s * 2048:8192 + (s + 1) * 2048],
                                         dr["exp_dn"][bass.ds(now, 1), :, :].rearrange(
                                             "a p n -> p (a n)")).then_inc(dn_in[s], 16)
            if stop_at is None:
                sp.wait_ge(xn_ready, KD * len(NORMS))
                sp.dma_start(out, xn_buf[:, :]).then_inc(out_done, 16)
            else:
                sp.wait_ge(h_ready, H_AT[stop_at])
                sp.dma_start(out, h_buf[:, :]).then_inc(out_done, 16)
            sp.wait_ge(out_done, 16)

        @block.tensor
        def _(pe):
            pe.wait_ge(set_up, 1)
            pe.wait_ge(consts_in, 16 * 4)

            def unit_waits(turn, U, s):
                pe.wait_ge(loaded[s], turn * 16 + 16 * (U // 2 + 1))
                pe.wait_ge(evac_done, turn * 2 + (U + 1))

            @contextmanager
            def turns(n):
                if n == 1:
                    yield 0
                else:
                    with pe.Fori(0, n) as i:
                        yield i

            def norm_sum(name):
                n = NORM_N[name] * KD
                for k in range(KD):
                    pe.wait_ge(sq_ready, n + k + 1)
                    nc.tensor.matmul(ps[:, 7, :], ones[:, :], sq[:, k % 2, :], start=(k == 0), stop=(k == KD - 1)
                                     ).then_inc(sq_used, 1)

            def dense(phase, rhs, n=T, kt=KD):
                U, units = BASE[phase]
                with turns(units // 2) as i:
                    for s in range(2):
                        unit_waits(i, U + s, s)
                        w = tiles(ring[s][:, 0:kt * 256], 256)
                        for j in range(2):
                            for k in range(kt):
                                last = nc.tensor.matmul(ps[:, 2 * s + j, 0:n], w[:, k, j * P:j * P + P], rhs(k),
                                                        start=(k == 0), stop=(k == kt - 1))
                        last.then_inc(units_done, 1)

            def token_major(phase, first=0, units=None, width=256):
                U = u(phase) + first
                with turns((units or BASE[phase][1]) // 2) as i:
                    for s in range(2):
                        unit_waits(i, U + s, s)
                        w = tiles(ring[s][:, 0:UNIT], 256)
                        for t in range(TT):
                            for k in range(KD):
                                last = nc.tensor.matmul(ps[:, 2 * s + t // 2, 256 * (t % 2):256 * (t % 2) + 256],
                                                        xn[:, k, t * P:t * P + P], w[:, k, :],
                                                        start=(k == 0), stop=(k == KD - 1))
                        last.then_inc(units_done, 1)

            def xn_rhs(k):
                return xn[:, k, :]

            def ffn(st):
                l, k = st[-1], int(st[3]) - 1
                norm_sum(st)
                pe.wait_ge(xn_ready, KD * (NORM_N[st] + 1))
                dense(f"gu_{l}_{k}", xn_rhs)
                U, n = BASE[f"down_{l}_{k}"]
                pe.wait_ge(evac_done, U + 2)
                with turns(n // 2) as i:
                    for s in range(2):
                        unit_waits(i, U + s, s)
                        w = tiles(ring[s][:, 0:NF * P], P)
                        for f in range(NF):
                            last = nc.tensor.matmul(ps[:, 2 * s, :], w[:, f, :], hid[:, f, :],
                                                    start=(f == 0), stop=(f == NF - 1))
                        last.then_inc(units_done, 1)

            def attention(name):
                a = ATT[name]
                units, ns, np_ = a["units"], len(a["sc"]), len(a["pt"])
                pe.wait_ge(a["qkv"], 1)
                for i in range(len(units) + 3):
                    if i < len(units):
                        if i >= ns:
                            pe.wait_ge(a["sc_read"], i - ns + 1)
                        for g, (q, kk, _, _, n) in enumerate(units[i]["segs"]):
                            last = nc.tensor.matmul(ps[:, a["sc"][i % ns] + g, 0:n], q, kk, start=True, stop=True)
                        last.then_inc(a["sc_ready"], 1)
                    if 2 <= i <= len(units) + 1:
                        j = i - 2
                        un = units[j]
                        pe.wait_ge(a["diag"], j + 1)
                        if j >= np_:
                            pe.wait_ge(a["pts"], j - np_ + 1)
                        for c, (g, c0, n, _) in enumerate(un["chunks"]):
                            b = a["pt"][j % np_] + c // 4
                            last = nc.tensor.matmul(ps[0:n, b, (c % 4) * P:(c % 4) * P + P],
                                                    s_buf[:, (j % NS) * SCMAX + c0:(j % NS) * SCMAX + c0 + n],
                                                    diag[:, 3 * (j % 2) + g, :], start=True, stop=True)
                        last.then_inc(a["pt_ready"], 1)
                    if i >= 3:
                        j = i - 3
                        un = units[j]
                        pe.wait_ge(a["pts"], j + 1)
                        if un["first"] and un["pair"] >= 2:
                            pe.wait_ge(a["out"], un["pair"] - 1)
                        o = ps[64 * un["half"]:64 * un["half"] + 64, 6 + un["pair"] % 2, un["t"] * P:un["t"] * P + P]
                        for c, (_, _, n, v) in enumerate(un["chunks"]):
                            b0 = (j % 2) * SCMAX + c * P
                            last = nc.tensor.matmul(o, v, pt_buf[0:n, b0:b0 + P],
                                                    start=(c == 0), stop=(c == len(un["chunks"]) - 1))
                        last.then_inc(a["pv"], 1)

            def project_out(phase, ready):
                pe.wait_ge(*ready)
                dense(phase, lambda k: mixed[:, k, :])

            def hgrn():
                q, kk = tiles(big[:, R_HQ:R_HF], T), tiles(big[:, R_HF:R_HG], T)
                v = tiles(big[:, R_VI:R_VSW], T)
                for hd in range(4):
                    for lv in range(8):
                        i = 8 * hd + lv
                        if lv < 7:
                            pe.wait_ge(hg["ql"], 7 * hd + lv + 1)
                            pe.wait_ge(hg["kl"], 7 * hd + lv + 1)
                        if i >= 2:
                            pe.wait_ge(hg["mul"], i - 1)
                        for t in range(TT):
                            if lv == 7:
                                kl, ql = kk[:, hd, t * P:t * P + P], q[:, hd, t * P:t * P + P]
                            else:
                                kl = s_buf[:, (i % 2) * T + t * P:(i % 2) * T + t * P + P]
                                ql = s_buf[:, (2 + i % 2) * T + t * P:(2 + i % 2) * T + t * P + P]
                            last = nc.tensor.matmul(ps[:, i % 2, t * P:t * P + P], kl, ql, start=True, stop=True)
                        last.then_inc(hg["qk"], 1)
                    pe.wait_ge(hg["kx"], hd + 1)
                    for n, (a, b) in enumerate(X_PAIRS):
                        kx = pt_buf[:, (b - a) * T + a * P:(b - a) * T + a * P + P]
                        last = nc.tensor.matmul(ps[:, 2 + n // 4, (n % 4) * P:(n % 4) * P + P], kx,
                                                pt_buf[:, b * P:b * P + P], start=True, stop=True)
                    last.then_inc(hg["x_ps"], 1)
                    pe.wait_ge(hg["x_sb"], hd + 1)
                    pe.wait_ge(hg["acc"], 8 * (hd + 1))
                    if hd >= 1:
                        pe.wait_ge(hg["o_out"], hd)
                    for b in range(TT):
                        for a in range(b + 1):
                            if a == b:
                                at = xn_buf[:, b * P:b * P + P]
                            else:
                                n = X_PAIRS.index((a, b))
                                at = xn_buf[:, T + n * P:T + n * P + P]
                            last = nc.tensor.matmul(ps[:, 4, b * P:b * P + P], v[:, a, hd * P:hd * P + P], at,
                                                    start=(a == 0), stop=(a == b))
                    last.then_inc(hg["o_ps"], 1)
                    pe.wait_ge(hg["o_sq"], hd + 1)
                    nc.tensor.matmul(ps[:, 5, :], ones[:, :], sq[:, 0, :], start=True, stop=True
                                     ).then_inc(hg["o_sum"], 1)

            def compress():
                U = u("cmp")
                for kv in range(2):
                    pe.wait_ge(cm["blk"], kv + 1)
                    blk = s_buf[:, kv * 1024:kv * 1024 + 992].rearrange("p (l n) -> p l n", l=16)
                    for s in range(2):
                        pe.wait_ge(loaded[s], 16 * (U // 2 + kv + 1))
                        pe.wait_ge(evac_done, U + 2 * kv + s + 1)
                        w = tiles(ring[s][:, 0:UNIT], 256)
                        for l in range(8):
                            for j in range(2):
                                last = nc.tensor.matmul(ps[:, 2 * kv + j, 0:62], w[:, l, j * P:j * P + P],
                                                        blk[:, 8 * s + l, :], start=(s == 0 and l == 0),
                                                        stop=(s == 1 and l == 7))
                        last.then_inc(units_done, 1)
                for kv in range(2):
                    pe.wait_ge(cm["hid"], kv + 1)
                    w2 = tiles(col("w2k" if kv == 0 else "w2v"), HD)
                    hb = s_buf[:, 2048 + kv * 128:2048 + kv * 128 + 124].rearrange("p (j n) -> p j n", j=2)
                    for g in range(2):
                        for j in range(2):
                            if kv == 0:
                                o, a, b = ps[64 * g:64 * g + 64, 4, 0:N_CMP], w2[:, j, :], hb[:, j, g * 31:g * 31 + 31]
                            else:
                                o, a, b = ps[0:N_CMP, 5, g * HD:g * HD + HD], hb[:, j, g * 31:g * 31 + 31], w2[:, j, :]
                            last = nc.tensor.matmul(o, a, b, start=(j == 0), stop=(j == 1))
                    last.then_inc(cm["kv"], 1)

            def router():
                for t in range(TT):
                    for k in range(KD):
                        last = nc.tensor.matmul(ps[:, 4, t * N_EXP:(t + 1) * N_EXP], xn[:, k, t * P:t * P + P],
                                                tiles(col("router_w"), N_EXP)[:, k, :], start=(k == 0), stop=(k == KD - 1))
                last.then_inc(rt["lg"], 1)

            def token_major_tokens():
                for t in range(TT):
                    if t >= 2:
                        pe.wait_ge(tab["tok_sb"], t - 1)
                    for k in range(KD):
                        last = nc.tensor.transpose(ps[:, 2 * (t % 2) + k // 4, (k % 4) * P:(k % 4) * P + P],
                                                   xn[:, k, t * P:t * P + P], eye[:, :])
                    last.then_inc(tab["tok_ps"], 1)

            def ranks():
                pe.wait_ge(tab["sel"], 1)
                pe.wait_ge(tab["const_in"], 16)
                sel = tiles(s_buf[:, 2560:2816], N_EXP)
                for t in range(TT):
                    for a in range(t + 1):
                        nc.tensor.matmul(ps[:, 5, t * N_EXP:(t + 1) * N_EXP], before if a == t else ones[:, :], sel[:, a, :],
                                         start=(a == 0), stop=(a == t))
                for a in range(TT):
                    last = nc.tensor.matmul(ps[:, 5, TT * N_EXP:(TT + 1) * N_EXP], ones[:, :], sel[:, a, :],
                                            start=(a == 0), stop=(a == TT - 1))
                last.then_inc(tab["rank"], 1)

            def turn_tokens(s, n):
                pe.wait_ge(gathered[s], n[0])
                if n[1] is not None:
                    pe.wait_ge(bk["xt"], n[1])
                for k in range(KD):
                    last = nc.tensor.transpose(ps[:, k // 4, (k % 4) * P:(k % 4) * P + P], xg[s][:, k * P:k * P + P], eye[:, :])
                last.then_inc(bk["tx"], 1)

            def gate_up(s, n):
                pe.wait_ge(gu_in[s], n[0])
                pe.wait_ge(bk["xt"], n[1])
                for k in range(KD):
                    last = nc.tensor.matmul(ps[:, 2, :], xgt[s][:, k, :], w_gu[s][:, k, :], start=(k == 0), stop=(k == KD - 1))
                last.then_inc(bk["gu"], 1)

            def send_two(i):
                pe.wait_ge(bk["ol"], i * 2 + 1)
                for m in range(KD):
                    pe.wait_ge(bk["added"], i * KD + (m + 1))
                    n = 0
                    for s in range(2):
                        for part in (o_hi, o_lo):
                            last = nc.tensor.matmul(ps[:, 6 + m % 2, :], part[:, s * D + m * P:s * D + m * P + P],
                                                    send[:, s * T:(s + 1) * T], start=(n == 0), stop=(n == 3))
                            n += 1
                    last.then_inc(bk["sum"], 1)

            def routed():
                pe.wait_ge(tab["ready"], 1)
                turns_n = pe.value_load(n_turns[0:1, 0:1], min_val=1, max_val=MAX_BLOCKS // 2)
                pe.sem_inc(bk["gu"], 1)
                pe.sem_inc(bk["dn"], 2)
                turn_tokens(0, (16, None))
                turn_tokens(1, (16, 1))
                gate_up(0, (16, 1))
                with pe.Fori(0, turns_n) as i:
                    for s in range(2):
                        pe.wait_ge(bk["hid"], i * 2 + (s + 1))
                        for j in range(2):
                            last = nc.tensor.transpose(ps[:, 3, j * P:j * P + P], hid_b[s][:, j * P:j * P + P], eye[:, :])
                        last.then_inc(bk["ht"], 1)
                        gate_up(1 - s, (i * 16 + 16 * (s + 1), i * 2 + (s + 2)))
                        turn_tokens(s, (i * 16 + 32, i * 2 + (s + 2)))
                        pe.wait_ge(bk["hts"], i * 2 + (s + 1))
                        pe.wait_ge(dn_in[s], i * 16 + 16)
                        pe.wait_ge(bk["ol"], i * 2 + (s + 1))
                        for n in range(2):
                            for j in range(2):
                                last = nc.tensor.matmul(ps[:, 4 + n, :], hid_t[s][:, j, :], w_dn[s][:, j, n * T:(n + 1) * T],
                                                        start=(j == 0), stop=(j == 1))
                        last.then_inc(bk["dn"], 1)
                        if s == 0:
                            send_two(i)
                send_two(turns_n)

            def expert_gu(turn, U, slots, n):
                for j in range(2):
                    s = slots[j]
                    pe.wait_ge(loaded[s], turn * 48 + 16 * ((U + j) // 2 + 1))
                    if j == 0 and n is not None:
                        pe.wait_ge(moe["hid"], n)
                    w = tiles(ring[s][:, 0:UNIT], 256)
                    for m in range(2):
                        for k in range(KD):
                            last = nc.tensor.matmul(ps[:, 2 * j + m, :], w[:, k, m * P:m * P + P], xn[:, k, :],
                                                    start=(k == 0), stop=(k == KD - 1))
                    last.then_inc(units_done, 1)

            def expert_dn(w, m, n, hbuf):
                if n is not None:
                    pe.wait_ge(moe["acc"], n)
                for k in range(2):
                    last = nc.tensor.matmul(ps[:, 4 + m % 4, :], w[:, k, :], hbuf[:, k, :], start=(k == 0), stop=(k == 1))
                last.then_inc(moe["dn"], 1)
                return last

            for st in STAGES:
                if st.startswith("ffn"):
                    ffn(st)
                elif st.startswith("ple"):
                    l = st[-1]
                    norm_sum(st)
                    pe.wait_ge(xn_ready, KD * (NORM_N[st] + 1))
                    dense(f"pg_{l}", xn_rhs)
                    pe.wait_ge(p_in, 16 * (int(l) + 1))
                    dense(f"pp_{l}", lambda k: big[:, (8 + k) * T:(9 + k) * T], kt=2)
                elif st == "mix_0":
                    norm_sum(st)
                    pe.wait_ge(xn_ready, KD * (NORM_N[st] + 1))
                    dense("in_ab", xn_rhs)
                    token_major("v_ab")
                    attention("a")
                    attention("b")
                    project_out("out_ab", (ATT["b"]["out"], 2))
                elif st == "mix_1":
                    norm_sum(st)
                    pe.wait_ge(xn_ready, KD * (NORM_N[st] + 1))
                    dense("in_c", xn_rhs)
                    token_major("v_c")
                    attention("c")
                    project_out("out_c", (ATT["c"]["out"], 8))
                elif st == "mix_2":
                    pe.wait_ge(rt["ada_c"], 1)
                    dense("ada", lambda k: mod[:, 56 + k:57 + k], n=1)
                    norm_sum("first")
                    norm_sum("norm1")
                    pe.wait_ge(xn_ready, KD * (NORM_N["norm1"] + 1))
                    dense("in_2", xn_rhs)
                    token_major("tok_2")
                    compress()
                    hgrn()
                    attention("n")
                    project_out("out_2", (ATT["n"]["out"], 4))
                elif st == "moe":
                    norm_sum("norm2")
                    pe.wait_ge(xn_ready, KD * (NORM_N["norm2"] + 1))
                    router()
                    token_major_tokens()
                    U = u("shared")
                    pe.wait_ge(evac_done, U + 2)
                    pe.wait_ge(tab["tok_sb"], TT)
                    expert_gu(0, U, (0, 1), None)
                    ranks()
                    hb = tiles(s_buf[:, 1536:2560], T)
                    pe.wait_ge(moe["hid"], 1)
                    for j in range(2):
                        pe.wait_ge(loaded[j], 16 * ((U + 2 + j) // 2 + 1))
                        for m in range(4):
                            w = ring[j][:, 0:1024].rearrange("p (k n) -> p k n", k=2)[:, :, m * P:m * P + P]
                            last = expert_dn(w, 4 * j + m, 4 * j + m - 3 if 4 * j + m >= 4 else None, hb)
                    pe.wait_ge(moe["acc"], KD)
                    routed()
                    norm_sum("final")


        @block.scalar
        def _(act):
            link = Chain(act, act_own)
            act.dma_start(cols[:, :], dr["cols"]).then_inc(consts_in, 16)
            act.dma_start(rot[:, :], dr["rot"]).then_inc(consts_in, 16)
            act.dma_start(eye[:, :], dr["eye"]).then_inc(consts_in, 16)
            act.wait_ge(consts_in, 64)
            act.wait_ge(set_up, 1)

            def norm(name):
                n = NORM_N[name] * KD
                if NORM_H[name]:
                    act.wait_ge(h_ready, NORM_H[name])
                for k in range(KD):
                    if n + k >= 2:
                        act.wait_ge(sq_used, n + k - 1)
                    nc.scalar.activation(sq[:, k % 2, :], h[:, k, :], ACT.Square).then_inc(sq_ready, 1)
                act.wait_ge(sq_used, n + KD)
                nc.scalar.activation(std[:, :], ps[:, 7, :], ACT.Sqrt, bias=eps[:, 0:1], scale=1.0 / D
                                     ).then_inc(std_ready, 1)

            def ffn(st):
                norm(st)
                phase = f"gu_{st[-1]}_{int(st[3]) - 1}"
                U, n = BASE[phase]
                with link.loop(n // 2, 0) as i:
                    for s in range(2):
                        act.wait_ge(units_done, i * 2 + (U + s + 1))
                        act.wait_ge(evac_done, i * 2 + (U + s + 1))
                        nc.scalar.activation(sil[:, s, :], ps[:, 2 * s, :], ACT.Silu).then_inc(sil_ready, 1)

            def attention(name):
                a = ATT[name]
                units, np_ = a["units"], len(a["pt"])
                for i in range(len(units) + 2):
                    if i < len(units):
                        un, b = units[i], i % 2
                        act.wait_ge(a["negm"], i + 1)
                        if i >= 2:
                            act.wait_ge(a["fac"], i - 1)
                        if un["sink"] is not None:
                            nc.scalar.activation(es[:, b:b + 1], negm[:, 4 * b:4 * b + 1], ACT.Exp,
                                                 bias=col("sink")[:, un["sink"]:un["sink"] + 1])
                        for g, (c0, n) in enumerate(un["groups"]):
                            p = s_buf[:, (i % NS) * SCMAX + c0:(i % NS) * SCMAX + c0 + n]
                            last = nc.scalar.activation(p, p, ACT.Exp, bias=negm[:, 4 * b + g:4 * b + g + 1],
                                                        accum_out=den[:, 4 * b + g:4 * b + g + 1])
                        last.then_inc(a["exps"], 1)
                    if i >= 2:
                        j = i - 2
                        un, b = units[j], j % 2
                        act.wait_ge(a["pt_ready"], j + 1)
                        if j >= 2:
                            act.wait_ge(a["pv"], j - 1)
                        full = sum(c[2] == P for c in un["chunks"])
                        bank = a["pt"][j % np_]
                        src = ps_t[:, bank * T:bank * T + full * P]
                        last = nc.scalar.activation(pt_buf[:, b * SCMAX:b * SCMAX + full * P], src, ACT.Copy)
                        if full < len(un["chunks"]):
                            n = un["chunks"][-1][2]
                            last = nc.scalar.activation(
                                pt_buf[0:n, b * SCMAX + full * P:b * SCMAX + full * P + P],
                                ps_t[0:n, bank * T + full * P:bank * T + full * P + P], ACT.Copy)
                        last.then_inc(a["pts"], 1)

            def hgrn():
                z = big[:, R_HF:R_HG]
                act.wait_ge(evac_done, u("in_2") + 2 + 6)
                nc.scalar.activation(z, z, ACT.Sigmoid).then_inc(hg["sig"], 1)
                nc.scalar.activation(big[:, R_HG:R_NQ], big[:, R_HG:R_NQ], ACT.Silu).then_inc(hg["sig"], 1)
                gt = big[:, R_GATE:R_GATE + TT * 24]
                act.wait_ge(evac_done, u("tok_2") + 2 + 4)
                link(nc.scalar.activation(gt, gt, ACT.Sigmoid))
                act.wait_ge(hg["ln_in"], 1)
                nc.scalar.activation(xn_buf[:, 4 * T:8 * T], z, ACT.Ln).then_inc(hg["ln"], 1)
                for hd in range(4):
                    for lv in range(7):
                        i = 7 * hd + lv
                        e = tmp[:, i % 2, :]
                        act.wait_ge(hg["diff"], i + 1)
                        link(nc.scalar.activation(e, e, ACT.Abs))
                        nc.scalar.activation(e, e, ACT.Exp, scale=-1.0).then_inc(hg["e"], 1)
                    b = xn_buf[:, (4 + hd) * T:(5 + hd) * T]
                    act.wait_ge(hg["ex_in"], hd + 1)
                    nc.scalar.activation(sil[:, 0, :], b, ACT.Exp)
                    for t in range(TT):
                        last = nc.scalar.activation(sil[:, 1, t * P:t * P + P], b[:, t * P:t * P + P], ACT.Exp, scale=-1.0,
                                                    bias=b[:, t * P + P - 1:t * P + P])
                    last.then_inc(hg["ex"], 1)
                    act.wait_ge(hg["o_ps"], hd + 1)
                    nc.scalar.activation(sq[:, 0, :], ps[:, 4, :], ACT.Square).then_inc(hg["o_sq"], 1)
                    act.wait_ge(hg["o_sum"], hd + 1)
                    nc.scalar.activation(std[:, :], ps[:, 5, :], ACT.Sqrt, bias=eps[:, 0:1], scale=1.0 / P
                                         ).then_inc(hg["o_std"], 1)

            for st in STAGES:
                if st.startswith("ffn"):
                    ffn(st)
                elif st.startswith("ple"):
                    norm(st)
                    U, n = BASE[f"pg_{st[-1]}"]
                    g = tiles(big[:, 0:8 * T], T)
                    for m in range(n):
                        act.wait_ge(units_done, U + m + 1)
                        for j in range(2):
                            last = nc.scalar.activation(g[:, 2 * m + j, :], ps[:, 2 * (m % 2) + j, :], ACT.Sigmoid)
                        last.then_inc(evac_done, 1)
                elif st == "mix_0":
                    norm(st)
                    attention("a")
                    attention("b")
                elif st == "mix_1":
                    norm(st)
                    attention("c")
                elif st == "mix_2":
                    nc.scalar.activation(mod[:, 56:64], col("c"), ACT.Silu).then_inc(rt["ada_c"], 1)
                    norm("first")
                    norm("norm1")
                    for kv in range(2):
                        act.wait_ge(cm["th"], kv + 1)
                        t3 = s_buf[:, 2304 + kv * 128:2304 + kv * 128 + 124]
                        nc.scalar.activation(t3, t3, ACT.Sigmoid, scale=GELU_C).then_inc(cm["g1"], 1)
                    act.wait_ge(hg["lbe"], 1)
                    nc.scalar.activation(small[:, 64:72], small[:, 64:72], ACT.Exp).then_inc(hg["lbe"], 1)
                    hgrn()
                    attention("n")
                elif st == "moe":
                    norm("norm2")
                    act.wait_ge(rt["lg"], 1)
                    nc.scalar.activation(s_buf[:, 0:256], ps[:, 4, 0:256], ACT.Sigmoid).then_inc(rt["sig"], 1)
                    for t in range(TT):
                        act.wait_ge(tab["tok_ps"], t + 1)
                        nc.scalar.activation(tok[:, t, :], ps_t[:, 2 * (t % 2) * T:2 * (t % 2) * T + D], ACT.Copy
                                             ).then_inc(tab["tok_sb"], 1)
                    U = u("shared")
                    act.wait_ge(units_done, U + 2)
                    for j in range(2):
                        last = nc.scalar.activation(sil[:, j, :], ps[:, j, :], ACT.Silu)
                    last.then_inc(moe["sil"], 1)
                    act.wait_ge(tab["ready"], 1)
                    turns_n = act.value_load(n_turns[0:1, 0:1], min_val=1, max_val=MAX_BLOCKS // 2)

                    def tokens(s, n, used):
                        act.wait_ge(bk["tx"], n)
                        if used is not None:
                            act.wait_ge(bk["gu"], used)
                        nc.scalar.activation(xgt[s], tiles(ps_t[:, 0:D], P), ACT.Copy).then_inc(bk["xt"], 1)

                    def silu(s, n):
                        act.wait_ge(bk["gu"], n)
                        nc.scalar.activation(sil_b[s], ps[:, 2, 0:EXP_H], ACT.Silu).then_inc(bk["sil"], 1)

                    tokens(0, 1, None)
                    tokens(1, 2, None)
                    silu(0, 2)
                    with act.Fori(0, turns_n) as i:
                        for s in range(2):
                            act.wait_ge(bk["ht"], i * 2 + (s + 1))
                            nc.scalar.activation(hid_t[s], tiles(ps[:, 3, 0:EXP_H], P), ACT.Copy).then_inc(bk["hts"], 1)
                            silu(1 - s, i * 2 + (s + 3))
                            tokens(s, i * 2 + (s + 3), i * 2 + (s + 2))
                            act.wait_ge(bk["dn"], i * 2 + (s + 3))
                            act.wait_ge(bk["sum"], i * KD + KD)
                            nc.scalar.activation(o_hi[:, s * D:(s + 1) * D], ps_t[:, 4 * T:4 * T + D], ACT.Copy
                                                 ).then_inc(bk["oh"], 1)
                    norm("final")

        @block.gpsimd
        def _(pool):
            link = Chain(pool, pool_own)
            link(nc.gpsimd.memset(ones[:, :], 1.0))
            nc.gpsimd.memset(eps[:, :], EPS).then_inc(set_up, 1)
            pool.wait_ge(consts_in, 64)

            def attention(name):
                a = ATT[name]
                for i, un in enumerate(a["units"]):
                    if name == "c":
                        hd = 2 * un["pair"] + un["half"]
                        if i == 0:
                            bias_mask(0)
                        if un["t"] == 1 and hd + 1 < 16:
                            bias_mask(hd + 1)
                    pool.wait_ge(a["fac"], i + 1)
                    if i >= 2:
                        pool.wait_ge(a["pt_ready"], i - 1)
                    for g in range(len(un["groups"])):
                        last = nc.gpsimd.tensor_scalar(diag[:, 3 * (i % 2) + g, :], eye[:, :],
                                                       fac[:, 4 * (i % 2) + g:4 * (i % 2) + g + 1], None, ALU.mult)
                    last.then_inc(a["diag"], 1)

            def bias_mask(hd):
                if hd == 0:
                    pool.wait_ge(ATT["c"]["mask_in"], 16)
                pool.wait_ge(c_bias_in[hd % 2], 32 * (hd // 2 + 1))
                a = 64 + 1024 * (hd % 2)
                b = mask[:, a:a + 1024].rearrange("p (a n) -> p a n", n=64)
                last = nc.gpsimd.tensor_tensor(b, b, mask[:, None, 0:64].to_broadcast([P, 16, 64]), ALU.add)
                last.then_inc(c_bias[hd % 2], 1)

            def hgrn():
                q, kk = tiles(big[:, R_HQ:R_HF], T), tiles(big[:, R_HF:R_HG], T)
                acc = tiles(xn_buf[:, 0:T], P)
                for hd in range(4):
                    for lv in range(8):
                        i = 8 * hd + lv
                        if lv < 7:
                            pool.wait_ge(hg["e"], 7 * hd + lv + 1)
                            if i >= 2:
                                pool.wait_ge(hg["qk"], i - 1)
                            nc.gpsimd.tensor_tensor(s_buf[:, (i % 2) * T:(i % 2) * T + T], kk[:, hd, :],
                                                    tmp[:, (7 * hd + lv) % 2, :], ALU.mult).then_inc(hg["kl"], 1)
                        if lv >= 1:
                            add(hd, lv - 1, acc)
                    add(hd, 7, acc)

            def add(hd, lv, acc):
                i = 8 * hd + lv
                pool.wait_ge(hg["mul"], i + 1)
                src = tiles(pt_buf[:, 4 * T:5 * T], P) if i % 2 else tiles(s_buf[:, 4 * T:5 * T], P)
                if lv == 0:
                    if hd >= 1:
                        pool.wait_ge(hg["o_ps"], hd)
                    ins = nc.gpsimd.tensor_copy(acc, src)
                else:
                    pool.wait_ge(hg["acc"], i)
                    ins = nc.gpsimd.tensor_tensor(acc, acc, src, ALU.add)
                ins.then_inc(hg["acc"], 1)

            for st in STAGES:
                if st == "mix_0":
                    attention("a")
                    attention("b")
                elif st == "mix_1":
                    attention("c")
                elif st == "mix_2":
                    hgrn()
                    attention("n")
                elif st == "moe":
                    pool.wait_ge(tab["pairs"], 1)
                    pool.wait_ge(tab["clear"], 16)
                    for n in range(TT * TOP_K):
                        nc.gpsimd.indirect_dma_start(
                            out=dr["table"], out_offset=bass.IndirectOffsetOnAxis(ap=place[:, n:n + 1], axis=0),
                            in_=pay[:, 2 * n:2 * n + 2], in_offset=None).then_inc(tab["filled"], 16)
                    pool.wait_ge(tab["ready"], 1)
                    turns_n = pool.value_load(n_turns[0:1, 0:1], min_val=1, max_val=MAX_BLOCKS // 2)
                    pool.wait_ge(tab["tok_out"], 16)

                    def gather(s, b, n):
                        nc.gpsimd.tensor_copy(idx[:, s:s + 1], tab_sb[:, b, 0].bitcast(I32)).then_inc(bk["staged"], 1)
                        pool.wait_ge(bk["staged"], n)
                        pool.sem_inc(bk["asked"], 1)
                        nc.gpsimd.indirect_dma_start(
                            out=xg[s], out_offset=None, in_=dr["tok"],
                            in_offset=bass.IndirectOffsetOnAxis(ap=idx[:, s:s + 1], axis=0)).then_inc(gathered[s], 16)

                    for s in range(2):
                        gather(s, slice(s, s + 1), s + 1)
                    with pool.Fori(0, turns_n) as i:
                        for s in range(2):
                            pool.wait_ge(bk["tx"], i * 2 + (s + 1))
                            gather(s, bass.ds(i * 2 + (s + 2), 1), i * 2 + (s + 3))

        @block.vector
        def _(dve):
            link = Chain(dve, dve_own)
            dve.wait_ge(consts_in, 64)
            dve.wait_ge(set_up, 1)
            dve.sem_inc(evac_done, 2)

            def norm(name, gain=None, shift=None, dst=xn):
                n = NORM_N[name] + 1
                gain = col(f"g_{name}") if gain is None else gain
                dve.wait_ge(std_ready, n)
                link(nc.vector.reciprocal(rstd[:, :], std[:, :]))
                for k in range(KD):
                    ins = nc.vector.scalar_tensor_tensor(out=dst[:, k, :], in0=h[:, k, :], scalar=gain[:, k:k + 1],
                                                         in1=rstd[:, :], op0=ALU.mult, op1=ALU.mult)
                    if shift is None:
                        ins.then_inc(xn_ready, 1)
                    else:
                        link(ins)
                        nc.vector.tensor_scalar(xn[:, k, :], xn[:, k, :], shift[:, k:k + 1], None, ALU.add
                                                ).then_inc(xn_ready, 1)

            def residual(phase, name, factor, per):
                U, n = BASE[phase]
                with link.loop(n // 2, 0) as i:
                    for s in range(2):
                        dve.wait_ge(units_done, i * 2 + (U + s + 1))
                        for j in range(per):
                            m = i * (2 * per) + (per * s + j)
                            hm = h_buf[:, bass.ds(m * T, T)]
                            f = factor if isinstance(factor, float) else factor[:, bass.ds(m, 1)]
                            last = nc.vector.scalar_tensor_tensor(out=hm, in0=ps[:, 2 * s + j, :], scalar=f, in1=hm,
                                                                  op0=ALU.mult, op1=ALU.add)
                            last.then_inc(h_ready, 1)
                        dve.wait_ge(h_ready, i * (2 * per) + (H_AT[name] - KD + per * (s + 1)))
                        dve.sem_inc(evac_done, 1)

            def ffn(st):
                norm(st)
                phase = f"gu_{st[-1]}_{int(st[3]) - 1}"
                U, n = BASE[phase]
                with link.loop(n // 2, 0) as i:
                    for s in range(2):
                        dve.wait_ge(sil_ready, i * 2 + (SIL_AT[phase] + s + 1))
                        nc.vector.tensor_tensor(big[:, bass.ds(i * (2 * T) + s * T, T)], sil[:, s, :],
                                                ps[:, 2 * s + 1, :], ALU.mult).then_inc(evac_done, 1)
                residual(f"down_{st[-1]}_{int(st[3]) - 1}", st, 0.5, 1)

            def rope_tile(src, dst, scale):
                link(nc.vector.scalar_tensor_tensor(out=dst, in0=src, scalar=scale, in1=cos, op0=ALU.mult, op1=ALU.mult))
                for g in range(4):
                    o, a = 32 * (g ^ 1), 32 * g
                    ins = nc.vector.scalar_tensor_tensor(out=tmp[o:o + 32, 0, :], in0=src[a:a + 32, :], scalar=scale,
                                                         in1=sin[a:a + 32, :], op0=ALU.mult, op1=ALU.mult)
                link(ins)
                return nc.vector.tensor_tensor(dst, dst, tmp[:, 0, :], ALU.add)

            def rope_units(phase, first, n, dst, scale):
                U = u(phase) + first
                with link.loop(n // 2, 12) as i:
                    for s in range(2):
                        dve.wait_ge(units_done, i * 2 + (U + s + 1))
                        for j in range(2):
                            d = big[:, bass.ds(i * (4 * T) + (dst + (2 * s + j) * T), T)]
                            link(rope_tile(ps[:, 2 * s + j, :], d, scale))
                        dve.sem_inc(evac_done, 1)

            def copy_units(phase, first, n, dst, scale=1.0):
                U = u(phase) + first
                for m in range(n):
                    dve.wait_ge(units_done, U + m + 1)
                    b = 2 * (m + first) % 4
                    nc.vector.tensor_scalar(big[:, dst + 2 * m * T:dst + 2 * (m + 1) * T],
                                            ps_t[:, b * T:(b + 2) * T], scale, None, ALU.mult).then_inc(evac_done, 1)

            def token_units(phase, first, n, dst, pitch, width=256):
                U = u(phase) + first
                d = tiles(big[:, dst:dst + TT * pitch], pitch)
                for m in range(n):
                    dve.wait_ge(units_done, U + m + 1)
                    b = 2 * (m + first) % 4
                    nc.vector.tensor_copy(d[:, :, m * 256:m * 256 + width],
                                          tiles(ps_t[:, b * T:(b + 2) * T], 256)[:, :, 0:width]).then_inc(evac_done, 1)

            def attention(name):
                a = ATT[name]
                units, ns = a["units"], len(a["sc"])
                dve.wait_ge(a["mask_in"], 16)
                done = 0
                for i in range(len(units) + 4):
                    if i < len(units):
                        un, b = units[i], i % 2
                        dve.wait_ge(a["sc_ready"], i + 1)
                        if i >= NS:
                            dve.wait_ge(a["pt_ready"], i - NS + 1)
                        if i >= 2:
                            dve.wait_ge(a["exps"], i - 1)
                        if name == "c" and un["t"] == 0:
                            hd = 2 * un["pair"] + un["half"]
                            dve.wait_ge(c_bias[hd % 2], hd // 2 + 1)
                        for g, (_, _, add, c0, n) in enumerate(un["segs"]):
                            last = nc.vector.tensor_tensor_reduce(
                                out=s_buf[:, (i % NS) * SCMAX + c0:(i % NS) * SCMAX + c0 + n], in0=ps[:, a["sc"][i % ns] + g, 0:n],
                                in1=add, scale=1.0, scalar=-3e38, op0=ALU.add, op1=ALU.max,
                                accum_out=mx[:, 4 * b + g:4 * b + g + 1])
                        last.then_inc(a["sc_read"], 1)
                        dve.wait_ge(a["sc_read"], i + 1)
                        ng = len(un["segs"])
                        m = mx[:, 4 * b:4 * b + ng]
                        if un["sink"] is not None:
                            ins = nc.vector.tensor_scalar(negm[:, 4 * b:4 * b + 1], m,
                                                          col("sink")[:, un["sink"]:un["sink"] + 1], -1.0, ALU.max, ALU.mult)
                        elif len(un["groups"]) < ng:
                            ins = nc.vector.tensor_reduce(negm[:, 4 * b:4 * b + 1], m, AX.X, ALU.max, negate=True)
                        else:
                            ins = nc.vector.tensor_scalar(negm[:, 4 * b:4 * b + ng], m, -1.0, None, ALU.mult)
                        ins.then_inc(a["negm"], 1)
                    if 1 <= i <= len(units):
                        j = i - 1
                        un, b = units[j], j % 2
                        ng = len(un["groups"])
                        dve.wait_ge(a["exps"], j + 1)
                        if j >= 2:
                            dve.wait_ge(a["diag"], j - 1)
                        dn = den[:, 4 * b:4 * b + ng]
                        if un["sink"] is not None:
                            link(nc.vector.tensor_tensor(rden[:, 4 * b:4 * b + 1], dn, es[:, b:b + 1], ALU.add))
                            dn = rden[:, 4 * b:4 * b + 1]
                        if "gate" in un:
                            link(nc.vector.reciprocal(rden[:, 4 * b:4 * b + ng], dn))
                            gt = gates[:, un["t"], un["gate"]:un["gate"] + 3]
                            nc.vector.tensor_tensor(fac[:, 4 * b:4 * b + 2], rden[:, 4 * b:4 * b + 2], gt[:, 1:3], ALU.mult)
                            ins = nc.vector.tensor_tensor(fac[:, 4 * b + 2:4 * b + 3], rden[:, 4 * b + 2:4 * b + 3], gt[:, 0:1],
                                                          ALU.mult)
                        else:
                            ins = nc.vector.reciprocal(fac[:, 4 * b:4 * b + ng], dn)
                        ins.then_inc(a["fac"], 1)
                    if i >= 4 and units[i - 4]["last"]:
                        un = units[i - 4]
                        dve.wait_ge(a["pv"], i - 3)
                        nc.vector.tensor_copy(mixed[:, un["out"], :], ps[:, 6 + un["pair"] % 2, :]).then_inc(a["out"], 1)

            def compress():
                for kv in range(2):
                    pe_c = col("pe_k" if kv == 0 else "pe_v")
                    blk = s_buf[:, kv * 1024:kv * 1024 + 992].rearrange("p (l g c) -> p g c l", l=16, g=2)
                    src = big[:, R_KCV + kv * T:R_KCV + (kv + 1) * T]
                    for g in range(2):
                        for par in range(2):
                            for half in range(2):
                                r = slice(64 * g, 64 * g + 64)
                                tk = src[r, 16 * half:16 * half + 16 * N_CMP].rearrange("p (c m q) -> p c m q", m=8, q=2)
                                pos = pe_c[r, 16 * half:16 * half + 16].rearrange("p (m q) -> p m q", q=2)
                                ins = nc.vector.tensor_tensor(
                                    blk[64 * par:64 * par + 64, g, :, 8 * half:8 * half + 8], tk[:, :, :, par],
                                    pos[:, None, :, par].to_broadcast([64, N_CMP, 8]), ALU.add)
                    ins.then_inc(cm["blk"], 1)
                U = u("cmp")
                for kv in range(2):
                    dve.wait_ge(units_done, U + 2 * kv + 2)
                    x1 = s_buf[:, 2048 + kv * 128:2048 + kv * 128 + 124].rearrange("p (j n) -> p j n", j=2)
                    t3 = s_buf[:, 2304 + kv * 128:2304 + kv * 128 + 124].rearrange("p (j n) -> p j n", j=2)
                    b1 = col("b1k" if kv == 0 else "b1v")
                    for j in range(2):
                        ins = nc.vector.tensor_scalar(x1[:, j, :], ps[:, 2 * kv + j, 0:62], b1[:, j:j + 1], None, ALU.add)
                    link(ins)
                    dve.sem_inc(evac_done, 2)
                    link(nc.vector.tensor_tensor(t3, x1, x1, ALU.mult))
                    link(nc.vector.tensor_scalar(t3, t3, 0.044715, 1.0, ALU.mult, ALU.add))
                    nc.vector.tensor_tensor(t3, t3, x1, ALU.mult).then_inc(cm["th"], 1)
                for kv in range(2):
                    x1 = s_buf[:, 2048 + kv * 128:2048 + kv * 128 + 124]
                    t3 = s_buf[:, 2304 + kv * 128:2304 + kv * 128 + 124]
                    dve.wait_ge(cm["g1"], kv + 1)
                    nc.vector.tensor_tensor(x1, x1, t3, ALU.mult).then_inc(cm["hid"], 1)
                nc.vector.memset(kcmp, 0.0)
                link(nc.vector.memset(big[0:32, R_VCMP:R_VCMP + 2 * HD], 0.0))
                dve.wait_ge(cm["kv"], 2)
                nc.vector.tensor_copy(kcmp[:, 0:N_CMP], ps[:, 4, 0:N_CMP])
                link(nc.vector.tensor_copy(big[0:N_CMP, R_VCMP:R_VCMP + 2 * HD], ps[0:N_CMP, 5, 0:2 * HD]))

            def hgrn():
                q, f = tiles(big[:, R_HQ:R_HF], T), tiles(big[:, R_HF:R_HG], T)
                lbs = small[:, 64:72]
                lg = col("lb")
                m = small[:, 72:76]
                link(nc.vector.tensor_tensor(m, lg[:, 0:4], lg[:, 4:8], ALU.max))
                nc.vector.tensor_tensor(lbs[:, 0:4], lg[:, 0:4], m, ALU.subtract)
                nc.vector.tensor_tensor(lbs[:, 4:8], lg[:, 4:8], m, ALU.subtract).then_inc(hg["lbe"], 1)
                dve.wait_ge(hg["lbe"], 2)
                link(nc.vector.tensor_tensor(m, lbs[:, 0:4], lbs[:, 4:8], ALU.add))
                link(nc.vector.reciprocal(small[:, 76:80], m))
                lb, lb1 = small[:, 80:84], small[:, 84:88]
                nc.vector.tensor_tensor(lb, lbs[:, 0:4], small[:, 76:80], ALU.mult)
                link(nc.vector.tensor_tensor(lb1, lbs[:, 4:8], small[:, 76:80], ALU.mult))
                dve.wait_ge(hg["sig"], 2)
                for hd in range(4):
                    ins = nc.vector.tensor_scalar(f[:, hd, :], f[:, hd, :], lb1[:, hd:hd + 1], lb[:, hd:hd + 1],
                                                  ALU.mult, ALU.add)
                link(ins)
                nc.vector.tensor_scalar(big[:, R_HF:R_HG], big[:, R_HF:R_HG], 2.0 ** -64, None, ALU.max
                                        ).then_inc(hg["ln_in"], 1)
                dve.wait_ge(hg["ln"], 1)
                link(nc.vector.tensor_scalar(big[:, R_HF:R_HG], big[:, R_HF:R_HG], -1.0, 1.0, ALU.mult, ALU.add))
                for n in range(4 * TT):
                    lf = xn_buf[:, 4 * T + n * P:4 * T + n * P + P]
                    ins = nc.vector.tensor_tensor_scan(mixed_buf[:, n * P:n * P + P],
                                                       ones[:, :], lf, 0.0, ALU.mult, ALU.add)
                link(ins)
                link(nc.vector.tensor_copy(xn_buf[:, 4 * T:8 * T], mixed_buf[:, 0:4 * T]))
                dve.sem_inc(hg["cum"], 1)
                dve.wait_ge(hg["mask_in"], 16)
                for hd in range(4):
                    b = xn_buf[:, (4 + hd) * T:(5 + hd) * T]

                    def diff(lv):
                        i = 7 * hd + lv
                        half = 64 >> lv
                        if i >= 2:
                            dve.wait_ge(hg["kl"], i - 1)
                            dve.wait_ge(hg["ql"], i - 1)
                        bv = b.rearrange("p (n c) -> p n c", c=2 * half)
                        nc.vector.tensor_tensor(tmp[:, i % 2, :].rearrange("p (n c) -> p n c", c=2 * half), bv,
                                                bv[:, :, half - 1:half].to_broadcast([P, T // (2 * half), 2 * half]),
                                                ALU.subtract).then_inc(hg["diff"], 1)

                    def masked(lv):
                        i = 8 * hd + lv
                        dve.wait_ge(hg["qk"], i + 1)
                        if i >= 2:
                            dve.wait_ge(hg["acc"], i - 1)
                        dst = tiles(pt_buf[:, 4 * T:5 * T], P) if i % 2 else tiles(s_buf[:, 4 * T:5 * T], P)
                        nc.vector.tensor_tensor(dst, tiles(ps[:, i % 2, :], P),
                                                mask[:, None, lv * P:lv * P + P].to_broadcast([P, TT, P]), ALU.mult
                                                ).then_inc(hg["mul"], 1)

                    diff(0)
                    for lv in range(8):
                        i = 8 * hd + lv
                        if lv + 1 < 7:
                            diff(lv + 1)
                        if lv < 7:
                            dve.wait_ge(hg["e"], 7 * hd + lv + 1)
                            if i >= 2:
                                dve.wait_ge(hg["qk"], i - 1)
                            nc.vector.tensor_tensor(s_buf[:, (2 + i % 2) * T:(3 + i % 2) * T], q[:, hd, :],
                                                    tmp[:, (7 * hd + lv) % 2, :], ALU.mult).then_inc(hg["ql"], 1)
                        if lv >= 1:
                            masked(lv - 1)
                    dve.sem_inc(hg["ex_in"], 1)
                    masked(7)
                    dve.wait_ge(hg["ex"], hd + 1)
                    if hd >= 1:
                        dve.wait_ge(hg["x_ps"], hd)
                    eb, ek = sil[:, 0, :], sil[:, 1, :]
                    nc.vector.tensor_tensor(pt_buf[:, 0:T], q[:, hd, :], eb, ALU.mult)
                    link(nc.vector.tensor_tensor(pt_buf[:, T:2 * T], f[:, hd, :], ek, ALU.mult))
                    for t in range(2):
                        ins = nc.vector.tensor_scalar(pt_buf[:, 2 * T + t * P:2 * T + t * P + P],
                                                      pt_buf[:, T + t * P:T + t * P + P],
                                                      eb[:, (t + 2) * P - 1:(t + 2) * P], None, ALU.mult)
                    link(ins)
                    nc.vector.tensor_scalar(pt_buf[:, 3 * T:3 * T + P], pt_buf[:, 2 * T:2 * T + P],
                                            eb[:, 3 * P - 1:3 * P], None, ALU.mult).then_inc(hg["kx"], 1)
                    dve.wait_ge(hg["x_ps"], hd + 1)
                    if hd >= 1:
                        dve.wait_ge(hg["o_ps"], hd)
                    nc.vector.tensor_copy(xn_buf[:, T:T + 6 * P], ps_t[:, 2 * T:2 * T + 6 * P]).then_inc(hg["x_sb"], 1)
                    dve.wait_ge(hg["o_std"], hd + 1)
                    link(nc.vector.reciprocal(rstd[:, :], std[:, :]))
                    link(nc.vector.scalar_tensor_tensor(out=mixed[:, hd, :], in0=ps[:, 4, :], scalar=col("hg_g")[:, hd:hd + 1],
                                                        in1=rstd[:, :], op0=ALU.mult, op1=ALU.mult))
                    nc.vector.tensor_tensor(mixed[:, hd, :], mixed[:, hd, :], tiles(big[:, R_HG:R_NQ], T)[:, hd, :],
                                            ALU.mult).then_inc(hg["o_out"], 1)

            def router():
                IMM = -3e30
                sc = tiles(s_buf[:, 0:256], N_EXP)
                ch = tiles(s_buf[:, 256:512], N_EXP)
                m8 = tiles(s_buf[:, 512:768], 8)
                rep = tiles(s_buf[:, 768:1024], N_EXP)
                wr = tiles(s_buf[:, 1024:1280], N_EXP)
                dve.wait_ge(rt["sig"], 1)
                link(nc.vector.tensor_tensor(ch, sc, col("router_bias")[:, None, :].to_broadcast([P, TT, N_EXP]), ALU.add))
                for n in range(32):
                    ins = nc.vector.max(m8[:, n, :], s_buf[:, 256 + 8 * n:264 + 8 * n])
                gs = tiles(small[:, 128:176], 12)
                g8, gr = tiles(small[:, 176:208], 8), tiles(small[:, 208:256], 12)
                link(nc.vector.memset(small[:, 128:176], 3e30))
                ins = nc.vector.tensor_tensor(gs[:, :, 0:8], s_buf[:, 512:768].rearrange("p (t g e) -> p t g e", g=8, e=8)[:, :, :, 0],
                                              s_buf[:, 512:768].rearrange("p (t g e) -> p t g e", g=8, e=8)[:, :, :, 1], ALU.add)
                link(ins)
                for t in range(TT):
                    ins = nc.vector.max(g8[:, t, :], gs[:, t, :])
                link(ins)
                for t in range(TT):
                    ins = nc.vector.match_replace(gr[:, t, :], g8[:, t, :], gs[:, t, :], IMM)
                link(ins)
                pen = tiles(small[:, 256:288], 8)
                link(nc.vector.tensor_scalar(pen, gr[:, :, 0:8], IMM, NEG, ALU.not_equal, ALU.mult))
                c4 = s_buf[:, 256:512].rearrange("p (t g e) -> p t g e", g=8, e=8)
                for t in range(TT):
                    ins = nc.vector.tensor_tensor(c4[:, t], c4[:, t], pen[:, t, :, None].to_broadcast([P, 8, 8]), ALU.add)
                link(ins)
                v8 = tiles(small[:, 288:320], 8)
                for t in range(TT):
                    ins = nc.vector.max(v8[:, t, :], ch[:, t, :])
                link(ins)
                for t in range(TT):
                    ins = nc.vector.match_replace(rep[:, t, :], v8[:, t, :], ch[:, t, :], IMM)
                link(ins)
                sm, rs = small[:, 320:324], small[:, 324:328]
                for t in range(TT):
                    ins = nc.vector.scalar_tensor_tensor(out=wr[:, t, :], in0=rep[:, t, :], scalar=IMM, in1=sc[:, t, :],
                                                         op0=ALU.is_equal, op1=ALU.mult)
                link(ins)
                link(nc.vector.tensor_reduce(sm, wr, AX.X, ALU.add))
                link(nc.vector.reciprocal(rs, sm))
                for t in range(TT):
                    ins = nc.vector.tensor_scalar(wr[:, t, :], wr[:, t, :], rs[:, t:t + 1], ROUTED_SCALE, ALU.mult, ALU.mult)
                link(ins)
                nc.vector.tensor_scalar(s_buf[:, 2560:2816], s_buf[:, 768:1024], IMM, None, ALU.is_equal).then_inc(tab["sel"], 1)

            def tables():
                wr, sel = tiles(s_buf[:, 1024:1280], N_EXP), tiles(s_buf[:, 2560:2816], N_EXP)
                pos, nth = s_buf[:, 2816:3072], tiles(s_buf[:, 3072:3328], N_EXP)
                terms = tiles(pt_buf[:, 0:2 * TOP_K * N_EXP], N_EXP)
                pay3 = pay.rearrange("p (n c) -> p n c", c=2)
                posk = s_buf[:, 3488:3520]
                nc.vector.memset(s_buf[:, 3584:3584 + 2 * MAX_BLOCKS + 8], 0.0).then_inc(tab["zero"], 1)
                dve.wait_ge(tab["const_in"], 16)
                dve.wait_ge(tab["rank"], 1)
                rank, count = ps[:, 5, 0:TT * N_EXP], ps[:, 5, TT * N_EXP:(TT + 1) * N_EXP]
                nb, end, begin = small[:, 332:396], small[:, 396:460], small[:, 128:192]
                link(nc.vector.tensor_scalar(nb, count, 0.0, None, ALU.is_gt))
                for j in range(1, T // P):
                    link(nc.vector.scalar_tensor_tensor(out=nb, in0=count, scalar=float(j * P), in1=nb,
                                                        op0=ALU.is_gt, op1=ALU.add))
                link(nc.vector.tensor_tensor_scan(end, ones[:, 0:N_EXP], nb, 0.0, ALU.mult, ALU.add))
                link(nc.vector.tensor_tensor(begin, end, nb, ALU.subtract))
                blk = tmp_buf[:, 0:TT * N_EXP]
                link(nc.vector.tensor_scalar(blk, rank, float(P), None, ALU.is_ge))
                for j in range(2, T // P):
                    link(nc.vector.scalar_tensor_tensor(out=blk, in0=rank, scalar=float(j * P), in1=blk,
                                                        op0=ALU.is_ge, op1=ALU.add))
                link(nc.vector.scalar_tensor_tensor(out=pos, in0=blk, scalar=-float(P), in1=rank, op0=ALU.mult, op1=ALU.add))
                link(nc.vector.scalar_tensor_tensor(out=pos, in0=pos, scalar=float(MAX_BLOCKS + 4), in1=blk,
                                                    op0=ALU.mult, op1=ALU.add))
                p3 = tiles(pos, N_EXP)
                link(nc.vector.tensor_tensor(p3, p3, begin[:, None, :].to_broadcast([P, TT, N_EXP]), ALU.add))
                for t in range(TT):
                    ins = nc.vector.tensor_tensor_scan(nth[:, t, :], ones[:, 0:N_EXP], sel[:, t, :], 0.0, ALU.mult, ALU.add)
                link(ins)
                link(nc.vector.tensor_tensor(nth, nth, sel, ALU.mult))
                for t in range(TT):
                    for k in range(TOP_K):
                        n = t * TOP_K + k
                        for c, (src, dst) in enumerate(((p3, posk[:, n:n + 1]), (wr, pay3[:, n, 1:2]))):
                            ins = nc.vector.scalar_tensor_tensor(out=terms[:, 2 * k + c, :], in0=nth[:, t, :], scalar=float(k + 1), in1=src[:, t, :],
                                                                 op0=ALU.is_equal, op1=ALU.mult, accum_out=dst)
                    link(ins)
                    link(nc.vector.tensor_copy(pay3[:, t * TOP_K:(t + 1) * TOP_K, 0].bitcast(I32),
                                               tok_no[:, t:t + 1].to_broadcast([P, TOP_K])))
                nc.vector.tensor_copy(place, posk).then_inc(tab["pairs"], 1)
                be, nt = small[:, 460:461], small[:, 461:462]
                nc.vector.scalar_tensor_tensor(out=terms[:, 0, :], in0=end, scalar=slot_no, in1=ones[:, 0:N_EXP],
                                               op0=ALU.is_le, op1=ALU.mult, accum_out=be)
                link(nc.vector.scalar_tensor_tensor(out=blk[:, 0:N_EXP], in0=iota_e2, scalar=end[:, N_EXP - 1:N_EXP],
                                                    in1=ones[:, 0:N_EXP], op0=ALU.is_lt, op1=ALU.mult, accum_out=nt))
                link(nc.vector.tensor_scalar(be, be, float(N_EXP - 1), None, ALU.min))
                nc.vector.tensor_copy(block_e, be)
                nc.vector.tensor_copy(n_turns, nt).then_inc(tab["blocks"], 1)

            def routed():
                dve.wait_ge(tab["in"], 16)
                link(nc.vector.tensor_copy(tab_f, tab_sb[:, :, 0].bitcast(I32)))
                dve.wait_ge(tab["filled"], 16 * TT * TOP_K)
                dve.wait_ge(moe["acc"], KD)
                nc.vector.memset(o_hi[:, :].bitcast(F32), 0.0)
                nc.vector.memset(o_lo[:, :].bitcast(F32), 0.0)
                link(nc.vector.memset(send[:, :].bitcast(F32), 0.0))
                dve.sem_inc(bk["ol"], 1)
                dve.sem_inc(bk["added"], 2)
                dve.sem_inc(tab["ready"], 1)
                turns_n = dve.value_load(n_turns[0:1, 0:1], min_val=1, max_val=MAX_BLOCKS // 2)

                def hidden(s, b, n):
                    dve.wait_ge(bk["sil"], n)
                    nc.vector.scalar_tensor_tensor(out=hid_b[s], in0=sil_b[s], scalar=tab_sb[:, b, 1],
                                                   in1=ps[:, 2, EXP_H:2 * EXP_H], op0=ALU.mult, op1=ALU.mult).then_inc(bk["hid"], 1)

                def add_sent(i):
                    for m in range(KD):
                        dve.wait_ge(bk["sum"], i * KD + (m + 1))
                        nc.vector.tensor_tensor(mixed[:, m, :], mixed[:, m, :], ps[:, 6 + m % 2, :], ALU.add
                                                ).then_inc(bk["added"], 1)

                hidden(0, slice(0, 1), 1)
                with dve.Fori(0, turns_n) as i:
                    for s in range(2):
                        hidden(1 - s, bass.ds(i * 2 + (s + 1), 1), i * 2 + (s + 2))
                        if s == 0:
                            add_sent(i)
                        nc.vector.tensor_scalar(send[:, s * T:(s + 1) * T], iota_t, tab_f[:, bass.ds(i * 2 + s, 1)], None,
                                                ALU.is_equal)
                        dve.wait_ge(bk["oh"], i * 2 + (s + 1))
                        nc.vector.tensor_tensor(o_lo[:, s * D:(s + 1) * D], ps_t[:, 4 * T:4 * T + D],
                                                o_hi[:, s * D:(s + 1) * D].bitcast(F32), ALU.subtract).then_inc(bk["ol"], 1)
                add_sent(turns_n)
                dve.wait_ge(bk["added"], turns_n * KD + (KD + 2))

            def expert_add(m, n, first):
                dve.wait_ge(moe["dn"], n)
                y = mixed[:, m, :]
                if first:
                    nc.vector.tensor_copy(y, ps[:, 4 + m % 4, :]).then_inc(moe["acc"], 1)
                else:
                    nc.vector.tensor_tensor(y, y, ps[:, 4 + m % 4, :], ALU.add).then_inc(moe["acc"], 1)

            for st in STAGES:
                if st.startswith("ffn"):
                    ffn(st)
                elif st.startswith("ple"):
                    l = st[-1]
                    norm(st)
                    g = tiles(big[:, 0:8 * T], T)
                    U, n = BASE[f"pp_{l}"]
                    dve.wait_ge(evac_done, U + 2)
                    for m in range(n):
                        dve.wait_ge(units_done, U + m + 1)
                        for j in range(2):
                            k = 2 * m + j
                            link(nc.vector.tensor_tensor(g[:, k, :], g[:, k, :], ps[:, 2 * (m % 2) + j, :], ALU.mult))
                            nc.vector.tensor_tensor(h[:, k, :], h[:, k, :], g[:, k, :], ALU.add).then_inc(h_ready, 1)
                        dve.sem_inc(evac_done, 1)
                elif st == "mix_0":
                    norm(st)
                    rope_units("in_ab", 0, 6, 0, HD ** -0.5)
                    rope_units("in_ab", 6, 4, 12 * T, 1.0)
                    token_units("v_ab", 0, 4, 20 * T, D)
                    dve.wait_ge(evac_done, u("v_ab") + 6)
                    dve.sem_inc(ATT["a"]["qkv"], 1)
                    dve.sem_inc(ATT["b"]["qkv"], 1)
                    dve.sem_inc(ATT["b"]["mask_in"], 16)
                    attention("a")
                    attention("b")
                    residual("out_ab", st, 1.0, 2)
                elif st == "mix_1":
                    norm(st)
                    copy_units("in_c", 0, 4, 0, HD ** -0.5)
                    copy_units("in_c", 4, 4, 8 * T)
                    token_units("v_c", 0, 4, 16 * T, D)
                    dve.wait_ge(evac_done, u("v_c") + 6)
                    dve.sem_inc(ATT["c"]["qkv"], 1)
                    attention("c")
                    residual("out_c", st, 1.0, 2)
                elif st == "mix_2":
                    U, n = BASE["ada"]
                    with link.loop(n // 2, 0) as i:
                        for s in range(2):
                            dve.wait_ge(units_done, i * 2 + (U + s + 1))
                            for j in range(2):
                                m = i * 4 + (2 * s + j)
                                a = COLS["b_ada"][0]
                                ins = nc.vector.tensor_tensor(mod[:, bass.ds(m, 1)], ps[:, 2 * s + j, 0:1],
                                                              cols[:, bass.ds(m + a, 1)], ALU.add)
                            ins.then_inc(evac_done, 1)
                    dve.wait_ge(evac_done, U + n + 2)
                    nc.vector.scalar_tensor_tensor(out=col("g_norm1"), in0=mod[:, 8:16], scalar=1.0, in1=col("g_norm1"),
                                                   op0=ALU.add, op1=ALU.mult)
                    link(nc.vector.scalar_tensor_tensor(out=col("g_norm2"), in0=mod[:, 32:40], scalar=1.0, in1=col("g_norm2"),
                                                        op0=ALU.add, op1=ALU.mult))
                    norm("first", dst=h)
                    dve.wait_ge(xn_ready, KD * (NORM_N["first"] + 1))
                    dve.sem_inc(h_ready, KD)
                    norm("norm1", shift=mod[:, 0:8])
                    copy_units("in_2", 0, 2, R_HQ, HG_SCALE)
                    copy_units("in_2", 2, 4, R_HF)
                    U = u("in_2") + 6
                    for m in range(2):
                        dve.wait_ge(units_done, U + m + 1)
                        for j in range(2):
                            k = 2 * m + j
                            src = ps[:, 2 * (m % 2) + j, :]
                            nc.vector.tensor_scalar(big[:, R_NQ + k * T:R_NQ + (k + 1) * T], src, HD ** -0.5, None, ALU.mult)
                            link(rope_tile(src, big[:, R_NR + k * T:R_NR + (k + 1) * T], HD ** -0.5))
                        dve.sem_inc(evac_done, 1)
                    copy_units("in_2", 8, 1, R_KCV)
                    U = u("in_2") + 9
                    dve.wait_ge(units_done, U + 1)
                    for j in range(2):
                        link(rope_tile(ps[:, 2 + j, :], big[:, R_KSW + j * T:R_KSW + (j + 1) * T], 1.0))
                    dve.sem_inc(evac_done, 1)
                    token_units("tok_2", 0, 2, R_VI, T)
                    token_units("tok_2", 2, 1, R_VSW, 256)
                    token_units("tok_2", 3, 1, R_GATE, 24, width=24)
                    dve.wait_ge(evac_done, u("tok_2") + 6)
                    compress()
                    hgrn()
                    g3 = gates[:, 0, :].rearrange("p (n c) -> p n c", c=3)
                    dve.wait_ge(ATT["n"]["mask_in"], 16)
                    link(nc.vector.tensor_scalar(g3[:, :, 0], g3[:, :, 0], mask[:, 640:641], None, ALU.mult))
                    dve.sem_inc(ATT["n"]["qkv"], 1)
                    attention("n")
                    residual("out_2", st, mod[:, 16:24], 2)
                elif st == "moe":
                    norm("norm2", shift=mod[:, 24:32])
                    router()
                    tables()
                    dve.wait_ge(moe["sil"], 1)
                    hb = tiles(s_buf[:, 1536:2560], T)
                    for j in range(2):
                        ins = nc.vector.tensor_tensor(hb[:, j, :], sil[:, j, :], ps[:, 2 + j, :], ALU.mult)
                    ins.then_inc(moe["hid"], 1)
                    for m in range(KD):
                        expert_add(m, m + 1, True)
                    routed()
                    for m in range(KD):
                        nc.vector.scalar_tensor_tensor(out=h[:, m, :], in0=mixed[:, m, :], scalar=mod[:, 40 + m:41 + m],
                                                       in1=h[:, m, :], op0=ALU.mult, op1=ALU.add).then_inc(h_ready, 1)
                    norm("final")


def _units(w, width=256):
    k, n = w.shape
    return np.ascontiguousarray(w.reshape(k // P, P, n // width, width).transpose(2, 1, 0, 3)).reshape(
        n // width, P, (k // P) * width)


def _column(v):
    return v.reshape(-1, P).T


def _heads(w, order):
    return np.concatenate([w[:, a * HD:(a + 1) * HD] for a in order], axis=1)


def _constants():
    q, kk = np.arange(P)[:, None], np.arange(896)[None, :]
    off = kk - 384 - q
    near = kk[:, :384] - P - q
    where = lambda ok: np.where(ok, np.float32(0), np.float32(NEG)).astype(np.float32)
    mask_ab = np.concatenate([
        where(np.abs(near) <= 128), where(np.abs(near) <= 64),
        where((np.abs(off) <= 256) & (off % 4 == 0)), where((np.abs(off) <= 1024) & (off % 16 == 0))], axis=1)
    qj, kj = np.arange(64)[:, None], np.arange(64)[None, :]
    start = np.clip(qj - 8, 0, 48)
    mask_c = np.tile(where((kj >= start) & (kj < start + 16)), (2, 1))
    causal = where(off[:, :512] <= 0)
    pos = np.arange(T).reshape(TT, P).T[:, :, None]
    c = np.arange(32)[None, None, :]
    cmp_ok = (c * 16 + 31 <= pos) & (c < N_CMP)
    mask_n = np.concatenate([causal, where(cmp_ok).reshape(P, TT * 32)], axis=1)
    mask_n = np.concatenate([mask_n, (np.arange(P) >= 31).astype(np.float32)[:, None]], axis=1)
    s, t = np.arange(P)[:, None], np.arange(P)[None, :]
    levels = []
    for lv in range(7):
        half = 64 >> lv
        levels.append((s // (2 * half) == t // (2 * half)) & (s % (2 * half) < half) & (t % (2 * half) >= half))
    levels.append(s == t)
    mask_h = np.concatenate(levels, axis=1).astype(np.float32)
    number = np.arange(P, dtype=np.float32)[:, None]
    mask_m = np.concatenate([(s < t).astype(np.float32), np.tile(np.arange(T, dtype=np.float32), (P, 1)),
                             np.tile(2 * np.arange(N_EXP, dtype=np.float32), (P, 1)),
                             number, number + P * np.arange(TT, dtype=np.float32)], axis=1)
    inv = (np.float32(10000.0) ** (-np.arange(32, dtype=np.float32) / np.float32(32))).astype(np.float32)
    ang = np.arange(T, dtype=np.float32)[None, :] * inv[:, None]
    co, si = np.cos(ang).astype(np.float32), np.sin(ang).astype(np.float32)
    rot = np.concatenate([np.tile(co, (4, 1)), np.concatenate([si, -si, si, -si], axis=0)], axis=1)
    return dict(mask_ab=mask_ab, mask_c=mask_c, mask_n=mask_n, mask_h=mask_h, mask_m=mask_m, rot=rot,
                eye=np.eye(P, dtype=np.float32))


def _lay_out(i):
    f = lambda n: np.asarray(i[n])
    c = _constants()
    a = {k: c[k] for k in ("mask_ab", "mask_c", "mask_n", "mask_h", "mask_m", "rot", "eye")}
    tok = lambda x: np.ascontiguousarray(x.T.reshape(-1, P, T).transpose(1, 0, 2)).reshape(P, -1)
    a["xT"] = tok(f("x")[0])
    a["pT"] = np.stack([tok(f("p")[l, 0]) for l in range(2)])
    for l in range(2):
        for k, n in enumerate(("ffn1", "ffn2")):
            g, up = f(f"{n}_w_gate")[l], f(f"{n}_w_up")[l]
            both = np.concatenate([g.reshape(D, NF, 1, P), up.reshape(D, NF, 1, P)], axis=2).reshape(D, 2 * FF)
            a[f"gu_{l}_{k}"] = _units(both)
            a[f"down_{l}_{k}"] = _units(f(f"{n}_w_down")[l], P)
        a[f"pg_{l}"] = _units(f("w_ple_gate")[l])
        a[f"pp_{l}"] = _units(f("w_ple_proj")[l])
    w = f("w_in_ab")[0]
    order_a = [x for p in A_PAIRS for x in p]
    qa, ka, va, qb, kb, vb = np.split(w, [768, 1024, 1280, 2048, 2816], axis=1)
    a["in_ab"] = _units(np.concatenate([_heads(qa, order_a), qb, ka, kb], axis=1))
    a["v_ab"] = _units(np.concatenate([va, vb], axis=1))
    w = f("w_out_ab")[0]
    a["out_ab"] = _units(np.concatenate([w[x * HD:(x + 1) * HD] for x in order_a] + [w[768:]], axis=0))
    w = f("w_in_c")[0]
    a["in_c"], a["v_c"] = _units(w[:, :2048]), _units(w[:, 2048:])
    a["out_c"] = _units(f("w_out_c")[0])
    rpb = np.pad(f("rpb_c")[0], ((0, 0), (0, 0), (48, 48)))
    a["rpb"] = np.ascontiguousarray(np.stack([rpb[:, :, 63 - j:127 - j] for j in range(64)], axis=1)).reshape(16, 64, 960)
    a["ada"] = _units(f("w_ada_2")[0])
    order_n = [x for p in N_PAIRS for x in p]
    hq, hf, hi, hgt, nq, kc, vc, ks, vs, kw, vw, ng = np.split(
        f("w_in_2")[0], np.cumsum([512] * 5 + [128] * 6).tolist(), axis=1)
    a["in_2"] = _units(np.concatenate([hq, hf, hgt, _heads(nq, order_n), kc, vc, ks, kw], axis=1))
    a["tok_2"] = _units(np.concatenate([hi, vs, vw, np.pad(ng, ((0, 0), (0, 232)))], axis=1))
    a["cmp"] = np.stack([x for n in ("k", "v") for x in
                         f(f"cmp_w1_{n}_2")[0].reshape(2, 8, P, 256).transpose(0, 2, 1, 3).reshape(2, P, UNIT)])
    w = f("w_out_2")[0]
    a["out_2"] = _units(np.concatenate([w[:512]] + [w[512 + x * HD:512 + (x + 1) * HD] for x in order_n], axis=0))
    down = f("w_sh_dn_2")[0].reshape(2, P, 2, 512).transpose(2, 1, 0, 3).reshape(2, P, 1024)
    a["shared"] = np.concatenate([_units(f("w_sh_gu_2")[0]), np.pad(down, ((0, 0), (0, 0), (0, UNIT - 1024)))], axis=0)
    gu, dn = f("w_exp_gu_2")[0], f("w_exp_dn_2")[0]
    a["exp_gu"] = gu.reshape(N_EXP, KD, P, 2 * EXP_H).transpose(0, 2, 1, 3).reshape(N_EXP, P, -1)
    a["exp_dn"] = dn.reshape(N_EXP, 2, P, D).transpose(0, 2, 1, 3).reshape(N_EXP, P, -1)
    gains = {"ffn1": "norm_ffn1", "mix": "norm_mix", "ffn2": "norm_ffn2", "ple": "norm_ple"}
    parts = []
    for n in NORMS:
        if n[-2] == "_":
            parts.append(_column(f(gains[n[:-2]])[int(n[-1])]))
        else:
            parts.append(_column({"first": f("norm_final"), "norm1": f("norm1_g_2")[0], "norm2": f("norm2_g_2")[0], "final": f("final_g_2")}[n]))
    parts += [_column(f("b_ada_2")[0]), _column(f("c_2")[0]), _column(f("hg_lb_logits_2")[0]), _column(f("hg_lb_logits_2")[1]),
              _column(f("hg_norm_g_2")[0]), _column(f("cmp_b1_k_2")[0]), _column(f("cmp_b1_v_2")[0]),
              np.tile(f("cmp_pos_k_2")[0].T, (2, 1)), np.tile(f("cmp_pos_v_2")[0].T, (2, 1)),
              np.broadcast_to(f("sink_a")[0], (P, 12)), np.broadcast_to(f("router_bias_2")[0], (P, N_EXP))]
    cols3 = lambda w: w.reshape(-1, P, w.shape[1]).transpose(1, 0, 2).reshape(P, -1)
    parts += [cols3(f("cmp_w2_k_2")[0]), cols3(f("cmp_w2_v_2")[0]), cols3(f("router_w_2")[0])]
    a["cols"] = np.concatenate(parts, axis=1)
    assert a["cols"].shape == (P, NCOL)
    return {k: np.ascontiguousarray(v, dtype=v.dtype) for k, v in a.items()}


def _program(nc, arrays, stop_at=None):
    dr = {n: nc.dram_tensor(f"in_{n}", a.shape, F32, kind="ExternalInput").ap() for n, a in arrays.items()}
    dr["tok"] = nc.dram_tensor("tokens", [T, D], F32, kind="Internal").ap()
    dr["table"] = nc.dram_tensor("slots", [P * (MAX_BLOCKS + 4), 2], F32, kind="Internal").ap()
    dr["block_e"] = nc.dram_tensor("block_experts", [1, P], I32, kind="Internal").ap()
    out = nc.dram_tensor("out_0", [P, KD * T], F32, kind="ExternalOutput").ap()
    block_kernel(nc, dr, out, stop_at)


def kernel(**inputs):
    import concourse.bacc as bacc
    from concourse.bass_utils import run_bass_kernel_spmd
    arrays = _lay_out(inputs)
    nc = bacc.Bacc("TRN2", target_bir_lowering=False, num_devices=1)
    _program(nc, arrays)
    r = run_bass_kernel_spmd(nc, [{f"in_{n}": a for n, a in arrays.items()}], core_ids=[0])
    y = r.results[0]["out_0"].reshape(P, KD, T)
    return np.ascontiguousarray(y.transpose(2, 1, 0)).reshape(1, T, D)
```

```python
from contextlib import ExitStack, contextmanager

import numpy as np

import concourse.bass as bass
from concourse import mybir

ALU = mybir.AluOpType
ACT = mybir.ActivationFunctionType
AX = mybir.AxisListType
F32 = mybir.dt.float32
F32R = mybir.dt.float32r
I32 = mybir.dt.int32

P = 128
T = 512
TT = T // P
D = 1024
KD = D // P
FF = 2816
NF = FF // P
HD = 64
NEG = -1e30
EPS = 1e-6
UNIT = KD * P
DOWN = (8, 8, NF - 16)
N_EXP = 64
EXP_H = 256
TOP_K = 8
MAX_BLOCKS = T * TOP_K // P + N_EXP
NS = 3
SCMAX = 384 + 512 + 512
ROUTED_SCALE = 2.5
HG_SCALE = 128 ** -0.5
N_CMP = (T - 32) // 16 + 1
GELU_C = 2.0 * (2.0 / np.pi) ** 0.5

A_PAIRS = [(0, 3), (1, 4), (2, 5), (6, 9), (7, 10), (8, 11)]
N_PAIRS = [(0, 4), (1, 5), (2, 6), (3, 7)]

NORMS = ["ffn1_0", "mix_0", "ffn2_0", "ple_0", "ffn1_1", "mix_1", "ffn2_1", "ple_1", "first", "norm1", "norm2", "final"]
COLS = {}
_at = 0
for _name, _n in ([(f"g_{n}", KD) for n in NORMS] + [
        ("b_ada", 48), ("c", KD), ("lb", 8), ("hg_g", 4), ("b1k", 2), ("b1v", 2), ("pe_k", 32), ("pe_v", 32),
        ("sink", 12), ("router_bias", N_EXP), ("w2k", 128), ("w2v", 128), ("router_w", KD * N_EXP)]):
    COLS[_name] = (_at, _n)
    _at += _n
NCOL = _at

PHASES = []
for _l in range(2):
    PHASES += [(f"gu_{_l}_0", 2 * NF), (f"down_{_l}_0", KD * len(DOWN))]
    PHASES += [("in_ab", 20), ("v_ab", 8), ("out_ab", 8)] if _l == 0 else [("in_c", 16), ("v_c", 8), ("out_c", 8)]
    PHASES += [(f"gu_{_l}_1", 2 * NF), (f"down_{_l}_1", KD * len(DOWN)), (f"pg_{_l}", 8), (f"pp_{_l}", 2)]
PHASES += [("in_2", 20), ("tok_2", 8), ("cmp", 8), ("out_2", 8), ("shared", 6)]
WHOLE = ("cmp", "shared")
BASE, CUT = {}, {}
_at = _cut = 0
for _name, _n in PHASES:
    assert _n % 2 == 0
    BASE[_name], CUT[_name] = (_at, _n), _cut
    _at += _n
    _cut += 0 if _name in WHOLE else _n
PARTS = ["ffn1_0", "mix_0", "out_ab", "ffn2_0", "ple_0", "ffn1_1", "mix_1", "out_c", "ffn2_1", "ple_1", "norm1", "out_2",
         "norm2"]
PART_AT = {n: KD * k for k, n in enumerate(PARTS)}
STAGE_PHASES = {"mix_0": ["in_ab", "v_ab", "out_ab"], "mix_1": ["in_c", "v_c", "out_c"],
                "mix_2": ["in_2", "tok_2", "cmp", "out_2"], "moe": ["shared"]}
for _l in range(2):
    for _k in range(2):
        STAGE_PHASES[f"ffn{_k + 1}_{_l}"] = [f"gu_{_l}_{_k}", f"down_{_l}_{_k}"]
    STAGE_PHASES[f"ple_{_l}"] = [f"pg_{_l}", f"pp_{_l}"]


class Chain:

    def __init__(self, eng, sem):
        self.eng, self.sem, self.n, self.turn = eng, sem, 0, None

    def __call__(self, ins):
        ins.then_inc(self.sem, 1)
        self.n += 1
        self.eng.wait_ge(self.sem, self.n if self.turn is None else self.turn + self.n)

    @contextmanager
    def loop(self, turns, per):
        if turns == 1:
            yield 0
            return
        start = self.n
        with self.eng.Fori(0, turns) as i:
            self.turn = i * per
            yield i
            assert self.n == start + per, (self.n - start, per)
            self.turn = None
        self.n += per * (turns - 1)


def block_kernel(nc, dr, out, stop_at=None):
    with ExitStack() as ctx:
        def sb(name, n):
            return ctx.enter_context(nc.sbuf_tensor(name, [P, n], F32))

        def sem(name):
            return ctx.enter_context(nc.semaphore(name))

        def tiles(ap, n):
            return ap.rearrange("p (a n) -> p a n", n=n)

        h_buf = sb("h_buf", KD * T)
        with ExitStack() as overlay:
            x_hi_buf, x_lo_buf = (overlay.enter_context(nc.sbuf_tensor(n, [P, KD * T], F32R)) for n in ("x_hi", "x_lo"))
        xn_buf = sb("xn_buf", KD * T)
        mixed_buf = sb("mixed_buf", KD * T)
        stage_buf = sb("stage_buf", 2 * UNIT)
        w_hi_buf, w_lo_buf = (ctx.enter_context(nc.sbuf_tensor(n, [P, 2 * UNIT], F32R)) for n in ("w_hi", "w_lo"))
        with ExitStack() as overlay:
            hid_buf = overlay.enter_context(nc.sbuf_tensor("hid", [P, 2 * NF * T], F32R))
        big = sb("big", 16384)
        with ExitStack() as overlay:
            o_hi, o_lo, send = (overlay.enter_context(nc.sbuf_tensor(n, [P, w], F32R))
                                for n, w in (("o_hi", 2 * D), ("o_lo", 2 * D), ("send", 2 * T)))
        s_buf = sb("s_buf", NS * SCMAX)
        pt_buf = sb("pt_buf", 2 * SCMAX)
        assert 2 * NF * T <= 16384 + NS * SCMAX + 2 * SCMAX
        mask = sb("mask", 3072)
        rot = sb("rot", 2 * T)
        eye = sb("eye", P)
        ones = sb("ones", P)
        eps = sb("eps", 1)
        sq_buf = sb("sq_buf", 2 * T)
        sil_buf = sb("sil_buf", 2 * T)
        std = sb("std", T)
        rstd = sb("rstd", T)
        tmp_buf = sb("tmp_buf", 2 * T)
        acc = sb("acc", T)
        small = sb("small", 512)
        cols = sb("cols", NCOL)
        mod = sb("mod", 64)
        ps_t = ctx.enter_context(nc.psum_tensor("ps", [P, 8 * T], F32))

        h, xn, mixed = tiles(h_buf[:, :], T), tiles(xn_buf[:, :], T), tiles(mixed_buf[:, :], T)
        x_hi, x_lo = tiles(x_hi_buf[:, :], T), tiles(x_lo_buf[:, :], T)
        stage, w_hi, w_lo = ([b[:, s * UNIT:(s + 1) * UNIT] for s in range(2)] for b in (stage_buf, w_hi_buf, w_lo_buf))
        hid_hi, hid_lo = tiles(hid_buf[:, 0:NF * T], T), tiles(hid_buf[:, NF * T:2 * NF * T], T)
        p_buf, p_hi, p_lo = big[:, 8 * T:10 * T], hid_buf[:, 10 * T:12 * T], hid_buf[:, 12 * T:14 * T]
        sq, sil, tmp = tiles(sq_buf[:, :], T), tiles(sil_buf[:, :], T), tiles(tmp_buf[:, :], T)
        ps = tiles(ps_t[:, :], T)
        ada_w = [xn_buf[:, s * UNIT:(s + 1) * UNIT] for s in range(4)]
        ADA, ADA_S = 48, len(ada_w)
        ADA_UNITS = {"mix_0": range(0, 32), "mix_1": range(32, ADA)}
        ADA_G = len(ADA_UNITS["mix_0"]) // 4
        ada_acc = [b[:, j, :] for b in (sq, sil, tmp) for j in range(2)] + [std[:, :], rstd[:, :]]
        cos, sin = rot[:, 0:T], rot[:, T:2 * T]

        def col(name):
            a, n = COLS[name]
            return cols[:, a:a + n]

        x_in = [sem(f"x_in{s}") for s in range(2)]
        consts_in = sem("consts_in")
        set_up = sem("set_up")
        loaded = [sem(f"loaded{s}") for s in range(2)]
        upper_done = sem("upper_done")
        parted = sem("parted")
        units_done = sem("units_done")
        evac_done = sem("evac_done")
        h_ready = sem("h_ready")
        acc_ready = sem("acc_ready")
        sum_ready = sem("sum_ready")
        sq_ready = sem("sq_ready")
        sq_used = sem("sq_used")
        std_ready = sem("std_ready")
        xn_ready = sem("xn_ready")
        x_hi_ready = sem("x_hi_ready")
        x_ready = sem("x_ready")
        hid_hi_ready = sem("hid_hi_ready")
        hid_ready = sem("hid_ready")
        ada = {n: sem(f"ada_{n}") for n in ("c", "used", "ps", "read")}
        ada_in = [sem(f"ada_in{s}") for s in range(ADA_S)]
        dve_own = sem("dve_own")
        act_own = sem("act_own")
        pool_own = sem("pool_own")
        out_done = sem("out_done")

        block = ctx.enter_context(nc.Block())

        NORM_N = {n: k for k, n in enumerate(NORMS)}
        TILEWISE = ["ffn1_0", "ffn1_1", "first", "norm1", "final"]
        SUM_N = {n: k for k, n in enumerate(n for n in NORMS if n not in TILEWISE)}
        SUM_BANK = {n: 0 if n in TILEWISE else 7 for n in NORMS}
        TILE_N = {n: KD * k for k, n in enumerate(TILEWISE)}
        H_STAGES = ["ffn1_0", "mix_0", "ffn2_0", "ple_0", "ffn1_1", "mix_1", "ffn2_1", "ple_1", "first", "mix_2", "moe"]
        H_AT = {n: KD * (k + 1) for k, n in enumerate(H_STAGES)}
        NORM_H = {"ffn1_0": 0, "mix_0": 8, "ffn2_0": 16, "ple_0": 24, "ffn1_1": 32, "mix_1": 40, "ffn2_1": 48,
                  "ple_1": 56, "first": 64, "norm1": 72, "norm2": 80, "final": 88}
        HID_AT = {f"ffn{k + 1}_{l}": NF * (2 * l + k) for l in range(2) for k in range(2)}

        def plan_a():
            q, kk = tiles(big[:, 0:12 * T], T), tiles(big[:, 12 * T:20 * T], T)
            v = tiles(big[:, 20 * T:20 * T + 4 * D], D)
            units = []
            for p in range(6):
                for hf in range(2):
                    r = slice(64 * hf, 64 * hf + 64)
                    for t in range(TT):
                        lo, hi = max(t - 1, 0), min(t + 2, TT)
                        n = (hi - lo) * P
                        a = (lo - t + 1) * P
                        kv = 2 * (p // 3) + hf
                        units.append(dict(
                            segs=[(q[r, p, t * P:t * P + P], kk[r, p // 3, lo * P:hi * P], mask[:, a:a + n], 0, n)],
                            groups=[(0, n)], sink=A_PAIRS[p][hf],
                            chunks=[(0, c * P, P, v[:, lo + c, kv * HD:kv * HD + HD]) for c in range(hi - lo)],
                            pair=p, out=p, half=hf, t=t, last=hf == 1 and t == TT - 1, first=hf == 0 and t == 0))
            return units

        def plan_b():
            q, kk = tiles(big[:, 0:12 * T], T), tiles(big[:, 12 * T:20 * T], T)
            v = tiles(big[:, 20 * T:20 * T + 4 * D], D)
            units = []
            for p in range(2):
                for hf in range(2):
                    r = slice(64 * hf, 64 * hf + 64)
                    for t in range(TT):
                        segs, chunks, at = [], [], 0
                        for g in range(3):
                            lo, hi = (max(t - 1, 0), min(t + 2, TT)) if g == 0 else (0, TT)
                            n = (hi - lo) * P
                            m0 = 384 + (lo - t + 1) * P if g == 0 else 768 + 896 * (g - 1) + 384 - t * P
                            segs.append((q[r, 6 + 2 * g + p, t * P:t * P + P], kk[r, 2 + 2 * g + p, lo * P:hi * P],
                                         mask[:, m0:m0 + n], at, n))
                            c0 = 256 + (4 * g + 2 * p + hf) * HD
                            chunks += [(0, at + c * P, P, v[:, lo + c, c0:c0 + HD]) for c in range(hi - lo)]
                            at += n
                        units.append(dict(segs=segs, groups=[(0, at)], sink=None, chunks=chunks, pair=p, out=6 + p,
                                          half=hf, t=t, last=hf == 1 and t == TT - 1, first=hf == 0 and t == 0))
            return units

        def plan_c():
            q, kk = tiles(big[:, 0:8 * T], T), tiles(big[:, 8 * T:16 * T], T)
            v = tiles(big[:, 16 * T:16 * T + 4 * D], D)
            units = []
            for p in range(8):
                for hf in range(2):
                    r = slice(64 * hf, 64 * hf + 64)
                    for t in range(TT):
                        a = 64 + 1024 * hf + (7 - 2 * t) * 64
                        units.append(dict(
                            segs=[(q[r, p, t * P:t * P + P], kk[r, p, :], mask[:, a:a + T], 0, T)],
                            groups=[(0, T)], sink=None,
                            chunks=[(0, c * P, P, v[:, c, (2 * p + hf) * HD:(2 * p + hf) * HD + HD]) for c in range(TT)],
                            pair=p, out=p, half=hf, t=t, last=hf == 1 and t == TT - 1, first=hf == 0 and t == 0))
            return units

        R_HQ, R_HF, R_HG = 0, 4 * T, 8 * T
        R_NQ, R_NR, R_KCV, R_KSW = 12 * T, 16 * T, 20 * T, 22 * T
        R_VI = 24 * T
        R_VSW = R_VI + TT * T
        R_GATE = R_VSW + TT * 256
        R_KCMP = R_GATE + TT * 24
        R_VCMP = R_KCMP + 32
        gates = tiles(big[:, R_GATE:R_GATE + TT * 24], 24)
        kcmp = big[:, R_KCMP:R_KCMP + 32]
        vcmp = tiles(big[:, R_VCMP:R_VCMP + 2 * HD], HD)

        def plan_n():
            q, qr = tiles(big[:, R_NQ:R_NR], T), tiles(big[:, R_NR:R_KCV], T)
            kk = tiles(big[:, R_KSW:R_VI], T)
            v = tiles(big[:, R_VSW:R_GATE], 256)
            units = []
            for p in range(4):
                for hf in range(2):
                    r = slice(64 * hf, 64 * hf + 64)
                    for t in range(TT):
                        n = (t + 1) * P
                        segs = [(qr[r, p, t * P:t * P + P], kk[r, 0, 0:n], mask[:, 384 - t * P:512], 0, n),
                                (qr[r, p, t * P:t * P + P], kk[r, 1, 0:n], mask[:, 384 - t * P:512], n, n),
                                (q[r, p, t * P:t * P + P], kcmp[r, :], mask[:, 512 + 32 * t:544 + 32 * t], 2 * n, 32)]
                        chunks = [(g, g * n + c * P, P, v[:, c, g * P + hf * HD:g * P + hf * HD + HD])
                                  for g in range(2) for c in range(t + 1)]
                        chunks.append((2, 2 * n, 32, vcmp[0:32, hf, :]))
                        units.append(dict(segs=segs, groups=[(0, n), (n, n), (2 * n, 32)], sink=None, chunks=chunks,
                                          gate=3 * N_PAIRS[p][hf], pair=p, out=4 + p, half=hf, t=t,
                                          last=hf == 1 and t == TT - 1, first=hf == 0 and t == 0))
            return units

        ATT = {}
        for name, units, sc_banks, pt_banks in (("a", plan_a(), (0, 1, 2), (3, 4)), ("b", plan_b(), (0,), (3,)),
                                                ("c", plan_c(), (0, 1, 2), (3, 4)), ("n", plan_n(), (0,), (3,))):
            ATT[name] = dict(
                units=units, sc=sc_banks, pt=pt_banks,
                mask_in=sem(f"{name}_mask_in"),
                qkv=sem(f"{name}_qkv"),
                sc_ready=sem(f"{name}_sc_ready"),
                sc_read=sem(f"{name}_sc_read"),
                negm=sem(f"{name}_negm"),
                exps=sem(f"{name}_exps"),
                probs=sem(f"{name}_probs"),
                pt_ready=sem(f"{name}_pt_ready"),
                pts=sem(f"{name}_pts"),
                pv=sem(f"{name}_pv"),
                out=sem(f"{name}_out"),
            )
        c_bias_in = [sem(f"c_bias_in{s}") for s in range(2)]
        c_bias = [sem(f"c_bias{s}") for s in range(2)]
        mx = small[:, 0:8]
        negm = small[:, 8:16]
        den = small[:, 16:24]
        es = small[:, 24:26]
        fac = small[:, 32:40]
        rden = small[:, 40:48]

        p_in, p_upper, p_parted = sem("p_in"), sem("p_upper"), sem("p_parted")
        hg = {n: sem(f"hg_{n}") for n in ("mask_in", "sig", "ln_in", "ln", "diff", "e", "ql", "kl", "qk", "mul", "pv",
                                          "ex", "kx", "x_ps", "x_sb", "o_sq", "o_sum", "o_std", "o_out", "lbe")}
        cm = {n: sem(f"cm_{n}") for n in ("blk", "g1", "th", "hid", "kv")}
        rt = {n: sem(f"rt_{n}") for n in ("lg", "sig")}
        moe = {n: sem(f"moe_{n}") for n in ("sil", "hid", "dn", "acc")}
        tab = {n: sem(f"tab_{n}") for n in (
            "const_in",
            "tok_ps", "tok_sb", "tok_out",
            "sel", "rank",
            "pairs",
            "filled",
            "in",
            "blocks", "blocks_out", "ready")}
        gathered = [sem(f"gathered{s}") for s in range(2)]
        raw_in = [sem(f"raw_in{j}") for j in range(3)]
        raw_upper = [sem(f"raw_upper{j}") for j in range(3)]
        raw_parted = [sem(f"raw_parted{j}") for j in range(3)]
        bk = {n: sem(f"bk_{n}") for n in (
            "staged",
            "asked",
            "tx", "xt",
            "xh",
            "gua",
            "gu",
            "sil", "hid",
            "ht", "hth", "hts",
            "dn",
            "oh", "ol",
            "sum",
            "added")}
        RAW = 2048
        raw = [big[:, 12288:14336], big[:, 14336:16384], xn_buf[:, 0:RAW]]
        raw_hi = [hid_buf[:, 2 * j * RAW:(2 * j + 1) * RAW] for j in range(3)]
        raw_lo = [hid_buf[:, (2 * j + 1) * RAW:(2 * j + 2) * RAW] for j in range(3)]
        xg = [xn_buf[:, RAW + s * D:RAW + (s + 1) * D] for s in range(2)]
        xgt_hi, xgt_lo = ([tiles(b[:, s * D:(s + 1) * D], P) for s in range(2)] for b in (w_hi_buf, w_lo_buf))
        ht_at = 16384 + 4 * D + 2 * T
        hid_t_hi, hid_t_lo = ([tiles(hid_buf[:, ht_at + (2 * j + s) * EXP_H:ht_at + (2 * j + s + 1) * EXP_H], P)
                               for s in range(2)] for j in range(2))
        tok = big[:, 12288:16384].rearrange("p (t n) -> p t n", n=D)
        hid_b = [stage_buf[:, s * EXP_H:(s + 1) * EXP_H] for s in range(2)]
        sil_b = [stage_buf[:, 1024 + s * EXP_H:1024 + (s + 1) * EXP_H] for s in range(2)]
        slot_r, slot_b, slot_w = (pt_buf[:, 1920 + 32 * j:1952 + 32 * j] for j in range(3))
        before, iota_t = mask[:, 0:P], mask[:, P:P + T]
        iota_e2 = mask[:, 640:704]
        slot_no, tok_no = mask[:, 704:705], mask[:, 705:709]
        BLOCKS = MAX_BLOCKS + 4
        tab_f, tab_w = mask[:, 1024:1024 + BLOCKS], mask[:, 1024 + BLOCKS:1024 + 2 * BLOCKS]
        at_r = [mask[:, 1408 + P * j:1408 + P * (j + 1)] for j in range(4)]
        at_b = [mask[:, 1920 + 2 * BLOCKS * j:1920 + 2 * BLOCKS * (j + 1)] for j in range(4)]
        idx = mask[:, 1400:1402].bitcast(I32)
        n_turns = mask[:, 1404:1405].bitcast(I32)
        block_e = mask[:, 1405:1406].bitcast(I32)

        def u(phase):
            return BASE[phase][0]

        hg_e = [tmp[:, 0, :], tmp[:, 1, :], s_buf[:, 5 * T:6 * T], s_buf[:, 6 * T:7 * T]]
        hg_kl, hg_ql = ([s_buf[:, (j + s) * T:(j + s + 1) * T] for s in range(2)] for j in (0, 2))
        hg_masked = [tiles(b[:, 4 * T:5 * T], P) for b in (s_buf, pt_buf)]
        X_PAIRS = [(a, b) for a in range(TT) for b in range(a + 1, TT)]

        STAGES = ["ffn1_0", "mix_0", "ffn2_0", "ple_0", "ffn1_1", "mix_1", "ffn2_1", "ple_1", "mix_2", "moe"]
        if stop_at is not None:
            STAGES = STAGES[:STAGES.index(stop_at) + 1]
        ORDER = [ph for st in STAGES for ph in STAGE_PHASES[st]]

        def each_unit(eng, phase, part, work=None):
            n = BASE[phase][1]
            step = 6 if phase.startswith("down") else 2
            then = ORDER[ORDER.index(phase) + 1:][:1]
            ahead = bool(then) and then[0] not in WHOLE

            def floats(j):
                return DOWN[j % 3] * P if phase.startswith("down") else UNIT

            def turn(i, last):
                for j in range(step):
                    if not last or j + 2 < step:
                        part(phase, i, step, j + 2, floats((j + 2) % step))
                    if work is not None:
                        work(i, j)

            turns = n // step if ahead else n // step - 1
            if turns > 1:
                with eng.Fori(0, turns) as i:
                    turn(i, False)
            elif turns == 1:
                turn(0, False)
            if not ahead:
                turn(n // step - 1, True)

        @block.sync
        def _(sp):
            for s in range(2):
                c = slice(s * KD // 2 * T, (s + 1) * KD // 2 * T)
                sp.dma_start(h_buf[:, c], dr["xT"][:, c]).then_inc(x_in[s], 16)

            def load(phase, turn, s):
                sp.dma_start(stage[s], dr[phase][bass.ds(2 * turn + s, 1), :, :].rearrange("a p n -> p (a n)")
                             ).then_inc(loaded[s], 16)

            def first_two(phase):
                base, cut = BASE[phase][0], CUT[phase]
                for s in range(2):
                    if phase == "out_2":
                        sp.wait_ge(units_done, base + s - 1)
                    elif base:
                        sp.wait_ge(parted, cut + s - 1)
                    load(phase, 0, s)

            def others(phase):
                (base, n), cut = BASE[phase], CUT[phase]
                if n > 2:
                    with sp.Fori(1, n // 2) as i:
                        for s in range(2):
                            if phase in WHOLE:
                                sp.wait_ge(units_done, i * 2 + (base + s - 1))
                            else:
                                sp.wait_ge(parted, i * 2 + (cut + s - 1))
                            load(phase, i, s)

            def stream(phase):
                first_two(phase)
                others(phase)

            def load_ada(m, first):
                if not first:
                    sp.wait_ge(ada["used"], m + 1 - ADA_S)
                sp.dma_start(ada_w[m % ADA_S], dr["ada"][m, :, :]).then_inc(ada_in[m % ADA_S], 16)

            def stream_down(phase):
                with sp.Fori(0, KD // 2) as i:
                    for j in range(6):
                        a = sum(DOWN[:j % 3]) * P
                        n = DOWN[j % 3] * P
                        sp.wait_ge(parted, i * 6 + (CUT[phase] + j - 1))
                        sp.dma_start(stage[j % 2][:, 0:n], dr[phase][bass.ds(2 * i + j // 3, 1), :, a:a + n].rearrange(
                            "a p n -> p (a n)")).then_inc(loaded[j % 2], 16)

            def att_mask(name, ap, n, after=None):
                if after is not None:
                    sp.wait_ge(*after)
                sp.dma_start(mask[:, 0:n], dr[ap]).then_inc(ATT[name]["mask_in"], 16)

            for st in STAGES:
                if st.startswith("ffn"):
                    l, k = st[-1], int(st[3]) - 1
                    stream(f"gu_{l}_{k}")
                    stream_down(f"down_{l}_{k}")
                elif st.startswith("ple"):
                    l = st[-1]
                    sp.wait_ge(h_ready, NORM_H[f"ple_{l}"])
                    sp.dma_start(p_buf, dr["pT"][int(l), :, :]).then_inc(p_in, 16)
                    stream(f"pg_{l}")
                    stream(f"pp_{l}")
                elif st == "mix_0":
                    att_mask("a", "mask_ab", 2560)
                    stream("in_ab")
                    stream("v_ab")
                    first_two("out_ab")
                    sp.wait_ge(units_done, u("v_ab") + 8)
                    for m in ADA_UNITS[st]:
                        load_ada(m, m < ADA_S)
                    others("out_ab")
                elif st == "mix_1":
                    att_mask("c", "mask_c", 64, (h_ready, H_AT["mix_0"]))
                    stream("in_c")
                    stream("v_c")
                    first_two("out_c")
                    sp.wait_ge(units_done, u("v_c") + 8)
                    for hd in range(16):
                        if hd >= 2:
                            sp.wait_ge(ATT["c"]["sc_read"], TT * (hd - 1))
                        b = 64 + 1024 * (hd % 2)
                        for r in range(2):
                            sp.dma_start(mask[64 * r:64 * r + 64, b + 64 * r:b + 64 * r + 960],
                                         dr["rpb"][hd, :, :]).then_inc(c_bias_in[hd % 2], 16)
                        load_ada(ADA_UNITS[st][hd], False)
                    others("out_c")
                elif st == "mix_2":
                    stream("in_2")
                    stream("tok_2")
                    sp.wait_ge(h_ready, H_AT["mix_1"])
                    sp.dma_start(mask[:, 0:1024], dr["mask_h"]).then_inc(hg["mask_in"], 16)
                    stream("cmp")
                    att_mask("n", "mask_n", 641, (hg["o_out"], 4))
                    stream("out_2")
                elif st == "moe":
                    first_two("shared")
                    sp.wait_ge(h_ready, H_AT["mix_2"])
                    sp.dma_start(mask[:, 0:709], dr["mask_m"]).then_inc(tab["const_in"], 16)
                    others("shared")
                    sp.wait_ge(tab["tok_sb"], TT)
                    sp.dma_start(dr["tok"].rearrange("(t p) n -> p t n", p=P), tok).then_inc(tab["tok_out"], 16)
                    sp.wait_ge(tab["blocks"], 1)
                    sp.dma_start(dr["block_e"].rearrange("a p -> p a"), block_e).then_inc(tab["blocks_out"], 16)
                    sp.wait_ge(tab["blocks_out"], 16)
                    turns = sp.value_load(n_turns[0:1, 0:1], min_val=1, max_val=MAX_BLOCKS // 2)

                    def load_raw(e, j):
                        src = dr["exp_dn" if j == 2 else "exp_gu"][bass.ds(e, 1), :, :].rearrange("a p n -> p (a n)")
                        sp.dma_start(raw[j], src if j == 2 else src[:, j * RAW:(j + 1) * RAW]).then_inc(raw_in[j], 16)

                    def expert_of(b):
                        return sp.value_load(dr["block_e"][0:1, b], min_val=0, max_val=N_EXP - 1)

                    sp.wait_ge(tab["tok_out"], 16)
                    sp.wait_ge(units_done, u("shared") + 4)
                    first, second = expert_of(slice(0, 1)), expert_of(slice(1, 2))
                    for j in range(3):
                        load_raw(first, j)
                    for j in range(2):
                        sp.wait_ge(raw_parted[j], j + 1)
                        load_raw(second, j)
                    with sp.Fori(0, turns) as i:
                        for s in range(2):
                            e1, e2 = expert_of(bass.ds(i * 2 + (s + 1), 1)), expert_of(bass.ds(i * 2 + (s + 2), 1))
                            for j in range(2):
                                sp.wait_ge(raw_parted[j], i * 2 + (s + 2) if j == 0 else i * 4 + (2 * s + 4))
                                load_raw(e2, j)
                            sp.wait_ge(raw_parted[2], i * 2 + (s + 1))
                            load_raw(e1, 2)
            if stop_at is None:
                for k in range(0, KD, 2):
                    sp.wait_ge(xn_ready, KD * (len(NORMS) - 1) + k + 2)
                    sp.dma_start(out[:, k * T:(k + 2) * T], mixed_buf[:, k * T:(k + 2) * T]).then_inc(out_done, 16)
                sp.wait_ge(out_done, 16 * (KD // 2))
            else:
                sp.wait_ge(h_ready, H_AT[stop_at])
                sp.dma_start(out, h_buf[:, :]).then_inc(out_done, 16)
                sp.wait_ge(out_done, 16)

        @block.tensor
        def _(pe):
            pe.wait_ge(set_up, 1)
            pe.wait_ge(consts_in, 48)

            def unit_waits(phase, turn, j):
                pe.wait_ge(parted, turn * 2 + (CUT[phase] + j + 1))
                pe.wait_ge(evac_done, turn * 2 + (BASE[phase][0] + j + 1))

            @contextmanager
            def turns(n):
                if n == 1:
                    yield 0
                else:
                    with pe.Fori(0, n) as i:
                        yield i

            def norm_sum(name):
                if name in TILEWISE:
                    for k in range(KD):
                        pe.wait_ge(sq_ready, TILE_N[name] + k + 1)
                        nc.tensor.matmul(ps[:, SUM_BANK[name], :], ones[:, :], sq[:, k % 2, :], start=(k == 0), stop=(k == KD - 1)
                                         ).then_inc(sq_used, 1)
                else:
                    pe.wait_ge(acc_ready, SUM_N[name] + 1)
                    nc.tensor.matmul(ps[:, SUM_BANK[name], :], ones[:, :], acc[:, :], start=True, stop=True).then_inc(sum_ready, 1)

            def three(o, a_hi, a_lo, b_hi, b_lo, start, stop):
                nc.tensor.matmul(o, a_hi, b_hi, start=start, stop=False)
                nc.tensor.matmul(o, a_hi, b_lo, start=False, stop=False)
                return nc.tensor.matmul(o, a_lo, b_hi, start=False, stop=stop)

            def dense(phase, operand):
                for s in range(2):
                    unit_waits(phase, 0, s)
                    wh, wl = tiles(w_hi[s], P), tiles(w_lo[s], P)
                    for k in range(KD):
                        if s == 0:
                            pe.wait_ge(x_hi_ready, PART_AT[operand] + k + 1)
                        nc.tensor.matmul(ps[:, s, :], wh[:, k, :], x_hi[:, k, :], start=(k == 0), stop=False)
                        nc.tensor.matmul(ps[:, s, :], wl[:, k, :], x_hi[:, k, :], start=False, stop=False)
                for s in range(2):
                    for k in range(KD):
                        if s == 0:
                            pe.wait_ge(x_ready, PART_AT[operand] + k + 1)
                        last = nc.tensor.matmul(ps[:, s, :], tiles(w_hi[s], P)[:, k, :], x_lo[:, k, :],
                                                start=False, stop=(k == KD - 1))
                    last.then_inc(units_done, 1)
                with pe.Fori(1, BASE[phase][1] // 2) as i:
                    for s in range(2):
                        unit_waits(phase, i, s)
                        wh, wl = tiles(w_hi[s], P), tiles(w_lo[s], P)
                        for k in range(KD):
                            last = three(ps[:, s, :], wh[:, k, :], wl[:, k, :], x_hi[:, k, :], x_lo[:, k, :],
                                         k == 0, k == KD - 1)
                        last.then_inc(units_done, 1)

            def token_major(phase):
                U, units = BASE[phase]
                for c in range(units // 2):
                    pe.wait_ge(evac_done, U + 2 * c)
                    for s in range(2):
                        pe.wait_ge(parted, CUT[phase] + 2 * c + s + 1)
                        wh, wl = tiles(w_hi[s], 256), tiles(w_lo[s], 256)
                        for t in range(TT):
                            for kk in range(KD // 2):
                                k, tk = 4 * s + kk, slice(t * P, t * P + P)
                                last = three(ps[:, 4 * ((c + 1) % 2) + t, 0:256], x_hi[:, k, tk], x_lo[:, k, tk],
                                             wh[:, kk, :], wl[:, kk, :], k == 0, k == KD - 1)
                        last.then_inc(units_done, 1)

            def ada_group(g):
                pe.wait_ge(ada["used"], 4 * g + 4)
                for m in range(4):
                    last = nc.tensor.matmul(ps[:, 5, 4 * g + m:4 * g + m + 1], ada_acc[g % len(ada_acc)][:, m * P:m * P + P],
                                            ones[:, 0:1], start=True, stop=True)
                last.then_inc(ada["ps"], 1)

            def ffn(st):
                l, k = st[-1], int(st[3]) - 1
                norm_sum(st)
                dense(f"gu_{l}_{k}", st)
                phase = f"down_{l}_{k}"
                U = u(phase)
                with turns(KD // 2) as i:
                    for j in range(6):
                        m, q = j // 3, j % 3
                        pe.wait_ge(parted, i * 6 + (CUT[phase] + j + 1))
                        if q == 0:
                            pe.wait_ge(evac_done, i * 6 + (U + 3 * m - 1))
                        wh, wl = tiles(w_hi[j % 2], P), tiles(w_lo[j % 2], P)
                        f0, f1 = sum(DOWN[:q]), sum(DOWN[:q + 1])
                        pe.wait_ge(hid_ready, HID_AT[st] + f1)
                        for f in range(f0, f1):
                            last = three(ps[:, 2 + m, :], wh[:, f - f0, :], wl[:, f - f0, :], hid_hi[:, f, :], hid_lo[:, f, :],
                                         f == 0, f == NF - 1)
                        last.then_inc(units_done, 1)

            def attention(name):
                a = ATT[name]
                units, ns, np_ = a["units"], len(a["sc"]), len(a["pt"])
                pe.wait_ge(a["qkv"], 1)
                for i in range(len(units) + 3):
                    if i < len(units):
                        if i >= ns:
                            pe.wait_ge(a["sc_read"], i - ns + 1)
                        for g, (q, kk, _, _, n) in enumerate(units[i]["segs"]):
                            last = nc.tensor.matmul(ps[:, a["sc"][i % ns] + g, 0:n], q, kk, start=True, stop=True)
                        last.then_inc(a["sc_ready"], 1)
                    if 2 <= i <= len(units) + 1:
                        j = i - 2
                        un = units[j]
                        pe.wait_ge(a["probs"], j + 1)
                        if j >= np_:
                            pe.wait_ge(a["pts"], j - np_ + 1)
                        for c, (g, c0, n, _) in enumerate(un["chunks"]):
                            b = a["pt"][j % np_] + c // 4
                            last = nc.tensor.transpose(ps[0:n, b, (c % 4) * P:(c % 4) * P + P],
                                                       s_buf[:, (j % NS) * SCMAX + c0:(j % NS) * SCMAX + c0 + n], eye[:, :])
                        last.then_inc(a["pt_ready"], 1)
                    if i >= 3:
                        j = i - 3
                        un = units[j]
                        pe.wait_ge(a["pts"], j + 1)
                        if un["first"] and un["pair"] >= 2:
                            pe.wait_ge(a["out"], un["pair"] - 1)
                        o = ps[64 * un["half"]:64 * un["half"] + 64, 6 + un["pair"] % 2, un["t"] * P:un["t"] * P + P]
                        for c, (_, _, n, v) in enumerate(un["chunks"]):
                            b0 = (j % 2) * SCMAX + c * P
                            last = nc.tensor.matmul(o, v, pt_buf[0:n, b0:b0 + P],
                                                    start=(c == 0), stop=(c == len(un["chunks"]) - 1))
                        last.then_inc(a["pv"], 1)

            def hgrn():
                q, kk = tiles(big[:, R_HQ:R_HF], T), tiles(big[:, R_HF:R_HG], T)
                v = tiles(big[:, R_VI:R_VSW], T)
                def values(i):
                    hd, lv = i // 8, i % 8
                    pe.wait_ge(hg["mul"], i + 1)
                    if lv == 0 and hd >= 2:
                        pe.wait_ge(hg["o_out"], hd - 1)
                    for b in range(TT):
                        last = nc.tensor.matmul(ps[:, 4 + hd % 2, b * P:b * P + P], v[:, b, hd * P:hd * P + P],
                                                hg_masked[i % 2][:, b, :], start=(lv == 0 and b == 0),
                                                stop=(lv == 7 and b == TT - 1))
                    last.then_inc(hg["pv"], 1)

                for i in range(33):
                    hd, lv = i // 8, i % 8
                    if i < 32:
                        if lv < 7:
                            pe.wait_ge(hg["ql"], 7 * hd + lv + 1)
                            pe.wait_ge(hg["kl"], 7 * hd + lv + 1)
                        if i >= 2:
                            pe.wait_ge(hg["mul"], i - 1)
                        for t in range(TT):
                            c = slice(t * P, t * P + P)
                            kl, ql = (kk[:, hd, c], q[:, hd, c]) if lv == 7 else (hg_kl[i % 2][:, c], hg_ql[i % 2][:, c])
                            last = nc.tensor.matmul(ps[:, i % 2, c], kl, ql, start=True, stop=True)
                        last.then_inc(hg["qk"], 1)
                    if i >= 1:
                        values(i - 1)
                    if lv == 3:
                        pe.wait_ge(hg["kx"], hd + 1)
                        if hd >= 1:
                            pe.wait_ge(hg["x_sb"], hd)
                        for n, (a, b) in enumerate(X_PAIRS):
                            kx = pt_buf[:, (b - a) * T + a * P:(b - a) * T + a * P + P]
                            last = nc.tensor.matmul(ps[:, 2 + n // 4, (n % 4) * P:(n % 4) * P + P], kx,
                                                    pt_buf[:, b * P:b * P + P], start=True, stop=True)
                        last.then_inc(hg["x_ps"], 1)
                    if lv == 5:
                        pe.wait_ge(hg["x_sb"], hd + 1)
                        for n, (a, b) in enumerate(X_PAIRS):
                            nc.tensor.matmul(ps[:, 4 + hd % 2, b * P:b * P + P], v[:, a, hd * P:hd * P + P],
                                             xn_buf[:, n * P:n * P + P], start=False, stop=False)
                    if (lv == 2 and i > 8) or i == 32:
                        pe.wait_ge(hg["o_sq"], i // 8)
                        nc.tensor.matmul(ps[:, 6, :], ones[:, :], sq[:, 0, :], start=True, stop=True).then_inc(hg["o_sum"], 1)

            def compress():
                U = u("cmp")
                pe.wait_ge(evac_done, U + 2)
                for kv in range(2):
                    pe.wait_ge(cm["blk"], kv + 1)
                    blk = s_buf[:, kv * 1024:kv * 1024 + 992].rearrange("p (l n) -> p l n", l=16)
                    for q in range(4):
                        s = q % 2
                        pe.wait_ge(loaded[s], 16 * ((U + 4 * kv + q) // 2 + 1))
                        w = tiles(stage[s], 256)
                        for l in range(4):
                            for j in range(2):
                                last = nc.tensor.matmul(ps[:, 2 * kv + j, 0:62], w[:, l, j * P:j * P + P],
                                                        blk[:, 4 * q + l, :], start=(q == 0 and l == 0),
                                                        stop=(q == 3 and l == 3))
                        last.then_inc(units_done, 1)
                for kv in range(2):
                    pe.wait_ge(cm["hid"], kv + 1)
                    w2 = tiles(col("w2k" if kv == 0 else "w2v"), HD)
                    hb = s_buf[:, 2048 + kv * 128:2048 + kv * 128 + 124].rearrange("p (j n) -> p j n", j=2)
                    for g in range(2):
                        for j in range(2):
                            if kv == 0:
                                o, a, b = ps[64 * g:64 * g + 64, 4, 0:N_CMP], w2[:, j, :], hb[:, j, g * 31:g * 31 + 31]
                            else:
                                o, a, b = ps[0:N_CMP, 5, g * HD:g * HD + HD], hb[:, j, g * 31:g * 31 + 31], w2[:, j, :]
                            last = nc.tensor.matmul(o, a, b, start=(j == 0), stop=(j == 1))
                    last.then_inc(cm["kv"], 1)

            def router():
                for t in range(TT):
                    for k in range(KD):
                        if t == 0:
                            pe.wait_ge(x_hi_ready, PART_AT["norm2"] + k + 1)
                        last = nc.tensor.matmul(ps[:, 4, t * N_EXP:(t + 1) * N_EXP], xn[:, k, t * P:t * P + P],
                                                tiles(col("router_w"), N_EXP)[:, k, :], start=(k == 0), stop=(k == KD - 1))
                last.then_inc(rt["lg"], 1)

            def token_major_tokens():
                for t in range(TT):
                    if t >= 2:
                        pe.wait_ge(tab["tok_sb"], t - 1)
                    for k in range(KD):
                        last = nc.tensor.transpose(ps[:, 2 * (t % 2) + k // 4, (k % 4) * P:(k % 4) * P + P],
                                                   xn[:, k, t * P:t * P + P], eye[:, :])
                    last.then_inc(tab["tok_ps"], 1)

            def ranks():
                pe.wait_ge(tab["sel"], 1)
                pe.wait_ge(tab["const_in"], 16)
                sel = tiles(s_buf[:, 2560:2816], N_EXP)
                for t in range(TT):
                    for a in range(t + 1):
                        nc.tensor.matmul(ps[:, 5, t * N_EXP:(t + 1) * N_EXP], before if a == t else ones[:, :], sel[:, a, :],
                                         start=(a == 0), stop=(a == t))
                for a in range(TT):
                    last = nc.tensor.matmul(ps[:, 5, TT * N_EXP:(TT + 1) * N_EXP], ones[:, :], sel[:, a, :],
                                            start=(a == 0), stop=(a == TT - 1))
                last.then_inc(tab["rank"], 1)

            def fill_table():
                for n in range(TT * TOP_K):
                    pe.wait_ge(tab["pairs"], n + 1)
                    nc.tensor.matmul(ps[:, 6, 0:2 * BLOCKS], at_r[n % 4], at_b[n % 4], start=(n == 0),
                                     stop=(n == TT * TOP_K - 1)).then_inc(tab["filled"], 1)

            def turn_tokens(s, n):
                pe.wait_ge(gathered[s], n[0])
                if n[1] is not None:
                    pe.wait_ge(bk["xt"], n[1])
                for k in range(KD):
                    last = nc.tensor.transpose(ps[:, k // 4, (k % 4) * P:(k % 4) * P + P], xg[s][:, k * P:k * P + P], eye[:, :])
                last.then_inc(bk["tx"], 1)

            def gate_up(s, n):
                pe.wait_ge(bk["xt"], n + 1)
                for j in range(2):
                    pe.wait_ge(raw_parted[j], n + 1 if j == 0 else 2 * n + 2)
                    wh, wl = tiles(raw_hi[j], T), tiles(raw_lo[j], T)
                    for kk in range(KD // 2):
                        k = KD // 2 * j + kk
                        last = three(ps[:, 2, :], xgt_hi[s][:, k, :], xgt_lo[s][:, k, :], wh[:, kk, :], wl[:, kk, :],
                                     k == 0, k == KD - 1)
                    last.then_inc(bk["gua" if j == 0 else "gu"], 1)

            def send_two(i):
                pe.wait_ge(bk["ol"], i * 2 + 1)
                for m in range(KD):
                    pe.wait_ge(bk["added"], i * KD + (m + 1))
                    n = 0
                    for s in range(2):
                        for part in (o_hi, o_lo):
                            last = nc.tensor.matmul(ps[:, 6 + m % 2, :], part[:, s * D + m * P:s * D + m * P + P],
                                                    send[:, s * T:(s + 1) * T], start=(n == 0), stop=(n == 3))
                            n += 1
                    last.then_inc(bk["sum"], 1)

            def routed():
                pe.wait_ge(tab["ready"], 1)
                turns_n = pe.value_load(n_turns[0:1, 0:1], min_val=1, max_val=MAX_BLOCKS // 2)
                pe.sem_inc(bk["gu"], 1)
                pe.sem_inc(bk["dn"], 2)
                turn_tokens(0, (16, None))
                turn_tokens(1, (16, 1))
                gate_up(0, 0)
                with pe.Fori(0, turns_n) as i:
                    for s in range(2):
                        pe.wait_ge(bk["hid"], i * 2 + (s + 1))
                        for j in range(2):
                            last = nc.tensor.transpose(ps[:, 3, j * P:j * P + P], hid_b[s][:, j * P:j * P + P], eye[:, :])
                        last.then_inc(bk["ht"], 1)
                        gate_up(1 - s, i * 2 + (s + 1))
                        turn_tokens(s, (i * 16 + 32, i * 2 + (s + 2)))
                        pe.wait_ge(bk["hts"], i * 2 + (s + 1))
                        pe.wait_ge(raw_parted[2], i * 2 + (s + 1))
                        pe.wait_ge(bk["ol"], i * 2 + (s + 1))
                        wh, wl = tiles(raw_hi[2], D), tiles(raw_lo[2], D)
                        for n in range(2):
                            for j in range(2):
                                c = slice(n * T, (n + 1) * T)
                                last = three(ps[:, 4 + n, :], hid_t_hi[s][:, j, :], hid_t_lo[s][:, j, :],
                                             wh[:, j, c], wl[:, j, c], j == 0, j == 1)
                        last.then_inc(bk["dn"], 1)
                        if s == 0:
                            send_two(i)
                send_two(turns_n)

            def expert_gu(U, units):
                for j in units:
                    s = j % 2
                    pe.wait_ge(loaded[s], 16 * ((U + j) // 2 + 1))
                    w = tiles(stage[s], P)
                    for k in range(KD):
                        last = nc.tensor.matmul(ps[:, j, :], w[:, k, :], xn[:, k, :], start=(k == 0), stop=(k == KD - 1))
                    last.then_inc(units_done, 1)

            def expert_dn(w, m, n, hbuf):
                if n is not None:
                    pe.wait_ge(moe["acc"], n)
                for k in range(2):
                    last = nc.tensor.matmul(ps[:, 4 + m % 4, :], w[:, k, :], hbuf[:, k, :], start=(k == 0), stop=(k == 1))
                last.then_inc(moe["dn"], 1)
                return last

            for st in STAGES:
                if st.startswith("ffn"):
                    ffn(st)
                elif st.startswith("ple"):
                    l = st[-1]
                    norm_sum(st)
                    dense(f"pg_{l}", st)
                    pe.wait_ge(p_parted, int(l) + 1)
                    U = u(f"pp_{l}")
                    pe.wait_ge(evac_done, U + 2)
                    for s in range(2):
                        pe.wait_ge(parted, CUT[f"pp_{l}"] + s + 1)
                        wh, wl = tiles(w_hi[s], T), tiles(w_lo[s], T)
                        for m in range(4):
                            for k in range(2):
                                c, t = slice(m * P, m * P + P), slice(k * T, k * T + T)
                                last = three(ps[:, 4 * s + m, :], wh[:, k, c], wl[:, k, c], p_hi[:, t], p_lo[:, t],
                                             k == 0, k == 1)
                        last.then_inc(units_done, 1)
                elif st == "mix_0":
                    norm_sum(st)
                    dense("in_ab", st)
                    token_major("v_ab")
                    attention("a")
                    attention("b")
                    for g in range(ADA_G):
                        ada_group(g)
                    dense("out_ab", "out_ab")
                elif st == "mix_1":
                    norm_sum(st)
                    dense("in_c", st)
                    token_major("v_c")
                    attention("c")
                    for g in range(ADA_G, ADA // 4):
                        ada_group(g)
                    dense("out_c", "out_c")
                elif st == "mix_2":
                    norm_sum("first")
                    norm_sum("norm1")
                    dense("in_2", "norm1")
                    token_major("tok_2")
                    compress()
                    hgrn()
                    attention("n")
                    dense("out_2", "out_2")
                elif st == "moe":
                    norm_sum("norm2")
                    router()
                    token_major_tokens()
                    U = u("shared")
                    pe.wait_ge(evac_done, U + 2)
                    pe.wait_ge(tab["tok_sb"], TT)
                    expert_gu(U, range(1))
                    ranks()
                    expert_gu(U, range(1, 4))
                    fill_table()
                    hb = tiles(s_buf[:, 1536:2560], T)
                    pe.wait_ge(moe["hid"], 1)
                    for j in range(2):
                        pe.wait_ge(loaded[j], 16 * ((U + 4 + j) // 2 + 1))
                        for m in range(4):
                            w = tiles(stage[j], T)[:, :, m * P:m * P + P]
                            last = expert_dn(w, 4 * j + m, 4 * j + m - 3 if 4 * j + m >= 4 else None, hb)
                    pe.wait_ge(moe["acc"], KD)
                    routed()
                    norm_sum("final")


        @block.scalar
        def _(act):
            link = Chain(act, act_own)
            act.dma_start(cols[:, :], dr["cols"]).then_inc(consts_in, 16)
            act.dma_start(rot[:, :], dr["rot"]).then_inc(consts_in, 16)
            act.dma_start(eye[:, :], dr["eye"]).then_inc(consts_in, 16)
            act.wait_ge(set_up, 1)

            def upper(phase, turn, step, j, n=UNIT):
                U = BASE[phase][0] + j
                s = U % 2
                act.wait_ge(loaded[s], turn * (8 * step) + 16 * (U // 2 + 1))
                if U >= 2:
                    act.wait_ge(units_done, turn * step + (U - 1))
                nc.scalar.activation(w_hi[s][:, 0:n], stage[s][:, 0:n], ACT.Copy).then_inc(upper_done, 1)

            def weights(phase, work=None):
                each_unit(act, phase, upper, work)

            def squares(name, ready, n):
                for k in range(KD):
                    if ready is not None:
                        act.wait_ge(ready, n + k + 1)
                    else:
                        act.wait_ge(x_in[2 * k // KD], 16)
                    if TILE_N[name] + k >= 2:
                        act.wait_ge(sq_used, TILE_N[name] + k - 1)
                    nc.scalar.activation(sq[:, k % 2, :], h[:, k, :], ACT.Square).then_inc(sq_ready, 1)

            def norm(name, part=True, shift=None):
                if name in TILEWISE:
                    act.wait_ge(sq_used, TILE_N[name] + KD)
                else:
                    act.wait_ge(sum_ready, SUM_N[name] + 1)
                nc.scalar.activation(std[:, :], ps[:, SUM_BANK[name], :], ACT.Sqrt, bias=eps[:, 0:1], scale=1.0 / D
                                     ).then_inc(std_ready, 1)
                if part:
                    for k in range(KD):
                        operand(k, xn_ready, KD * NORM_N[name] + k + 1, shift=shift)

            def operand(k, *ready, shift=None):
                act.wait_ge(*ready)
                if shift is None:
                    ins = nc.scalar.activation(x_hi[:, k, :], mixed[:, k, :], ACT.Copy)
                else:
                    ins = nc.scalar.activation(x_hi[:, k, :], mixed[:, k, :], ACT.Identity, bias=shift[:, k:k + 1])
                ins.then_inc(x_hi_ready, 1)

            def ffn(st):
                norm(st)
                l, k = st[-1], int(st[3]) - 1
                U = u(f"gu_{l}_{k}")

                def work(i, j):
                    act.wait_ge(units_done, i * 2 + (U + j + 1))
                    if j == 0:
                        act.wait_ge(evac_done, i * 2 + (U + 2))
                        nc.scalar.activation(sil[:, 0, :], ps[:, 0, :], ACT.Silu).then_inc(evac_done, 1)
                    else:
                        act.wait_ge(evac_done, i * 2 + (U + 4))
                        nc.scalar.activation(hid_buf[:, bass.ds(i * T, T)], tmp[:, 0, :], ACT.Copy).then_inc(hid_hi_ready, 1)

                weights(f"gu_{l}_{k}", work)
                weights(f"down_{l}_{k}")

            def attention(name):
                a = ATT[name]
                units, np_ = a["units"], len(a["pt"])
                for i in range(len(units) + 2):
                    if i < len(units):
                        un, b = units[i], i % 2
                        act.wait_ge(a["negm"], i + 1)
                        if i >= 2:
                            act.wait_ge(a["probs"], i - 1)
                        if un["sink"] is not None:
                            nc.scalar.activation(es[:, b:b + 1], negm[:, 4 * b:4 * b + 1], ACT.Exp,
                                                 bias=col("sink")[:, un["sink"]:un["sink"] + 1])
                        for g, (c0, n) in enumerate(un["groups"]):
                            p = s_buf[:, (i % NS) * SCMAX + c0:(i % NS) * SCMAX + c0 + n]
                            last = nc.scalar.activation(p, p, ACT.Exp, bias=negm[:, 4 * b + g:4 * b + g + 1],
                                                        accum_out=den[:, 4 * b + g:4 * b + g + 1])
                        last.then_inc(a["exps"], 1)
                    if i >= 2:
                        j = i - 2
                        un, b = units[j], j % 2
                        act.wait_ge(a["pt_ready"], j + 1)
                        if j >= 2:
                            act.wait_ge(a["pv"], j - 1)
                        full = sum(c[2] == P for c in un["chunks"])
                        bank = a["pt"][j % np_]
                        src = ps_t[:, bank * T:bank * T + full * P]
                        last = nc.scalar.activation(pt_buf[:, b * SCMAX:b * SCMAX + full * P], src, ACT.Copy)
                        if full < len(un["chunks"]):
                            n = un["chunks"][-1][2]
                            last = nc.scalar.activation(
                                pt_buf[0:n, b * SCMAX + full * P:b * SCMAX + full * P + P],
                                ps_t[0:n, bank * T + full * P:bank * T + full * P + P], ACT.Copy)
                        last.then_inc(a["pts"], 1)

            def hgrn_gates():
                z = big[:, R_HF:R_HG]
                act.wait_ge(evac_done, u("in_2") + 2 + 12)
                nc.scalar.activation(z, z, ACT.Sigmoid).then_inc(hg["sig"], 1)
                nc.scalar.activation(big[:, R_HG:R_NQ], big[:, R_HG:R_NQ], ACT.Silu).then_inc(hg["sig"], 1)
                gt = big[:, R_GATE:R_GATE + TT * 24]
                act.wait_ge(evac_done, u("tok_2") + 2 + 8)
                link(nc.scalar.activation(gt, gt, ACT.Sigmoid))
                act.wait_ge(hg["ln_in"], 1)
                nc.scalar.activation(xn_buf[:, 4 * T:8 * T], z, ACT.Ln).then_inc(hg["ln"], 1)
            def hgrn():
                def head_norm(hd):
                    act.wait_ge(hg["pv"], 8 * (hd + 1))
                    nc.scalar.activation(sq[:, 0, :], ps[:, 4 + hd % 2, :], ACT.Square).then_inc(hg["o_sq"], 1)
                    act.wait_ge(hg["o_sum"], hd + 1)
                    nc.scalar.activation(std[:, :], ps[:, 6, :], ACT.Sqrt, bias=eps[:, 0:1], scale=1.0 / P
                                         ).then_inc(hg["o_std"], 1)

                for hd in range(4):
                    for lv in range(7):
                        i = 7 * hd + lv
                        e = hg_e[i % 4]
                        act.wait_ge(hg["diff"], i + 1)
                        link(nc.scalar.activation(e, e, ACT.Abs))
                        nc.scalar.activation(e, e, ACT.Exp, scale=-1.0).then_inc(hg["e"], 1)
                        if lv == 1:
                            b = xn_buf[:, (4 + hd) * T:(5 + hd) * T]
                            if hd >= 1:
                                act.wait_ge(hg["kx"], hd)
                            nc.scalar.activation(sil[:, 0, :], b, ACT.Exp)
                            for t in range(TT):
                                last = nc.scalar.activation(sil[:, 1, t * P:t * P + P], b[:, t * P:t * P + P], ACT.Exp,
                                                            scale=-1.0, bias=b[:, t * P + P - 1:t * P + P])
                            last.then_inc(hg["ex"], 1)
                        if lv == 3 and hd >= 1:
                            head_norm(hd - 1)
                head_norm(3)

            squares("ffn1_0", None, 0)
            act.wait_ge(consts_in, 48)
            for j in range(2):
                upper(ORDER[0], 0, 2, j)
            for st in STAGES:
                if st.startswith("ffn"):
                    ffn(st)
                elif st.startswith("ple"):
                    norm(st)
                    l = st[-1]
                    act.wait_ge(p_in, 16 * (int(l) + 1))
                    nc.scalar.activation(p_hi, p_buf, ACT.Copy).then_inc(p_upper, 1)

                    def gate(i, j):
                        act.wait_ge(units_done, i * 2 + (u(f"pg_{l}") + j + 1))
                        nc.scalar.activation(big[:, bass.ds(i * (2 * T) + j * T, T)], ps[:, j, :], ACT.Sigmoid
                                             ).then_inc(evac_done, 1)

                    weights(f"pg_{l}", gate)
                    weights(f"pp_{l}")
                    if l == "0" and stop_at != st:
                        squares("ffn1_1", h_ready, H_AT[st] - KD)
                elif st == "mix_0":
                    nc.scalar.activation(mod[:, 56:64], col("c"), ACT.Silu).then_inc(ada["c"], 1)
                    norm(st)
                    weights("in_ab")
                    weights("v_ab")
                    attention("a")
                    attention("b")
                    act.wait_ge(ada["used"], 4 * ADA_G)
                    for k in range(KD):
                        operand(k, ATT["a" if k < 6 else "b"]["out"], k % 6 + 1)
                    weights("out_ab")
                elif st == "mix_1":
                    norm(st)
                    weights("in_c")
                    weights("v_c")
                    attention("c")
                    act.wait_ge(ada["used"], ADA)
                    for k in range(KD):
                        operand(k, ATT["c"]["out"], k + 1)
                    weights("out_c")
                elif st == "mix_2":
                    squares("first", h_ready, H_AT["ple_1"] - KD)
                    norm("first", part=False)
                    squares("norm1", xn_ready, KD * NORM_N["first"])
                    norm("norm1", shift=mod[:, 0:8])
                    weights("in_2")
                    weights("tok_2")
                    act.wait_ge(hg["lbe"], 1)
                    nc.scalar.activation(small[:, 64:72], small[:, 64:72], ACT.Exp).then_inc(hg["lbe"], 1)
                    hgrn_gates()
                    for kv in range(2):
                        act.wait_ge(cm["th"], kv + 1)
                        t3 = s_buf[:, 2304 + kv * 128:2304 + kv * 128 + 124]
                        nc.scalar.activation(t3, t3, ACT.Sigmoid, scale=GELU_C).then_inc(cm["g1"], 1)
                    hgrn()
                    attention("n")
                    for k in range(KD):
                        operand(k, *((hg["o_out"], k + 1) if k < 4 else (ATT["n"]["out"], k - 3)))
                    for j in range(2):
                        upper("out_2", 0, 2, j)
                    weights("out_2")
                elif st == "moe":
                    norm("norm2", part=False)
                    for k in range(KD):
                        act.wait_ge(xn_ready, KD * NORM_N["norm2"] + k + 1)
                        nc.scalar.activation(xn[:, k, :], xn[:, k, :], ACT.Identity, bias=mod[:, 24 + k:25 + k]
                                             ).then_inc(x_hi_ready, 1)
                    act.wait_ge(rt["lg"], 1)
                    nc.scalar.activation(s_buf[:, 0:256], ps[:, 4, 0:256], ACT.Sigmoid).then_inc(rt["sig"], 1)
                    for t in range(TT):
                        act.wait_ge(tab["tok_ps"], t + 1)
                        nc.scalar.activation(tok[:, t, :], ps_t[:, 2 * (t % 2) * T:2 * (t % 2) * T + D], ACT.Copy
                                             ).then_inc(tab["tok_sb"], 1)
                    U = u("shared")
                    act.wait_ge(units_done, U + 4)
                    for j in range(2):
                        last = nc.scalar.activation(sil[:, j, :], ps[:, j, :], ACT.Silu)
                    last.then_inc(moe["sil"], 1)
                    act.wait_ge(tab["blocks"], 1)
                    turns_n = act.value_load(n_turns[0:1, 0:1], min_val=1, max_val=MAX_BLOCKS // 2)

                    def raw_part(j, n, used=None):
                        act.wait_ge(raw_in[j], n * 16 + 16)
                        if used is not None:
                            act.wait_ge(*used)
                        nc.scalar.activation(raw_hi[j], raw[j], ACT.Copy).then_inc(raw_upper[j], 1)

                    def tokens(s, n, used):
                        act.wait_ge(bk["tx"], n)
                        if used is not None:
                            act.wait_ge(bk["gu"], used)
                        nc.scalar.activation(xgt_hi[s], tiles(ps_t[:, 0:D], P), ACT.Copy).then_inc(bk["xh"], 1)

                    def silu(s, n):
                        act.wait_ge(bk["gu"], n)
                        nc.scalar.activation(sil_b[s], ps[:, 2, 0:EXP_H], ACT.Silu).then_inc(bk["sil"], 1)

                    for j in range(3):
                        raw_part(j, 0)
                    tokens(0, 1, None)
                    tokens(1, 2, None)
                    raw_part(0, 1, (bk["gua"], 1))
                    silu(0, 2)
                    raw_part(1, 1, (bk["gu"], 2))
                    with act.Fori(0, turns_n) as i:
                        for s in range(2):
                            n = i * 2 + s
                            act.wait_ge(bk["ht"], n + 1)
                            nc.scalar.activation(hid_t_hi[s], tiles(ps[:, 3, 0:EXP_H], P), ACT.Copy).then_inc(bk["hth"], 1)
                            raw_part(0, n + 2, (bk["gua"], n + 2))
                            silu(1 - s, n + 3)
                            tokens(s, n + 3, n + 2)
                            raw_part(1, n + 2, (bk["gu"], n + 3))
                            raw_part(2, n + 1, (bk["dn"], n + 3))
                            act.wait_ge(bk["dn"], n + 3)
                            act.wait_ge(bk["sum"], i * KD + KD)
                            nc.scalar.activation(o_hi[:, s * D:(s + 1) * D], ps_t[:, 4 * T:4 * T + D], ACT.Copy
                                                 ).then_inc(bk["oh"], 1)
                    squares("final", h_ready, H_AT["moe"] - KD)
                    norm("final", part=False)

        @block.gpsimd
        def _(pool):
            link = Chain(pool, pool_own)
            link(nc.gpsimd.memset(ones[:, :], 1.0))
            nc.gpsimd.memset(eps[:, :], EPS).then_inc(set_up, 1)
            pool.wait_ge(consts_in, 48)

            def lower(phase, turn, step, j, n=UNIT):
                s = j % 2
                pool.wait_ge(upper_done, turn * step + (CUT[phase] + j + 1))
                nc.gpsimd.tensor_tensor(w_lo[s][:, 0:n], stage[s][:, 0:n], w_hi[s][:, 0:n].bitcast(F32), ALU.subtract
                                        ).then_inc(parted, 1)

            def weights(phase):
                each_unit(pool, phase, lower)

            def ada_unit(m):
                pool.wait_ge(ada_in[m % ADA_S], 16 * (m // ADA_S + 1))
                o = ada_acc[m // 4 % len(ada_acc)]
                for j in range(2):
                    k = 2 * (m % 4) + j
                    w = ada_w[m % ADA_S][:, j * T:(j + 1) * T]
                    link(nc.gpsimd.tensor_scalar(o if k == 0 else w, w, mod[:, 56 + k:57 + k], None, ALU.mult))
                    if k > 0:
                        link(nc.gpsimd.tensor_tensor(o, o, w, ALU.add))
                pool.sem_inc(ada["used"], 1)

            def bias_mask(hd):
                if hd == 0:
                    pool.wait_ge(ATT["c"]["mask_in"], 16)
                pool.wait_ge(c_bias_in[hd % 2], 32 * (hd // 2 + 1))
                a = 64 + 1024 * (hd % 2)
                b = mask[:, a:a + 1024].rearrange("p (a n) -> p a n", n=64)
                last = nc.gpsimd.tensor_tensor(b, b, mask[:, None, 0:64].to_broadcast([P, 16, 64]), ALU.add)
                last.then_inc(c_bias[hd % 2], 1)

            def hgrn():
                q, kk = tiles(big[:, R_HQ:R_HF], T), tiles(big[:, R_HF:R_HG], T)
                for i in range(28):
                    hd, lv = i // 7, i % 7
                    n = 8 * hd + lv
                    pool.wait_ge(hg["e"], i + 1)
                    if n >= 2:
                        pool.wait_ge(hg["qk"], n - 1)
                    nc.gpsimd.tensor_tensor(hg_kl[n % 2], kk[:, hd, :], hg_e[i % 4], ALU.mult).then_inc(hg["kl"], 1)

            for j in range(2):
                lower(ORDER[0], 0, 2, j)
            for st in STAGES:
                if st == "mix_1":
                    weights("in_c")
                    weights("v_c")
                    bias_mask(0)
                    bias_mask(1)
                    for hd in range(16):
                        ada_unit(ADA_UNITS[st][hd])
                        if hd + 2 < 16:
                            bias_mask(hd + 2)
                    weights("out_c")
                elif st == "mix_2":
                    weights("in_2")
                    weights("tok_2")
                    hgrn()
                    for j in range(2):
                        lower("out_2", 0, 2, j)
                    weights("out_2")
                elif st != "moe":
                    for phase in STAGE_PHASES[st]:
                        if phase == "out_ab":
                            pool.wait_ge(ada["c"], 1)
                            for m in ADA_UNITS[st]:
                                ada_unit(m)
                        weights(phase)
                else:
                    pool.wait_ge(tab["in"], 1)
                    turns_n = pool.value_load(n_turns[0:1, 0:1], min_val=1, max_val=MAX_BLOCKS // 2)
                    pool.wait_ge(tab["tok_out"], 16)

                    def gather(s, b, n):
                        nc.gpsimd.tensor_copy(idx[:, s:s + 1], tab_f[:, b]).then_inc(bk["staged"], 1)
                        pool.wait_ge(bk["staged"], n)
                        pool.sem_inc(bk["asked"], 1)
                        nc.gpsimd.indirect_dma_start(
                            out=xg[s], out_offset=None, in_=dr["tok"],
                            in_offset=bass.IndirectOffsetOnAxis(ap=idx[:, s:s + 1], axis=0)).then_inc(gathered[s], 16)

                    def raw_part(j, n):
                        c = slice(RAW // 2 if j == 1 else 0, RAW)
                        pool.wait_ge(raw_upper[j], n + 1)
                        nc.gpsimd.tensor_tensor(raw_lo[j][:, c], raw[j][:, c], raw_hi[j][:, c].bitcast(F32), ALU.subtract
                                                ).then_inc(raw_parted[j], 1)

                    pool.wait_ge(units_done, u("shared") + 4)
                    for s in range(2):
                        gather(s, slice(s, s + 1), s + 1)
                    raw_part(1, 0)
                    raw_part(2, 0)
                    pool.wait_ge(bk["tx"], 1)
                    gather(0, slice(2, 3), 3)
                    raw_part(1, 1)
                    with pool.Fori(0, turns_n) as i:
                        for s in range(2):
                            pool.wait_ge(bk["tx"], i * 2 + (s + 2))
                            gather(1 - s, bass.ds(i * 2 + (s + 3), 1), i * 2 + (s + 4))
                            raw_part(1, i * 2 + (s + 2))
                            raw_part(2, i * 2 + (s + 1))
                    pool.wait_ge(gathered[0], turns_n * 16 + 32)

        @block.vector
        def _(dve):
            link = Chain(dve, dve_own)
            dve.wait_ge(consts_in, 48)
            for s in range(2):
                dve.wait_ge(x_in[s], 16)
            dve.wait_ge(set_up, 1)
            dve.sem_inc(evac_done, 2)

            def clear_squares():
                link(nc.vector.memset(acc[:, :], 0.0))

            def add_square(hm):
                link(nc.vector.tensor_tensor(sq[:, 0, :], hm, hm, ALU.mult))
                link(nc.vector.tensor_tensor(acc[:, :], acc[:, :], sq[:, 0, :], ALU.add))

            def norm(name, dst):
                gain = col(f"g_{name}")
                dve.wait_ge(std_ready, NORM_N[name] + 1)
                link(nc.vector.reciprocal(rstd[:, :], std[:, :]))
                for k in range(KD):
                    ins = nc.vector.scalar_tensor_tensor(out=dst[:, k, :], in0=h[:, k, :], scalar=gain[:, k:k + 1],
                                                         in1=rstd[:, :], op0=ALU.mult, op1=ALU.mult)
                    ins.then_inc(xn_ready, 1)

            def operand(name, shift=None):
                for k in range(KD):
                    dve.wait_ge(x_hi_ready, PART_AT[name] + k + 1)
                    hi = x_hi[:, k, :].bitcast(F32)
                    if shift is None:
                        ins = nc.vector.tensor_tensor(x_lo[:, k, :], mixed[:, k, :], hi, ALU.subtract)
                    else:
                        ins = nc.vector.scalar_tensor_tensor(out=x_lo[:, k, :], in0=mixed[:, k, :], scalar=shift[:, k:k + 1],
                                                             in1=hi, op0=ALU.add, op1=ALU.subtract)
                    ins.then_inc(x_ready, 1)

            def residual(phase, name, factor, per=1, bank=0):
                U, n = BASE[phase]
                clear_squares()
                with link.loop(KD // 2, 4) as i:
                    for s in range(2):
                        dve.wait_ge(units_done, i * (2 * per) + (U + per * (s + 1)))
                        m = i * 2 + s
                        hm = h_buf[:, bass.ds(m * T, T)]
                        f = factor if isinstance(factor, float) else factor[:, bass.ds(m, 1)]
                        nc.vector.scalar_tensor_tensor(out=hm, in0=ps[:, bank + s, :], scalar=f, in1=hm,
                                                       op0=ALU.mult, op1=ALU.add).then_inc(h_ready, 1)
                        dve.wait_ge(h_ready, i * 2 + (H_AT[name] - KD + s + 1))
                        dve.sem_inc(evac_done, per)
                        add_square(hm)
                dve.sem_inc(acc_ready, 1)

            def modulation(g0, g1):
                dve.wait_ge(ada["ps"], g1)
                c = slice(4 * g0, 4 * g1)
                nc.vector.tensor_tensor(mod[:, c], ps[:, 5, c], col("b_ada")[:, c], ALU.add).then_inc(ada["read"], 1)

            def ffn(st):
                norm(st, mixed)
                operand(st)
                l, k = st[-1], int(st[3]) - 1
                U, n = BASE[f"gu_{l}_{k}"]
                with link.loop(NF, 0) as i:
                    dve.wait_ge(units_done, i * 2 + (U + 2))
                    dve.wait_ge(evac_done, i * 2 + (U + 3))
                    nc.vector.tensor_tensor(tmp[:, 0, :], sil[:, 0, :], ps[:, 1, :], ALU.mult).then_inc(evac_done, 1)
                    dve.wait_ge(hid_hi_ready, i + (HID_AT[st] + 1))
                    nc.vector.tensor_tensor(hid_buf[:, bass.ds(i * T + NF * T, T)], tmp[:, 0, :],
                                            hid_buf[:, bass.ds(i * T, T)].bitcast(F32), ALU.subtract).then_inc(hid_ready, 1)
                    dve.wait_ge(hid_ready, i + (HID_AT[st] + 1))
                residual(f"down_{l}_{k}", st, 0.5, per=len(DOWN), bank=2)

            def rope_tile(src, dst, scale):
                link(nc.vector.scalar_tensor_tensor(out=dst, in0=src, scalar=scale, in1=cos, op0=ALU.mult, op1=ALU.mult))
                for g in range(4):
                    o, a = 32 * (g ^ 1), 32 * g
                    ins = nc.vector.scalar_tensor_tensor(out=tmp[o:o + 32, 0, :], in0=src[a:a + 32, :], scalar=scale,
                                                         in1=sin[a:a + 32, :], op0=ALU.mult, op1=ALU.mult)
                link(ins)
                return nc.vector.tensor_tensor(dst, dst, tmp[:, 0, :], ALU.add)

            def rope_units(phase, first, n, dst, scale):
                U = u(phase) + first
                with link.loop(n // 2, 6) as i:
                    for s in range(2):
                        dve.wait_ge(units_done, i * 2 + (U + s + 1))
                        link(rope_tile(ps[:, s, :], big[:, bass.ds(i * (2 * T) + (dst + s * T), T)], scale))
                        dve.sem_inc(evac_done, 1)

            def copy_units(phase, first, n, dst, scale=1.0):
                U = u(phase) + first
                for m in range(n):
                    dve.wait_ge(units_done, U + m + 1)
                    nc.vector.tensor_scalar(big[:, dst + m * T:dst + (m + 1) * T], ps[:, (first + m) % 2, :],
                                            scale, None, ALU.mult).then_inc(evac_done, 1)

            def token_units(phase, first, n, dst, pitch, width=256):
                U = u(phase)
                d = tiles(big[:, dst:dst + TT * pitch], pitch)
                for m in range(n):
                    c = first + m
                    dve.wait_ge(units_done, U + 2 * c + 2)
                    b = 4 * ((c + 1) % 2)
                    link(nc.vector.tensor_copy(d[:, :, m * 256:m * 256 + width], ps[:, b:b + 4, 0:width]))
                    dve.sem_inc(evac_done, 2)

            def attention(name):
                a = ATT[name]
                units, ns = a["units"], len(a["sc"])
                dve.wait_ge(a["mask_in"], 16)
                done = 0
                for i in range(len(units) + 4):
                    if i < len(units):
                        un, b = units[i], i % 2
                        dve.wait_ge(a["sc_ready"], i + 1)
                        if i >= NS:
                            dve.wait_ge(a["pt_ready"], i - NS + 1)
                        if i >= 2:
                            dve.wait_ge(a["exps"], i - 1)
                        if name == "c" and un["t"] == 0:
                            hd = 2 * un["pair"] + un["half"]
                            dve.wait_ge(c_bias[hd % 2], hd // 2 + 1)
                        for g, (_, _, add, c0, n) in enumerate(un["segs"]):
                            last = nc.vector.tensor_tensor_reduce(
                                out=s_buf[:, (i % NS) * SCMAX + c0:(i % NS) * SCMAX + c0 + n], in0=ps[:, a["sc"][i % ns] + g, 0:n],
                                in1=add, scale=1.0, scalar=-3e38, op0=ALU.add, op1=ALU.max,
                                accum_out=mx[:, 4 * b + g:4 * b + g + 1])
                        last.then_inc(a["sc_read"], 1)
                        dve.wait_ge(a["sc_read"], i + 1)
                        ng = len(un["segs"])
                        m = mx[:, 4 * b:4 * b + ng]
                        if un["sink"] is not None:
                            ins = nc.vector.tensor_scalar(negm[:, 4 * b:4 * b + 1], m,
                                                          col("sink")[:, un["sink"]:un["sink"] + 1], -1.0, ALU.max, ALU.mult)
                        elif len(un["groups"]) < ng:
                            ins = nc.vector.tensor_reduce(negm[:, 4 * b:4 * b + 1], m, AX.X, ALU.max, negate=True)
                        else:
                            ins = nc.vector.tensor_scalar(negm[:, 4 * b:4 * b + ng], m, -1.0, None, ALU.mult)
                        ins.then_inc(a["negm"], 1)
                    if 1 <= i <= len(units):
                        j = i - 1
                        un, b = units[j], j % 2
                        ng = len(un["groups"])
                        dve.wait_ge(a["exps"], j + 1)
                        dn = den[:, 4 * b:4 * b + ng]
                        if un["sink"] is not None:
                            link(nc.vector.tensor_tensor(rden[:, 4 * b:4 * b + 1], dn, es[:, b:b + 1], ALU.add))
                            dn = rden[:, 4 * b:4 * b + 1]
                        if "gate" in un:
                            link(nc.vector.reciprocal(rden[:, 4 * b:4 * b + ng], dn))
                            gt = gates[:, un["t"], un["gate"]:un["gate"] + 3]
                            nc.vector.tensor_tensor(fac[:, 4 * b:4 * b + 2], rden[:, 4 * b:4 * b + 2], gt[:, 1:3], ALU.mult)
                            ins = nc.vector.tensor_tensor(fac[:, 4 * b + 2:4 * b + 3], rden[:, 4 * b + 2:4 * b + 3], gt[:, 0:1],
                                                          ALU.mult)
                        else:
                            ins = nc.vector.reciprocal(fac[:, 4 * b:4 * b + ng], dn)
                        link(ins)
                        for g, (c0, n) in enumerate(un["groups"]):
                            p = s_buf[:, (j % NS) * SCMAX + c0:(j % NS) * SCMAX + c0 + n]
                            ins = nc.vector.tensor_scalar(p, p, fac[:, 4 * b + g:4 * b + g + 1], None, ALU.mult)
                        ins.then_inc(a["probs"], 1)
                    if i >= 4 and units[i - 4]["last"]:
                        un = units[i - 4]
                        dve.wait_ge(a["pv"], i - 3)
                        nc.vector.tensor_copy(mixed[:, un["out"], :], ps[:, 6 + un["pair"] % 2, :]).then_inc(a["out"], 1)

            def compress_blocks():
                for kv in range(2):
                    pe_c = col("pe_k" if kv == 0 else "pe_v")
                    blk = s_buf[:, kv * 1024:kv * 1024 + 992].rearrange("p (l g c) -> p g c l", l=16, g=2)
                    src = big[:, R_KCV + kv * T:R_KCV + (kv + 1) * T]
                    for g in range(2):
                        for par in range(2):
                            for half in range(2):
                                r = slice(64 * g, 64 * g + 64)
                                tk = src[r, 16 * half:16 * half + 16 * N_CMP].rearrange("p (c m q) -> p c m q", m=8, q=2)
                                pos = pe_c[r, 16 * half:16 * half + 16].rearrange("p (m q) -> p m q", q=2)
                                ins = nc.vector.tensor_tensor(
                                    blk[64 * par:64 * par + 64, g, :, 8 * half:8 * half + 8], tk[:, :, :, par],
                                    pos[:, None, :, par].to_broadcast([64, N_CMP, 8]), ALU.add)
                    ins.then_inc(cm["blk"], 1)

            def compress():
                U = u("cmp")
                for kv in range(2):
                    dve.wait_ge(units_done, U + 4 * kv + 4)
                    x1 = s_buf[:, 2048 + kv * 128:2048 + kv * 128 + 124].rearrange("p (j n) -> p j n", j=2)
                    t3 = s_buf[:, 2304 + kv * 128:2304 + kv * 128 + 124].rearrange("p (j n) -> p j n", j=2)
                    b1 = col("b1k" if kv == 0 else "b1v")
                    for j in range(2):
                        ins = nc.vector.tensor_scalar(x1[:, j, :], ps[:, 2 * kv + j, 0:62], b1[:, j:j + 1], None, ALU.add)
                    link(ins)
                    dve.sem_inc(evac_done, 4)
                    link(nc.vector.tensor_tensor(t3, x1, x1, ALU.mult))
                    link(nc.vector.tensor_scalar(t3, t3, 0.044715, 1.0, ALU.mult, ALU.add))
                    nc.vector.tensor_tensor(t3, t3, x1, ALU.mult).then_inc(cm["th"], 1)
                for kv in range(2):
                    x1 = s_buf[:, 2048 + kv * 128:2048 + kv * 128 + 124]
                    t3 = s_buf[:, 2304 + kv * 128:2304 + kv * 128 + 124]
                    dve.wait_ge(cm["g1"], kv + 1)
                    nc.vector.tensor_tensor(x1, x1, t3, ALU.mult).then_inc(cm["hid"], 1)
                nc.vector.memset(kcmp, 0.0)
                link(nc.vector.memset(big[0:32, R_VCMP:R_VCMP + 2 * HD], 0.0))
                dve.wait_ge(cm["kv"], 2)
                nc.vector.tensor_copy(kcmp[:, 0:N_CMP], ps[:, 4, 0:N_CMP])
                link(nc.vector.tensor_copy(big[0:N_CMP, R_VCMP:R_VCMP + 2 * HD], ps[0:N_CMP, 5, 0:2 * HD]))

            def hgrn_gates():
                f = tiles(big[:, R_HF:R_HG], T)
                lbs = small[:, 64:72]
                lg = col("lb")
                m = small[:, 72:76]
                link(nc.vector.tensor_tensor(m, lg[:, 0:4], lg[:, 4:8], ALU.max))
                nc.vector.tensor_tensor(lbs[:, 0:4], lg[:, 0:4], m, ALU.subtract)
                nc.vector.tensor_tensor(lbs[:, 4:8], lg[:, 4:8], m, ALU.subtract).then_inc(hg["lbe"], 1)
                dve.wait_ge(hg["lbe"], 2)
                link(nc.vector.tensor_tensor(m, lbs[:, 0:4], lbs[:, 4:8], ALU.add))
                link(nc.vector.reciprocal(small[:, 76:80], m))
                lb, lb1 = small[:, 80:84], small[:, 84:88]
                nc.vector.tensor_tensor(lb, lbs[:, 0:4], small[:, 76:80], ALU.mult)
                link(nc.vector.tensor_tensor(lb1, lbs[:, 4:8], small[:, 76:80], ALU.mult))
                dve.wait_ge(hg["sig"], 2)
                for hd in range(4):
                    ins = nc.vector.tensor_scalar(f[:, hd, :], f[:, hd, :], lb1[:, hd:hd + 1], lb[:, hd:hd + 1],
                                                  ALU.mult, ALU.add)
                link(ins)
                nc.vector.tensor_scalar(big[:, R_HF:R_HG], big[:, R_HF:R_HG], 2.0 ** -64, None, ALU.max
                                        ).then_inc(hg["ln_in"], 1)
                dve.wait_ge(hg["ln"], 1)
                link(nc.vector.tensor_scalar(big[:, R_HF:R_HG], big[:, R_HF:R_HG], -1.0, 1.0, ALU.mult, ALU.add))
                for n in range(4 * TT):
                    lf = xn_buf[:, 4 * T + n * P:4 * T + n * P + P]
                    ins = nc.vector.tensor_tensor_scan(mixed_buf[:, n * P:n * P + P],
                                                       ones[:, :], lf, 0.0, ALU.mult, ALU.add)
                link(ins)
                link(nc.vector.tensor_copy(xn_buf[:, 4 * T:8 * T], mixed_buf[:, 0:4 * T]))

            def hgrn():
                q, f = tiles(big[:, R_HQ:R_HF], T), tiles(big[:, R_HF:R_HG], T)
                dve.wait_ge(hg["mask_in"], 16)

                def diff(i):
                    half = 64 >> i % 7
                    if i >= 4:
                        dve.wait_ge(hg["kl"], i - 3)
                        dve.wait_ge(hg["ql"], i - 3)
                    bv = xn_buf[:, (4 + i // 7) * T:(5 + i // 7) * T].rearrange("p (n c) -> p n c", c=2 * half)
                    nc.vector.tensor_tensor(hg_e[i % 4].rearrange("p (n c) -> p n c", c=2 * half), bv,
                                            bv[:, :, half - 1:half].to_broadcast([P, T // (2 * half), 2 * half]),
                                            ALU.subtract).then_inc(hg["diff"], 1)

                def masked(i):
                    lv = i % 8
                    dve.wait_ge(hg["qk"], i + 1)
                    if i >= 2:
                        dve.wait_ge(hg["pv"], i - 1)
                    nc.vector.tensor_tensor(hg_masked[i % 2], tiles(ps[:, i % 2, :], P),
                                            mask[:, None, lv * P:lv * P + P].to_broadcast([P, TT, P]), ALU.mult
                                            ).then_inc(hg["mul"], 1)

                def carried(hd):
                    dve.wait_ge(hg["ex"], hd + 1)
                    if hd >= 1:
                        dve.wait_ge(hg["x_ps"], hd)
                    eb, ek = sil[:, 0, :], sil[:, 1, :]
                    nc.vector.tensor_tensor(pt_buf[:, 0:T], q[:, hd, :], eb, ALU.mult)
                    link(nc.vector.tensor_tensor(pt_buf[:, T:2 * T], f[:, hd, :], ek, ALU.mult))
                    for t in range(2):
                        ins = nc.vector.tensor_scalar(pt_buf[:, 2 * T + t * P:2 * T + t * P + P],
                                                      pt_buf[:, T + t * P:T + t * P + P],
                                                      eb[:, (t + 2) * P - 1:(t + 2) * P], None, ALU.mult)
                    link(ins)
                    nc.vector.tensor_scalar(pt_buf[:, 3 * T:3 * T + P], pt_buf[:, 2 * T:2 * T + P],
                                            eb[:, 3 * P - 1:3 * P], None, ALU.mult).then_inc(hg["kx"], 1)

                def head_out(hd):
                    dve.wait_ge(hg["o_std"], hd + 1)
                    link(nc.vector.reciprocal(rstd[:, :], std[:, :]))
                    link(nc.vector.scalar_tensor_tensor(out=mixed[:, hd, :], in0=ps[:, 4 + hd % 2, :],
                                                        scalar=col("hg_g")[:, hd:hd + 1], in1=rstd[:, :],
                                                        op0=ALU.mult, op1=ALU.mult))
                    nc.vector.tensor_tensor(mixed[:, hd, :], mixed[:, hd, :], tiles(big[:, R_HG:R_NQ], T)[:, hd, :],
                                            ALU.mult).then_inc(hg["o_out"], 1)

                diff(0)
                diff(1)
                diff(2)
                for n in range(33):
                    hd, lv = n // 8, n % 8
                    i = 7 * hd + lv
                    if n < 32 and lv < 7:
                        dve.wait_ge(hg["e"], i + 1)
                        if n >= 2:
                            dve.wait_ge(hg["qk"], n - 1)
                        nc.vector.tensor_tensor(hg_ql[n % 2], q[:, hd, :], hg_e[i % 4], ALU.mult).then_inc(hg["ql"], 1)
                        if i + 3 < 28:
                            diff(i + 3)
                    if n >= 1:
                        masked(n - 1)
                    if lv == 2:
                        carried(hd)
                    if lv == 4:
                        dve.wait_ge(hg["x_ps"], hd + 1)
                        if hd >= 1:
                            dve.wait_ge(hg["pv"], 8 * hd)
                        nc.vector.tensor_copy(xn_buf[:, 0:6 * P], ps_t[:, 2 * T:2 * T + 6 * P]).then_inc(hg["x_sb"], 1)
                    if lv == 5 and hd >= 1:
                        head_out(hd - 1)
                head_out(3)

            def router():
                IMM = -3e30
                sc = tiles(s_buf[:, 0:256], N_EXP)
                ch = tiles(s_buf[:, 256:512], N_EXP)
                m8 = tiles(s_buf[:, 512:768], 8)
                rep = tiles(s_buf[:, 768:1024], N_EXP)
                wr = tiles(s_buf[:, 1024:1280], N_EXP)
                dve.wait_ge(rt["sig"], 1)
                link(nc.vector.tensor_tensor(ch, sc, col("router_bias")[:, None, :].to_broadcast([P, TT, N_EXP]), ALU.add))
                for n in range(32):
                    ins = nc.vector.max(m8[:, n, :], s_buf[:, 256 + 8 * n:264 + 8 * n])
                gs = tiles(small[:, 128:176], 12)
                g8, gr = tiles(small[:, 176:208], 8), tiles(small[:, 208:256], 12)
                link(nc.vector.memset(small[:, 128:176], 3e30))
                ins = nc.vector.tensor_tensor(gs[:, :, 0:8], s_buf[:, 512:768].rearrange("p (t g e) -> p t g e", g=8, e=8)[:, :, :, 0],
                                              s_buf[:, 512:768].rearrange("p (t g e) -> p t g e", g=8, e=8)[:, :, :, 1], ALU.add)
                link(ins)
                for t in range(TT):
                    ins = nc.vector.max(g8[:, t, :], gs[:, t, :])
                link(ins)
                for t in range(TT):
                    ins = nc.vector.match_replace(gr[:, t, :], g8[:, t, :], gs[:, t, :], IMM)
                link(ins)
                pen = tiles(small[:, 256:288], 8)
                link(nc.vector.tensor_scalar(pen, gr[:, :, 0:8], IMM, NEG, ALU.not_equal, ALU.mult))
                c4 = s_buf[:, 256:512].rearrange("p (t g e) -> p t g e", g=8, e=8)
                for t in range(TT):
                    ins = nc.vector.tensor_tensor(c4[:, t], c4[:, t], pen[:, t, :, None].to_broadcast([P, 8, 8]), ALU.add)
                link(ins)
                v8 = tiles(small[:, 288:320], 8)
                for t in range(TT):
                    ins = nc.vector.max(v8[:, t, :], ch[:, t, :])
                link(ins)
                for t in range(TT):
                    ins = nc.vector.match_replace(rep[:, t, :], v8[:, t, :], ch[:, t, :], IMM)
                link(ins)
                sm, rs = small[:, 320:324], small[:, 324:328]
                for t in range(TT):
                    ins = nc.vector.scalar_tensor_tensor(out=wr[:, t, :], in0=rep[:, t, :], scalar=IMM, in1=sc[:, t, :],
                                                         op0=ALU.is_equal, op1=ALU.mult)
                link(ins)
                link(nc.vector.tensor_reduce(sm, wr, AX.X, ALU.add))
                link(nc.vector.reciprocal(rs, sm))
                for t in range(TT):
                    ins = nc.vector.tensor_scalar(wr[:, t, :], wr[:, t, :], rs[:, t:t + 1], ROUTED_SCALE, ALU.mult, ALU.mult)
                link(ins)
                nc.vector.tensor_scalar(s_buf[:, 2560:2816], s_buf[:, 768:1024], IMM, None, ALU.is_equal).then_inc(tab["sel"], 1)

            def tables():
                wr, sel = tiles(s_buf[:, 1024:1280], N_EXP), tiles(s_buf[:, 2560:2816], N_EXP)
                pos, nth = s_buf[:, 2816:3072], tiles(s_buf[:, 3072:3328], N_EXP)
                terms = tiles(pt_buf[:, 0:3 * TOP_K * N_EXP], N_EXP)
                dve.wait_ge(tab["const_in"], 16)
                dve.wait_ge(tab["rank"], 1)
                rank, count = ps[:, 5, 0:TT * N_EXP], ps[:, 5, TT * N_EXP:(TT + 1) * N_EXP]
                nb, end, begin = small[:, 332:396], small[:, 396:460], small[:, 128:192]
                link(nc.vector.tensor_scalar(nb, count, 0.0, None, ALU.is_gt))
                for j in range(1, T // P):
                    link(nc.vector.scalar_tensor_tensor(out=nb, in0=count, scalar=float(j * P), in1=nb,
                                                        op0=ALU.is_gt, op1=ALU.add))
                link(nc.vector.tensor_tensor_scan(end, ones[:, 0:N_EXP], nb, 0.0, ALU.mult, ALU.add))
                link(nc.vector.tensor_tensor(begin, end, nb, ALU.subtract))
                be, nt = small[:, 460:461], small[:, 461:462]
                nc.vector.scalar_tensor_tensor(out=terms[:, 0, :], in0=end, scalar=slot_no, in1=ones[:, 0:N_EXP],
                                               op0=ALU.is_le, op1=ALU.mult, accum_out=be)
                link(nc.vector.scalar_tensor_tensor(out=terms[:, 1, :], in0=iota_e2, scalar=end[:, N_EXP - 1:N_EXP],
                                                    in1=ones[:, 0:N_EXP], op0=ALU.is_lt, op1=ALU.mult, accum_out=nt))
                link(nc.vector.tensor_scalar(be, be, float(N_EXP - 1), None, ALU.min))
                nc.vector.tensor_copy(block_e, be)
                nc.vector.tensor_copy(n_turns, nt).then_inc(tab["blocks"], 1)
                blk = tmp_buf[:, 0:TT * N_EXP]
                link(nc.vector.tensor_scalar(blk, rank, float(P), None, ALU.is_ge))
                for j in range(2, T // P):
                    link(nc.vector.scalar_tensor_tensor(out=blk, in0=rank, scalar=float(j * P), in1=blk,
                                                        op0=ALU.is_ge, op1=ALU.add))
                link(nc.vector.scalar_tensor_tensor(out=pos, in0=blk, scalar=-float(P), in1=rank, op0=ALU.mult, op1=ALU.add))
                p3, b3 = tiles(pos, N_EXP), tiles(blk, N_EXP)
                link(nc.vector.tensor_tensor(b3, b3, begin[:, None, :].to_broadcast([P, TT, N_EXP]), ALU.add))
                for t in range(TT):
                    ins = nc.vector.tensor_tensor_scan(nth[:, t, :], ones[:, 0:N_EXP], sel[:, t, :], 0.0, ALU.mult, ALU.add)
                link(ins)
                link(nc.vector.tensor_tensor(nth, nth, sel, ALU.mult))
                for t in range(TT):
                    for k in range(TOP_K):
                        n = t * TOP_K + k
                        for c, (src, dst) in enumerate(((p3, slot_r), (b3, slot_b), (wr, slot_w))):
                            ins = nc.vector.scalar_tensor_tensor(
                                out=terms[:, 3 * k + c, :], in0=nth[:, t, :], scalar=float(k + 1), in1=src[:, t, :],
                                op0=ALU.is_equal, op1=ALU.mult, accum_out=dst[:, n:n + 1])
                    link(ins)
                for n in range(TT * TOP_K):
                    if n >= 4:
                        dve.wait_ge(tab["filled"], n - 3)
                    r, b, w, t = slot_r[:, n:n + 1], slot_b[:, n:n + 1], slot_w[:, n:n + 1], n // TOP_K
                    nc.vector.tensor_scalar(at_r[n % 4], iota_t[:, 0:P], r, None, ALU.is_equal)
                    nc.vector.tensor_scalar(at_b[n % 4][:, 0:BLOCKS], iota_t[:, 0:BLOCKS], b, tok_no[:, t:t + 1],
                                            ALU.is_equal, ALU.mult)
                    nc.vector.tensor_scalar(at_b[n % 4][:, BLOCKS:2 * BLOCKS], iota_t[:, 0:BLOCKS], b, w,
                                            ALU.is_equal, ALU.mult).then_inc(tab["pairs"], 1)
                dve.wait_ge(tab["filled"], TT * TOP_K)
                nc.vector.tensor_copy(mask[:, 1024:1024 + 2 * BLOCKS], ps[:, 6, 0:2 * BLOCKS]).then_inc(tab["in"], 1)

            def routed():
                def raw_part(j, n):
                    dve.wait_ge(raw_upper[j], n + 1)
                    c = slice(0, RAW // 2 if j == 1 else RAW)
                    nc.vector.tensor_tensor(raw_lo[j][:, c], raw[j][:, c], raw_hi[j][:, c].bitcast(F32), ALU.subtract
                                            ).then_inc(raw_parted[j], 1)

                dve.wait_ge(moe["acc"], KD)
                nc.vector.memset(o_hi[:, :].bitcast(F32), 0.0)
                nc.vector.memset(o_lo[:, :].bitcast(F32), 0.0)
                link(nc.vector.memset(send[:, :].bitcast(F32), 0.0))
                dve.sem_inc(bk["ol"], 1)
                dve.sem_inc(bk["added"], 2)
                raw_part(0, 0)
                raw_part(1, 0)
                dve.wait_ge(tab["in"], 1)
                dve.sem_inc(tab["ready"], 1)
                turns_n = dve.value_load(n_turns[0:1, 0:1], min_val=1, max_val=MAX_BLOCKS // 2)

                def hidden(s, b, n):
                    dve.wait_ge(bk["sil"], n)
                    nc.vector.scalar_tensor_tensor(out=hid_b[s], in0=sil_b[s], scalar=tab_w[:, b],
                                                   in1=ps[:, 2, EXP_H:2 * EXP_H], op0=ALU.mult, op1=ALU.mult).then_inc(bk["hid"], 1)

                def tokens(s, n):
                    dve.wait_ge(bk["xh"], n)
                    nc.vector.tensor_tensor(xgt_lo[s], tiles(ps_t[:, 0:D], P), xgt_hi[s].bitcast(F32), ALU.subtract
                                            ).then_inc(bk["xt"], 1)

                def add_sent(i):
                    for m in range(KD):
                        dve.wait_ge(bk["sum"], i * KD + (m + 1))
                        nc.vector.tensor_tensor(mixed[:, m, :], mixed[:, m, :], ps[:, 6 + m % 2, :], ALU.add
                                                ).then_inc(bk["added"], 1)

                tokens(0, 1)
                tokens(1, 2)
                raw_part(0, 1)
                hidden(0, slice(0, 1), 1)
                raw_part(1, 1)
                with dve.Fori(0, turns_n) as i:
                    for s in range(2):
                        n = i * 2 + s
                        dve.wait_ge(bk["hth"], n + 1)
                        nc.vector.tensor_tensor(hid_t_lo[s], tiles(ps[:, 3, 0:EXP_H], P), hid_t_hi[s].bitcast(F32),
                                                ALU.subtract).then_inc(bk["hts"], 1)
                        raw_part(0, n + 2)
                        hidden(1 - s, bass.ds(i * 2 + (s + 1), 1), i * 2 + (s + 2))
                        tokens(s, n + 3)
                        raw_part(1, n + 2)
                        if s == 0:
                            add_sent(i)
                        nc.vector.tensor_scalar(send[:, s * T:(s + 1) * T], iota_t, tab_f[:, bass.ds(i * 2 + s, 1)], None,
                                                ALU.is_equal)
                        dve.wait_ge(bk["oh"], i * 2 + (s + 1))
                        nc.vector.tensor_tensor(o_lo[:, s * D:(s + 1) * D], ps_t[:, 4 * T:4 * T + D],
                                                o_hi[:, s * D:(s + 1) * D].bitcast(F32), ALU.subtract).then_inc(bk["ol"], 1)
                add_sent(turns_n)
                dve.wait_ge(bk["added"], turns_n * KD + (KD + 2))

            def expert_add(m):
                dve.wait_ge(moe["dn"], m + 1)
                nc.vector.tensor_copy(mixed[:, m, :], ps[:, 4 + m % 4, :]).then_inc(moe["acc"], 1)

            for st in STAGES:
                if st.startswith("ffn"):
                    ffn(st)
                elif st.startswith("ple"):
                    l = st[-1]
                    norm(st, mixed)
                    operand(st)
                    dve.wait_ge(p_upper, int(l) + 1)
                    nc.vector.tensor_tensor(p_lo, p_buf, p_hi.bitcast(F32), ALU.subtract).then_inc(p_parted, 1)
                    g = tiles(big[:, 0:8 * T], T)
                    U = u(f"pp_{l}")
                    dve.wait_ge(evac_done, U + 2)
                    for s in range(2):
                        dve.wait_ge(units_done, U + s + 1)
                        for m in range(4):
                            k = 4 * s + m
                            link(nc.vector.tensor_tensor(g[:, k, :], g[:, k, :], ps[:, k, :], ALU.mult))
                            nc.vector.tensor_tensor(h[:, k, :], h[:, k, :], g[:, k, :], ALU.add).then_inc(h_ready, 1)
                        dve.wait_ge(h_ready, H_AT[st] - KD + 4 * s + 4)
                        dve.sem_inc(evac_done, 1)
                elif st == "mix_0":
                    norm(st, mixed)
                    operand(st)
                    rope_units("in_ab", 0, 12, 0, HD ** -0.5)
                    rope_units("in_ab", 12, 8, 12 * T, 1.0)
                    token_units("v_ab", 0, 4, 20 * T, D)
                    dve.sem_inc(ATT["a"]["qkv"], 1)
                    dve.sem_inc(ATT["b"]["qkv"], 1)
                    dve.sem_inc(ATT["b"]["mask_in"], 16)
                    attention("a")
                    attention("b")
                    operand("out_ab")
                    modulation(0, ADA_G)
                    residual("out_ab", st, 1.0)
                elif st == "mix_1":
                    norm(st, mixed)
                    operand(st)
                    copy_units("in_c", 0, 8, 0, HD ** -0.5)
                    copy_units("in_c", 8, 8, 8 * T)
                    token_units("v_c", 0, 4, 16 * T, D)
                    dve.sem_inc(ATT["c"]["qkv"], 1)
                    attention("c")
                    operand("out_c")
                    modulation(ADA_G, ADA // 4)
                    residual("out_c", st, 1.0)
                elif st == "mix_2":
                    dve.wait_ge(ada["read"], 2)
                    nc.vector.scalar_tensor_tensor(out=col("g_norm1"), in0=mod[:, 8:16], scalar=1.0, in1=col("g_norm1"),
                                                   op0=ALU.add, op1=ALU.mult)
                    link(nc.vector.scalar_tensor_tensor(out=col("g_norm2"), in0=mod[:, 32:40], scalar=1.0, in1=col("g_norm2"),
                                                        op0=ALU.add, op1=ALU.mult))
                    norm("first", h)
                    dve.wait_ge(xn_ready, KD * (NORM_N["first"] + 1))
                    dve.sem_inc(h_ready, KD)
                    norm("norm1", mixed)
                    operand("norm1", shift=mod[:, 0:8])
                    copy_units("in_2", 0, 4, R_HQ, HG_SCALE)
                    copy_units("in_2", 4, 8, R_HF)
                    U = u("in_2") + 12
                    for k in range(4):
                        dve.wait_ge(units_done, U + k + 1)
                        src = ps[:, k % 2, :]
                        nc.vector.tensor_scalar(big[:, R_NQ + k * T:R_NQ + (k + 1) * T], src, HD ** -0.5, None, ALU.mult)
                        link(rope_tile(src, big[:, R_NR + k * T:R_NR + (k + 1) * T], HD ** -0.5))
                        dve.sem_inc(evac_done, 1)
                    copy_units("in_2", 16, 2, R_KCV)
                    rope_units("in_2", 18, 2, R_KSW, 1.0)
                    token_units("tok_2", 0, 2, R_VI, T)
                    token_units("tok_2", 2, 1, R_VSW, 256)
                    token_units("tok_2", 3, 1, R_GATE, 24, width=24)
                    compress_blocks()
                    hgrn_gates()
                    compress()
                    hgrn()
                    g3 = gates[:, 0, :].rearrange("p (n c) -> p n c", c=3)
                    dve.wait_ge(ATT["n"]["mask_in"], 16)
                    link(nc.vector.tensor_scalar(g3[:, :, 0], g3[:, :, 0], mask[:, 640:641], None, ALU.mult))
                    dve.sem_inc(ATT["n"]["qkv"], 1)
                    attention("n")
                    operand("out_2")
                    residual("out_2", st, mod[:, 16:24])
                elif st == "moe":
                    norm("norm2", xn)
                    router()
                    tables()
                    dve.wait_ge(moe["sil"], 1)
                    hb = tiles(s_buf[:, 1536:2560], T)
                    for j in range(2):
                        ins = nc.vector.tensor_tensor(hb[:, j, :], sil[:, j, :], ps[:, 2 + j, :], ALU.mult)
                    ins.then_inc(moe["hid"], 1)
                    for m in range(KD):
                        expert_add(m)
                    routed()
                    for m in range(KD):
                        nc.vector.scalar_tensor_tensor(out=h[:, m, :], in0=mixed[:, m, :], scalar=mod[:, 40 + m:41 + m],
                                                       in1=h[:, m, :], op0=ALU.mult, op1=ALU.add).then_inc(h_ready, 1)
                    norm("final", mixed)


def _units(w, width=P):
    k, n = w.shape
    return np.ascontiguousarray(w.reshape(k // P, P, n // width, width).transpose(2, 1, 0, 3)).reshape(
        n // width, P, (k // P) * width)


def _halves(w):
    n, _, cols = (u := _units(w, 256)).shape
    return np.ascontiguousarray(u.reshape(n, P, 2, cols // 2).transpose(0, 2, 1, 3)).reshape(2 * n, P, cols // 2)


def _column(v):
    return v.reshape(-1, P).T


def _heads(w, order):
    return np.concatenate([w[:, a * HD:(a + 1) * HD] for a in order], axis=1)


def _constants():
    q, kk = np.arange(P)[:, None], np.arange(896)[None, :]
    off = kk - 384 - q
    near = kk[:, :384] - P - q
    where = lambda ok: np.where(ok, np.float32(0), np.float32(NEG)).astype(np.float32)
    mask_ab = np.concatenate([
        where(np.abs(near) <= 128), where(np.abs(near) <= 64),
        where((np.abs(off) <= 256) & (off % 4 == 0)), where((np.abs(off) <= 1024) & (off % 16 == 0))], axis=1)
    qj, kj = np.arange(64)[:, None], np.arange(64)[None, :]
    start = np.clip(qj - 8, 0, 48)
    mask_c = np.tile(where((kj >= start) & (kj < start + 16)), (2, 1))
    causal = where(off[:, :512] <= 0)
    pos = np.arange(T).reshape(TT, P).T[:, :, None]
    c = np.arange(32)[None, None, :]
    cmp_ok = (c * 16 + 31 <= pos) & (c < N_CMP)
    mask_n = np.concatenate([causal, where(cmp_ok).reshape(P, TT * 32)], axis=1)
    mask_n = np.concatenate([mask_n, (np.arange(P) >= 31).astype(np.float32)[:, None]], axis=1)
    s, t = np.arange(P)[:, None], np.arange(P)[None, :]
    levels = []
    for lv in range(7):
        half = 64 >> lv
        levels.append((s // (2 * half) == t // (2 * half)) & (s % (2 * half) < half) & (t % (2 * half) >= half))
    levels.append(s == t)
    mask_h = np.concatenate(levels, axis=1).astype(np.float32)
    number = np.arange(P, dtype=np.float32)[:, None]
    mask_m = np.concatenate([(s < t).astype(np.float32), np.tile(np.arange(T, dtype=np.float32), (P, 1)),
                             np.tile(2 * np.arange(N_EXP, dtype=np.float32), (P, 1)),
                             number, number + P * np.arange(TT, dtype=np.float32)], axis=1)
    inv = (np.float32(10000.0) ** (-np.arange(32, dtype=np.float32) / np.float32(32))).astype(np.float32)
    ang = np.arange(T, dtype=np.float32)[None, :] * inv[:, None]
    co, si = np.cos(ang).astype(np.float32), np.sin(ang).astype(np.float32)
    rot = np.concatenate([np.tile(co, (4, 1)), np.concatenate([si, -si, si, -si], axis=0)], axis=1)
    return dict(mask_ab=mask_ab, mask_c=mask_c, mask_n=mask_n, mask_h=mask_h, mask_m=mask_m, rot=rot,
                eye=np.eye(P, dtype=np.float32))


def _lay_out(i):
    f = lambda n: np.asarray(i[n])
    c = _constants()
    a = {k: c[k] for k in ("mask_ab", "mask_c", "mask_n", "mask_h", "mask_m", "rot", "eye")}
    tok = lambda x: np.ascontiguousarray(x.T.reshape(-1, P, T).transpose(1, 0, 2)).reshape(P, -1)
    a["xT"] = tok(f("x")[0])
    a["pT"] = np.stack([tok(f("p")[l, 0]) for l in range(2)])
    for l in range(2):
        for k, n in enumerate(("ffn1", "ffn2")):
            g, up = f(f"{n}_w_gate")[l], f(f"{n}_w_up")[l]
            both = np.concatenate([g.reshape(D, NF, 1, P), up.reshape(D, NF, 1, P)], axis=2).reshape(D, 2 * FF)
            a[f"gu_{l}_{k}"] = _units(both)
            a[f"down_{l}_{k}"] = _units(f(f"{n}_w_down")[l])
        a[f"pg_{l}"] = _units(f("w_ple_gate")[l])
        a[f"pp_{l}"] = _units(f("w_ple_proj")[l], T)
    w = f("w_in_ab")[0]
    order_a = [x for p in A_PAIRS for x in p]
    qa, ka, va, qb, kb, vb = np.split(w, [768, 1024, 1280, 2048, 2816], axis=1)
    a["in_ab"] = _units(np.concatenate([_heads(qa, order_a), qb, ka, kb], axis=1))
    a["v_ab"] = _halves(np.concatenate([va, vb], axis=1))
    w = f("w_out_ab")[0]
    a["out_ab"] = _units(np.concatenate([w[x * HD:(x + 1) * HD] for x in order_a] + [w[768:]], axis=0))
    w = f("w_in_c")[0]
    a["in_c"], a["v_c"] = _units(w[:, :2048]), _halves(w[:, 2048:])
    a["out_c"] = _units(f("w_out_c")[0])
    rpb = np.pad(f("rpb_c")[0], ((0, 0), (0, 0), (48, 48)))
    a["rpb"] = np.ascontiguousarray(np.stack([rpb[:, :, 63 - j:127 - j] for j in range(64)], axis=1)).reshape(16, 64, 960)
    a["ada"] = _units(f("w_ada_2")[0], T).reshape(12, P, 4, UNIT).transpose(0, 2, 1, 3).reshape(48, P, UNIT)
    order_n = [x for p in N_PAIRS for x in p]
    hq, hf, hi, hgt, nq, kc, vc, ks, vs, kw, vw, ng = np.split(
        f("w_in_2")[0], np.cumsum([512] * 5 + [128] * 6).tolist(), axis=1)
    a["in_2"] = _units(np.concatenate([hq, hf, hgt, _heads(nq, order_n), kc, vc, ks, kw], axis=1))
    a["tok_2"] = _halves(np.concatenate([hi, vs, vw, np.pad(ng, ((0, 0), (0, 232)))], axis=1))
    a["cmp"] = np.stack([x for n in ("k", "v") for x in
                         f(f"cmp_w1_{n}_2")[0].reshape(4, 4, P, 256).transpose(0, 2, 1, 3).reshape(4, P, UNIT)])
    w = f("w_out_2")[0]
    a["out_2"] = _units(np.concatenate([w[:512]] + [w[512 + x * HD:512 + (x + 1) * HD] for x in order_n], axis=0))
    down = f("w_sh_dn_2")[0].reshape(2, P, 2, 512).transpose(2, 1, 0, 3).reshape(2, P, 1024)
    a["shared"] = np.concatenate([_units(f("w_sh_gu_2")[0]), down], axis=0)
    gu, dn = f("w_exp_gu_2")[0], f("w_exp_dn_2")[0]
    a["exp_gu"] = gu.reshape(N_EXP, KD, P, 2 * EXP_H).transpose(0, 2, 1, 3).reshape(N_EXP, P, -1)
    a["exp_dn"] = dn.reshape(N_EXP, 2, P, D).transpose(0, 2, 1, 3).reshape(N_EXP, P, -1)
    gains = {"ffn1": "norm_ffn1", "mix": "norm_mix", "ffn2": "norm_ffn2", "ple": "norm_ple"}
    parts = []
    for n in NORMS:
        if n[-2] == "_":
            parts.append(_column(f(gains[n[:-2]])[int(n[-1])]))
        else:
            parts.append(_column({"first": f("norm_final"), "norm1": f("norm1_g_2")[0], "norm2": f("norm2_g_2")[0], "final": f("final_g_2")}[n]))
    parts += [_column(f("b_ada_2")[0]), _column(f("c_2")[0]), _column(f("hg_lb_logits_2")[0]), _column(f("hg_lb_logits_2")[1]),
              _column(f("hg_norm_g_2")[0]), _column(f("cmp_b1_k_2")[0]), _column(f("cmp_b1_v_2")[0]),
              np.tile(f("cmp_pos_k_2")[0].T, (2, 1)), np.tile(f("cmp_pos_v_2")[0].T, (2, 1)),
              np.broadcast_to(f("sink_a")[0], (P, 12)), np.broadcast_to(f("router_bias_2")[0], (P, N_EXP))]
    cols3 = lambda w: w.reshape(-1, P, w.shape[1]).transpose(1, 0, 2).reshape(P, -1)
    parts += [cols3(f("cmp_w2_k_2")[0]), cols3(f("cmp_w2_v_2")[0]), cols3(f("router_w_2")[0])]
    a["cols"] = np.concatenate(parts, axis=1)
    assert a["cols"].shape == (P, NCOL)
    return {k: np.ascontiguousarray(v, dtype=v.dtype) for k, v in a.items()}


def _program(nc, arrays, stop_at=None):
    dr = {n: nc.dram_tensor(f"in_{n}", a.shape, F32, kind="ExternalInput").ap() for n, a in arrays.items()}
    dr["tok"] = nc.dram_tensor("tokens", [T, D], F32, kind="Internal").ap()
    dr["block_e"] = nc.dram_tensor("block_experts", [1, P], I32, kind="Internal").ap()
    out = nc.dram_tensor("out_0", [P, KD * T], F32, kind="ExternalOutput").ap()
    block_kernel(nc, dr, out, stop_at)


def kernel(**inputs):
    import concourse.bacc as bacc
    from concourse.bass_utils import run_bass_kernel_spmd
    arrays = _lay_out(inputs)
    nc = bacc.Bacc("TRN2", target_bir_lowering=False, num_devices=1)
    _program(nc, arrays)
    r = run_bass_kernel_spmd(nc, [{f"in_{n}": a for n, a in arrays.items()}], core_ids=[0])
    y = r.results[0]["out_0"].reshape(P, KD, T)
    return np.ascontiguousarray(y.transpose(2, 1, 0)).reshape(1, T, D)
```
